# Optimizing a Trainium2 kernel written in Bass

```python
import math
import numpy as np
import jax
import jax.numpy as jnp
from jax import lax
import jax, jax.numpy as jnp

D_MODEL = 1024
BATCH = 1
SEQ = 512
DEPTH = 2

HEAD_DIM = 64
ROPE_THETA = 10000.0
NORM_EPS = 1e-6
D_FF = 4 * D_MODEL
Q_BLOCK = 128

A_HEADS = D_MODEL // (2 * HEAD_DIM)
IDX_HEADS = 4
DSA_TOPK = 256

B_HEADS = D_MODEL // (2 * HEAD_DIM)
B_KV_GROUPS = 2
CMP_BLOCK = 32
CMP_STRIDE = 16
CMP_HIDDEN = 256
SLC_BLOCK = 64
SLC_TOPN = 16
WINDOW = 512

C_HEADS = D_MODEL // (2 * HEAD_DIM)

EVEN_SPLITS = (A_HEADS * HEAD_DIM, HEAD_DIM, HEAD_DIM, IDX_HEADS * HEAD_DIM, HEAD_DIM, IDX_HEADS, B_HEADS * HEAD_DIM, 6 * B_KV_GROUPS * HEAD_DIM, 3 * B_HEADS)
EVEN_IN = sum(EVEN_SPLITS)
EVEN_MIX = (A_HEADS + B_HEADS) * HEAD_DIM
ODD_MIX = C_HEADS * 2 * HEAD_DIM
ODD_IN = 3 * ODD_MIX


def rms_norm(x, g):
    xf = x.astype(jnp.float32)
    y = xf * lax.rsqrt(jnp.mean(xf * xf, axis=-1, keepdims=True) + NORM_EPS)
    return (y * g.astype(jnp.float32)).astype(x.dtype)

def rope_tables(T):
    inv = 1.0 / (ROPE_THETA ** (jnp.arange(0, HEAD_DIM, 2, dtype=jnp.float32) / HEAD_DIM))
    ang = jnp.arange(T, dtype=jnp.float32)[:, None] * inv[None, :]
    return jnp.cos(ang), jnp.sin(ang)

def apply_rope(x, cos, sin):
    x1, x2 = jnp.split(x, 2, axis=-1)
    shape = (1, cos.shape[0]) + (1,) * (x.ndim - 3) + (cos.shape[1],)
    c = cos.reshape(shape).astype(x.dtype)
    s = sin.reshape(shape).astype(x.dtype)
    return jnp.concatenate([x1 * c - x2 * s, x2 * c + x1 * s], axis=-1)

def masked_softmax(s, mask):
    s = jnp.where(mask, s.astype(jnp.float32), -jnp.inf)
    m = jnp.max(s, axis=-1, keepdims=True)
    m = jnp.where(jnp.isfinite(m), m, 0.0)
    e = jnp.exp(s - m)
    return e / jnp.maximum(jnp.sum(e, axis=-1, keepdims=True), 1e-30)

def split_cols(a, sizes):
    offs = np.cumsum(sizes)[:-1].tolist()
    return jnp.split(a, offs, axis=-1)

def sweep_query_blocks(fn, T):
    nb = T // Q_BLOCK
    out = lax.map(fn, jnp.arange(nb))
    out = jnp.moveaxis(out, 0, 1)
    return out.reshape((out.shape[0], T) + out.shape[3:])

def dsa_attention(q, k, v, q_idx, k_idx, w_idx):
    T = q.shape[1]
    topk = min(DSA_TOPK, T // 4)
    scale = HEAD_DIM ** -0.5
    key_pos = jnp.arange(T)

    def block(i):
        t0 = i * Q_BLOCK
        tq = t0 + jnp.arange(Q_BLOCK)
        qb = lax.dynamic_slice_in_dim(q, t0, Q_BLOCK, 1)
        qib = lax.dynamic_slice_in_dim(q_idx, t0, Q_BLOCK, 1)
        wb = lax.dynamic_slice_in_dim(w_idx, t0, Q_BLOCK, 1)
        rel = jax.nn.relu(jnp.einsum('bqhd,bsd->bqhs', qib, k_idx).astype(jnp.float32))
        score = jnp.einsum('bqh,bqhs->bqs', wb.astype(jnp.float32), rel)
        score = jnp.where(key_pos[None, :] <= tq[:, None], score, -jnp.inf)
        _, idx = lax.top_k(score, topk)
        valid = idx <= tq[None, :, None]
        kg = jax.vmap(lambda kk, ii: kk[ii])(k, idx)
        vg = jax.vmap(lambda vv, ii: vv[ii])(v, idx)
        s = jnp.einsum('bqhd,bqkd->bhqk', qb, kg) * scale
        p = masked_softmax(s, valid[:, None])
        return jnp.einsum('bhqk,bqkd->bqhd', p.astype(vg.dtype), vg)

    return sweep_query_blocks(block, T)

def compress_blocks(x, pe, w1, w2):
    bsz, T, G, D = x.shape
    n_ch = T // CMP_STRIDE
    r = CMP_BLOCK // CMP_STRIDE
    n_c = n_ch - r + 1
    ch = x.reshape(bsz, n_ch, CMP_STRIDE, G, D)
    blk = jnp.concatenate([ch[:, j:j + n_c] for j in range(r)], axis=2)
    blk = blk + pe[None, None, :, None, :].astype(x.dtype)
    h = jax.nn.gelu(jnp.einsum('bnlgd,ldf->bngf', blk, w1.reshape(CMP_BLOCK, D, CMP_HIDDEN)))
    return jnp.einsum('bngf,fd->bngd', h, w2)

def slc_overlap(n_c, n_s):
    c0 = np.arange(n_c) * CMP_STRIDE
    c1 = c0 + CMP_BLOCK
    s0 = np.arange(n_s) * SLC_BLOCK
    s1 = s0 + SLC_BLOCK
    return ((c0[:, None] < s1[None, :]) & (c1[:, None] > s0[None, :])).astype(np.float32)

def nsa_attention(q, k_c, v_c, k_s, v_s, k_w, v_w, gate_logits, cmp_pe, cmp_w1, cmp_w2):
    bsz, T = q.shape[0], q.shape[1]
    G, J, D = B_KV_GROUPS, B_HEADS // B_KV_GROUPS, HEAD_DIM
    scale = D ** -0.5
    qg = q.reshape(bsz, T, G, J, D)
    g = jax.nn.sigmoid(gate_logits.astype(jnp.float32)).astype(q.dtype).reshape(bsz, T, G, J, 3)
    t_all = jnp.arange(T)

    kc = compress_blocks(k_c, cmp_pe[0], cmp_w1[0], cmp_w2[0])
    vc = compress_blocks(v_c, cmp_pe[1], cmp_w1[1], cmp_w2[1])
    n_c = kc.shape[1]
    cmp_end = jnp.arange(n_c) * CMP_STRIDE + CMP_BLOCK - 1
    s_c = jnp.einsum('btgjd,bngd->bgjtn', qg, kc) * scale
    p_c = masked_softmax(s_c, cmp_end[None, :] <= t_all[:, None])
    o_c = jnp.einsum('bgjtn,bngd->btgjd', p_c.astype(vc.dtype), vc)

    n_s = T // SLC_BLOCK
    n_sel = min(SLC_TOPN, n_s)
    imp = jnp.einsum('bgjtn,nm->bgtm', p_c, jnp.asarray(slc_overlap(n_c, n_s)))
    ks_blk = k_s.reshape(bsz, n_s, SLC_BLOCK, G, D).transpose(0, 3, 1, 2, 4)
    vs_blk = v_s.reshape(bsz, n_s, SLC_BLOCK, G, D).transpose(0, 3, 1, 2, 4)
    kw_pad = jnp.pad(k_w, ((0, 0), (WINDOW, 0), (0, 0), (0, 0)))
    vw_pad = jnp.pad(v_w, ((0, 0), (WINDOW, 0), (0, 0), (0, 0)))
    b_ix = jnp.arange(bsz)[:, None, None, None]
    g_ix = jnp.arange(G)[None, :, None, None]
    blk_ids = jnp.arange(n_s)

    def block(i):
        t0 = i * Q_BLOCK
        tq = t0 + jnp.arange(Q_BLOCK)
        qb = lax.dynamic_slice_in_dim(qg, t0, Q_BLOCK, 1)
        gq = lax.dynamic_slice_in_dim(g, t0, Q_BLOCK, 1)
        sc = lax.dynamic_slice_in_dim(imp, t0, Q_BLOCK, 2)
        cur = tq // SLC_BLOCK
        forced = (blk_ids[None, :] == 0) | (blk_ids[None, :] == cur[:, None]) | (blk_ids[None, :] == cur[:, None] - 1)
        admissible = blk_ids[None, :] * SLC_BLOCK <= tq[:, None]
        sc = jnp.where(forced, jnp.inf, sc)
        sc = jnp.where(admissible, sc, -jnp.inf)
        _, idx = lax.top_k(sc, n_sel)
        kg = ks_blk[b_ix, g_ix, idx]
        vg = vs_blk[b_ix, g_ix, idx]
        pos = idx[..., None] * SLC_BLOCK + jnp.arange(SLC_BLOCK)
        valid = (pos <= tq[None, None, :, None, None]).reshape(bsz, G, Q_BLOCK, n_sel * SLC_BLOCK)[:, :, None]
        s_s = jnp.einsum('bqgjd,bgqnsd->bgjqns', qb, kg).reshape(bsz, G, J, Q_BLOCK, n_sel * SLC_BLOCK) * scale
        p_s = masked_softmax(s_s, valid)
        o_s = jnp.einsum('bgjqk,bgqkd->bqgjd', p_s.astype(vg.dtype), vg.reshape(bsz, G, Q_BLOCK, n_sel * SLC_BLOCK, D))
        kw = lax.dynamic_slice_in_dim(kw_pad, t0, WINDOW + Q_BLOCK, 1)
        vw = lax.dynamic_slice_in_dim(vw_pad, t0, WINDOW + Q_BLOCK, 1)
        pos_w = t0 - WINDOW + jnp.arange(WINDOW + Q_BLOCK)
        valid_w = (pos_w[None, :] >= 0) & (pos_w[None, :] <= tq[:, None]) & (pos_w[None, :] > tq[:, None] - WINDOW)
        s_w = jnp.einsum('bqgjd,bsgd->bgjqs', qb, kw) * scale
        p_w = masked_softmax(s_w, valid_w)
        o_w = jnp.einsum('bgjqs,bsgd->bqgjd', p_w.astype(vw.dtype), vw)
        return gq[..., 1:2] * o_s + gq[..., 2:3] * o_w

    o_sw = sweep_query_blocks(block, T)
    o = g[..., 0:1] * o_c + o_sw
    return o.reshape(bsz, T, B_HEADS, D)

def even_mixer(h, w_in, cmp_pe, cmp_w1, cmp_w2, w_out, cos, sin):
    bsz, T, _ = h.shape
    proj = jnp.einsum('btd,de->bte', h, w_in)
    qa, ka, va, qi, ki, wi, qb, kvb, gb = split_cols(proj, EVEN_SPLITS)
    qa = apply_rope(qa.reshape(bsz, T, A_HEADS, HEAD_DIM), cos, sin)
    ka = apply_rope(ka, cos, sin)
    qi = apply_rope(qi.reshape(bsz, T, IDX_HEADS, HEAD_DIM), cos, sin)
    ki = apply_rope(ki, cos, sin)
    o_a = dsa_attention(qa, ka, va, qi, ki, wi)
    qb = apply_rope(qb.reshape(bsz, T, B_HEADS, HEAD_DIM), cos, sin)
    kvb = kvb.reshape(bsz, T, 6, B_KV_GROUPS, HEAD_DIM)
    k_c = apply_rope(kvb[:, :, 0], cos, sin)
    v_c = kvb[:, :, 1]
    k_s = apply_rope(kvb[:, :, 2], cos, sin)
    v_s = kvb[:, :, 3]
    k_w = apply_rope(kvb[:, :, 4], cos, sin)
    v_w = kvb[:, :, 5]
    o_b = nsa_attention(qb, k_c, v_c, k_s, v_s, k_w, v_w, gb, cmp_pe, cmp_w1, cmp_w2)
    o = jnp.concatenate([o_a.reshape(bsz, T, -1), o_b.reshape(bsz, T, -1)], axis=-1)
    return jnp.einsum('bte,ed->btd', o, w_out)

def diff_mixer(h, w_in, lam, subln_g, w_out, cos, sin, lambda_init):
    bsz, T, _ = h.shape
    proj = jnp.einsum('btd,de->bte', h, w_in)
    q, k, v = jnp.split(proj, 3, axis=-1)
    q = apply_rope(q.reshape(bsz, T, C_HEADS * 2, HEAD_DIM), cos, sin).reshape(bsz, T, C_HEADS, 2, HEAD_DIM)
    k = apply_rope(k.reshape(bsz, T, C_HEADS * 2, HEAD_DIM), cos, sin).reshape(bsz, T, C_HEADS, 2, HEAD_DIM)
    v = v.reshape(bsz, T, C_HEADS, 2 * HEAD_DIM)
    lf = lam.astype(jnp.float32)
    lam_val = jnp.exp(jnp.sum(lf[0] * lf[1])) - jnp.exp(jnp.sum(lf[2] * lf[3])) + lambda_init
    scale = HEAD_DIM ** -0.5
    key_pos = jnp.arange(T)

    def block(i):
        t0 = i * Q_BLOCK
        tq = t0 + jnp.arange(Q_BLOCK)
        qb = lax.dynamic_slice_in_dim(q, t0, Q_BLOCK, 1)
        s = jnp.einsum('bqhcd,bshcd->bhcqs', qb, k) * scale
        p = masked_softmax(s, key_pos[None, :] <= tq[:, None])
        a = p[:, :, 0] - lam_val * p[:, :, 1]
        return jnp.einsum('bhqs,bshe->bqhe', a.astype(v.dtype), v)

    o = sweep_query_blocks(block, T)
    o = rms_norm(o, subln_g) * (1.0 - lambda_init)
    return jnp.einsum('bte,ed->btd', o.reshape(bsz, T, ODD_MIX), w_out)

def sq_relu_mlp(h, w_up, w_down):
    u = jnp.einsum('btd,df->btf', h, w_up)
    return jnp.einsum('btf,fd->btd', jnp.square(jax.nn.relu(u)), w_down)

def first_inputs(seed: int = 0) -> dict:
    key = jax.random.key(seed)
    ks = jax.random.split(key, 16)
    ne = (DEPTH + 1) // 2
    no = DEPTH // 2

    def nrm(k, shape, fan_in):
        return jax.random.normal(k, shape, jnp.float32) * (fan_in ** -0.5)

    def gain(k, shape):
        return 1.0 + 0.05 * jax.random.normal(k, shape, jnp.float32)

    return {
        'x': jax.random.normal(ks[0], (BATCH, SEQ, D_MODEL), jnp.float32),
        'mix_norm_g': gain(ks[1], (DEPTH, D_MODEL)),
        'mlp_norm_g': gain(ks[2], (DEPTH, D_MODEL)),
        'even_w_in': nrm(ks[3], (ne, D_MODEL, EVEN_IN), D_MODEL),
        'even_cmp_pe': 0.02 * jax.random.normal(ks[4], (ne, 2, CMP_BLOCK, HEAD_DIM), jnp.float32),
        'even_cmp_w1': nrm(ks[5], (ne, 2, CMP_BLOCK * HEAD_DIM, CMP_HIDDEN), CMP_BLOCK * HEAD_DIM),
        'even_cmp_w2': nrm(ks[6], (ne, 2, CMP_HIDDEN, HEAD_DIM), CMP_HIDDEN),
        'even_w_out': nrm(ks[7], (ne, EVEN_MIX, D_MODEL), EVEN_MIX),
        'odd_w_in': nrm(ks[8], (no, D_MODEL, ODD_IN), D_MODEL),
        'odd_lambda': 0.1 * jax.random.normal(ks[9], (no, 4, HEAD_DIM), jnp.float32),
        'odd_subln_g': gain(ks[10], (no, 2 * HEAD_DIM)),
        'odd_w_out': nrm(ks[11], (no, ODD_MIX, D_MODEL), ODD_MIX),
        'mlp_w_up': nrm(ks[12], (DEPTH, D_MODEL, D_FF), D_MODEL),
        'mlp_w_down': nrm(ks[13], (DEPTH, D_FF, D_MODEL), D_FF),
        'final_norm_g': gain(ks[14], (D_MODEL,)),
    }

def first_block(x, mix_norm_g, mlp_norm_g, even_w_in, even_cmp_pe, even_cmp_w1, even_cmp_w2, even_w_out, odd_w_in, odd_lambda, odd_subln_g, odd_w_out, mlp_w_up, mlp_w_down, final_norm_g):
    T = x.shape[1]
    cos, sin = rope_tables(T)
    h = x
    for layer in range(DEPTH):
        u = rms_norm(h, mix_norm_g[layer])
        if layer % 2 == 0:
            e = layer // 2
            h = h + even_mixer(u, even_w_in[e], even_cmp_pe[e], even_cmp_w1[e], even_cmp_w2[e], even_w_out[e], cos, sin)
        else:
            o = layer // 2
            lambda_init = 0.8 - 0.6 * math.exp(-0.3 * layer)
            h = h + diff_mixer(u, odd_w_in[o], odd_lambda[o], odd_subln_g[o], odd_w_out[o], cos, sin, lambda_init)
        h = h + sq_relu_mlp(rms_norm(h, mlp_norm_g[layer]), mlp_w_up[layer], mlp_w_down[layer])
    return rms_norm(h, final_norm_g)


DEPTH_2 = 1

GRID_W = 64
N_META = 16
EPS = 1e-6

NA_HEADS = 8
NA_HEAD_DIM = 64
NA_WIDTH = NA_HEADS * NA_HEAD_DIM
NA_WIN_H = 8
NA_WIN_W = 16

HG_HEADS = 4
HG_DK = 128
HG_DV = 128
HG_KDIM = HG_HEADS * HG_DK
HG_VDIM = HG_HEADS * HG_DV
HG_CHUNK = 16

D_FF_2 = 4 * D_MODEL

IN_SPLIT = (NA_WIDTH, NA_WIDTH, NA_WIDTH,
            HG_KDIM, HG_KDIM, HG_KDIM, HG_VDIM, HG_VDIM,
            D_MODEL, D_MODEL)
IN_COLS = sum(IN_SPLIT)


def rms_norm_2(x, g):
    xf = x.astype(jnp.float32)
    y = xf * lax.rsqrt(jnp.mean(xf * xf, axis=-1, keepdims=True) + EPS)
    return (y * g.astype(jnp.float32)).astype(x.dtype)

def split_cols_2(a):
    outs, off = [], 0
    for n in IN_SPLIT:
        outs.append(a[..., off:off + n])
        off += n
    return outs

def neighbourhood_attention(q, k, v, rpb):
    B, L, H, dh = q.shape
    T = L - N_META
    rows = T // GRID_W
    kh = min(NA_WIN_H, rows)
    scale = dh ** -0.5
    qm, km, vm = q[:, :N_META], k[:, :N_META], v[:, :N_META]
    qg = q[:, N_META:].reshape(B, rows, GRID_W, H, dh)
    kg = k[:, N_META:].reshape(B, rows, GRID_W, H, dh)
    vg = v[:, N_META:].reshape(B, rows, GRID_W, H, dh)

    r = jnp.arange(rows)
    row_start = jnp.clip(r - kh // 2, 0, rows - kh)
    row_idx = row_start[:, None] + jnp.arange(kh)[None, :]
    k_blk = kg[:, row_idx]
    v_blk = vg[:, row_idx]

    s_win = jnp.einsum('brchd,brjwhd->bhrcjw', qg, k_blk).astype(jnp.float32) * scale
    c = jnp.arange(GRID_W)
    col_start = jnp.clip(c - NA_WIN_W // 2, 0, GRID_W - NA_WIN_W)
    in_win = (c[None, :] >= col_start[:, None]) & (c[None, :] < col_start[:, None] + NA_WIN_W)
    dr = row_idx - r[:, None]
    dc = jnp.clip(c[None, :] - c[:, None], -(NA_WIN_W - 1), NA_WIN_W - 1)
    bias = rpb.astype(jnp.float32)[:, dr[:, None, :, None] + NA_WIN_H - 1,
                                   dc[None, :, None, :] + NA_WIN_W - 1]
    s_win = jnp.where(in_win[:, None, :], s_win + bias[None], -1e30)

    s_meta = jnp.einsum('brchd,bmhd->bhrcm', qg, km).astype(jnp.float32) * scale
    s = jnp.concatenate([s_win.reshape(B, H, rows, GRID_W, kh * GRID_W), s_meta], axis=-1)
    p = jax.nn.softmax(s, axis=-1).astype(v.dtype)
    p_win = p[..., :kh * GRID_W].reshape(B, H, rows, GRID_W, kh, GRID_W)
    p_meta = p[..., kh * GRID_W:]
    o_grid = (jnp.einsum('bhrcjw,brjwhd->brchd', p_win, v_blk)
              + jnp.einsum('bhrcm,bmhd->brchd', p_meta, vm)).reshape(B, T, H, dh)

    s_mm = jnp.einsum('bmhd,bnhd->bhmn', qm, km).astype(jnp.float32) * scale
    p_mm = jax.nn.softmax(s_mm, axis=-1).astype(v.dtype)
    o_meta = jnp.einsum('bhmn,bnhd->bmhd', p_mm, vm)
    return jnp.concatenate([o_meta, o_grid], axis=1)

def chunk_scan(q, k, v, log_f):
    B, L, H, dk = q.shape
    dv = v.shape[-1]
    n = L // HG_CHUNK

    def to_chunks(a):
        return a.reshape(B, n, HG_CHUNK, H, a.shape[-1]).transpose(1, 0, 3, 2, 4)

    tri = jnp.tril(jnp.ones((HG_CHUNK, HG_CHUNK), dtype=bool))

    def step(S, inp):
        qi, ki, vi, gi = inp
        b = jnp.cumsum(gi, axis=-2)
        o_inter = jnp.einsum('bhtk,bhkv->bhtv', qi * jnp.exp(b), S)
        diff = jnp.where(tri[:, :, None], b[..., :, None, :] - b[..., None, :, :], -jnp.inf)
        A = jnp.einsum('bhtk,bhsk,bhtsk->bhts', qi, ki, jnp.exp(diff))
        o_intra = jnp.einsum('bhts,bhsv->bhtv', A, vi)
        b_last = b[..., -1:, :]
        S_new = (jnp.exp(b_last[..., 0, :])[..., None] * S
                 + jnp.einsum('bhsk,bhsv->bhkv', ki * jnp.exp(b_last - b), vi))
        return S_new, o_inter + o_intra

    S0 = jnp.zeros((B, H, dk, dv), jnp.float32)
    _, o = lax.scan(step, S0, (to_chunks(q), to_chunks(k), to_chunks(v), to_chunks(log_f)))
    return o.transpose(1, 0, 3, 2, 4).reshape(B, L, H, dv)

def hgrn2_branch(q, z_fwd, z_bwd, i, g, lb, gain):
    B, L, _ = q.shape
    dtype = q.dtype

    def heads(a, d):
        return a.astype(jnp.float32).reshape(B, L, HG_HEADS, d)

    qh = jax.nn.silu(heads(q, HG_DK))
    vh = heads(i, HG_DV)

    def gates(z, lb_dir):
        lb_h = lb_dir.reshape(HG_HEADS, HG_DK)
        log_f = jnp.logaddexp(jnp.log(lb_h), jnp.log1p(-lb_h) + jax.nn.log_sigmoid(heads(z, HG_DK)))
        return -jnp.expm1(log_f), log_f

    k_f, lf_f = gates(z_fwd, lb[0])
    k_b, lf_b = gates(z_bwd, lb[1])
    rev = lambda a: jnp.flip(a, axis=1)
    o = chunk_scan(qh, k_f, vh, lf_f) + rev(chunk_scan(rev(qh), rev(k_b), rev(vh), rev(lf_b)))
    o = o * lax.rsqrt(jnp.mean(o * o, axis=-1, keepdims=True) + EPS)
    o = o.reshape(B, L, HG_VDIM) * gain.astype(jnp.float32) * jax.nn.silu(g.astype(jnp.float32))
    return o.astype(dtype)

def second_inputs(seed: int = 0) -> dict:
    key = jax.random.key(seed)
    ks = jax.random.split(key, 14)
    f32 = jnp.float32
    nrm = lambda k, shape, s: jax.random.normal(k, shape, f32) * s
    return {
        "x": nrm(ks[0], (BATCH, SEQ, D_MODEL), 1.0),
        "meta_tokens": nrm(ks[1], (N_META, D_MODEL), 1.0),
        "w_in": nrm(ks[2], (DEPTH_2, D_MODEL, IN_COLS), D_MODEL ** -0.5),
        "w_na_out": nrm(ks[3], (DEPTH_2, NA_WIDTH, D_MODEL), NA_WIDTH ** -0.5),
        "w_hg_out": nrm(ks[4], (DEPTH_2, HG_VDIM, D_MODEL), HG_VDIM ** -0.5),
        "w_o": nrm(ks[5], (DEPTH_2, D_MODEL, D_MODEL), D_MODEL ** -0.5),
        "w_up": nrm(ks[6], (DEPTH_2, D_MODEL, D_FF_2), D_MODEL ** -0.5),
        "w_down": nrm(ks[7], (DEPTH_2, D_FF_2, D_MODEL), D_FF_2 ** -0.5),
        "norm_mix": 1.0 + nrm(ks[8], (DEPTH_2, D_MODEL), 0.05),
        "norm_mlp": 1.0 + nrm(ks[9], (DEPTH_2, D_MODEL), 0.05),
        "norm_final": 1.0 + nrm(ks[10], (D_MODEL,), 0.05),
        "hg_norm": 1.0 + nrm(ks[11], (DEPTH_2, HG_VDIM), 0.05),
        "na_rpb": nrm(ks[12], (DEPTH_2, NA_HEADS, 2 * NA_WIN_H - 1, 2 * NA_WIN_W - 1), 0.1),
        "hg_lb_logits": nrm(ks[13], (2, DEPTH_2 + 1, HG_KDIM), 0.5),
    }

def second_block(x, meta_tokens, w_in, w_na_out, w_hg_out, w_o, w_up, w_down,
              norm_mix, norm_mlp, norm_final, hg_norm, na_rpb, hg_lb_logits):
    B = x.shape[0]
    h = jnp.concatenate([jnp.broadcast_to(meta_tokens.astype(x.dtype)[None], (B, N_META, D_MODEL)), x], axis=1)
    L = h.shape[1]
    lb_all = jnp.cumsum(jax.nn.softmax(hg_lb_logits.astype(jnp.float32), axis=1), axis=1)
    for l in range(DEPTH_2):
        a = rms_norm_2(h, norm_mix[l])
        (q_na, k_na, v_na, q_hg, z_f, z_b, i_hg, g_hg, gate_na, gate_hg) = split_cols_2(a @ w_in[l])
        hd = lambda t: t.reshape(B, L, NA_HEADS, NA_HEAD_DIM)
        y_na = neighbourhood_attention(hd(q_na), hd(k_na), hd(v_na), na_rpb[l]).reshape(B, L, NA_WIDTH) @ w_na_out[l]
        y_hg = hgrn2_branch(q_hg, z_f, z_b, i_hg, g_hg, lb_all[:, l], hg_norm[l]) @ w_hg_out[l]
        mix = jax.nn.sigmoid(gate_na) * y_na + jax.nn.sigmoid(gate_hg) * y_hg
        h = h + mix @ w_o[l]
        m = rms_norm_2(h, norm_mlp[l])
        h = h + jnp.square(jax.nn.relu(m @ w_up[l])) @ w_down[l]
    h = rms_norm_2(h, norm_final)
    return h[:, N_META:]


def setup_inputs(seed=0):
    out = dict(first_inputs(seed))
    for name, value in second_inputs(seed + 1).items():
        if name != "x":
            out[name + "_2"] = value
    return out


def reference(
    x, mix_norm_g, mlp_norm_g, even_w_in, even_cmp_pe, even_cmp_w1, even_cmp_w2, even_w_out,
    odd_w_in, odd_lambda, odd_subln_g, odd_w_out, mlp_w_up, mlp_w_down, final_norm_g,
    meta_tokens_2, w_in_2, w_na_out_2, w_hg_out_2, w_o_2, w_up_2, w_down_2, norm_mix_2,
    norm_mlp_2, norm_final_2, hg_norm_2, na_rpb_2, hg_lb_logits_2,
):
    x = first_block(
        x, mix_norm_g, mlp_norm_g, even_w_in, even_cmp_pe, even_cmp_w1, even_cmp_w2, even_w_out,
        odd_w_in, odd_lambda, odd_subln_g, odd_w_out, mlp_w_up, mlp_w_down, final_norm_g,
    )
    return second_block(
        x, meta_tokens_2, w_in_2, w_na_out_2, w_hg_out_2, w_o_2, w_up_2, w_down_2, norm_mix_2,
        norm_mlp_2, norm_final_2, hg_norm_2, na_rpb_2, hg_lb_logits_2,
    )


_drawn_inputs = setup_inputs


def setup_inputs(seed=0):
    import zlib

    import numpy as np

    out = dict(_drawn_inputs(seed))
    spreads = {}
    factors = {'even_cmp_pe': 7.324,
     'odd_lambda': 8.0,
     'hg_norm_2': 3.653,
     'na_rpb_2': 8.0,
     'hg_lb_logits_2': 5.391}
    for name, (base, spread) in spreads.items():
        noise = np.random.default_rng([zlib.crc32(name.encode()), seed]).standard_normal(out[name].shape)
        drawn = base * np.exp(spread * noise) if base else spread * noise
        out[name] = jnp.asarray(drawn.astype(out[name].dtype))
    for name, factor in factors.items():
        out[name] = (out[name] * factor).astype(out[name].dtype)
    return out
```

```python
import math
from contextlib import ExitStack

import numpy as np

import concourse.bass as bass
from concourse import mybir

F32 = mybir.dt.float32
BF16 = mybir.dt.bfloat16
U8 = mybir.dt.uint8
ALU = mybir.AluOpType
ACT = mybir.ActivationFunctionType
AX = mybir.AxisListType

T = 512
D = 1024
NT = 4
KT = 8
META = 16
EPS = 1e-6
TAKE = 128
NEG = -1e30
TAKEN = -3e38
LAMBDA_INIT = 0.8 - 0.6 * math.exp(-0.3)

ROW_NAMES = [("mix_norm_g", 16), ("mlp_norm_g", 16), ("norm_mix_2", 8), ("norm_mlp_2", 8),
             ("hg_lb_logits_2", 16), ("even_cmp_pe", 32), ("odd_subln_g", 1)]
ROW_AT = {}
for _n, _k in ROW_NAMES:
    ROW_AT[_n] = sum(k for _, k in ROW_NAMES[:len(ROW_AT)])
NROWS = sum(k for _, k in ROW_NAMES)


def shape_constants():
    c = {}
    inv = (1.0 / (np.float32(10000.0) ** (np.arange(0, 64, 2, dtype=np.float32) / np.float32(64)))).astype(np.float32)
    ang = np.arange(T, dtype=np.float32)[None, :] * inv[:, None]
    c["c_cos"] = np.tile(np.cos(ang), (4, 1)).astype(np.float32)
    c["c_sin"] = np.tile(np.sin(ang), (4, 1)).astype(np.float32)
    rot = np.zeros((128, 128), np.float32)
    for b in (0, 64):
        for d in range(32):
            rot[b + 32 + d, b + d] = -1.0
            rot[b + d, b + 32 + d] = 1.0
    c["c_rot"] = rot
    c["c_ident"] = np.eye(128, dtype=np.float32)
    q = np.arange(128)
    c["c_causal"] = np.where(q[None, :] <= q[:, None], 0.0, NEG).astype(np.float32)
    n = np.arange(32)
    end = n * 16 + 31
    t = np.arange(T).reshape(NT, 128).transpose(1, 0)
    c["c_cmp"] = np.where(end[None, None, :] <= t[:, :, None], 0.0, NEG).astype(np.float32).reshape(128, 128)
    masks = []
    for m in (1, 2, 4, 8, 16, 32, 64):
        same = (q[:, None] // (2 * m)) == (q[None, :] // (2 * m))
        left = (q // m) % 2 == 0
        masks.append(same & left[:, None] & ~left[None, :])
    for m in range(7):
        masks.append(masks[m].T)
    c["c_lev"] = np.concatenate([m.astype(np.float32) for m in masks], axis=1)
    col = np.arange(64)
    start = np.clip(col - 8, 0, 48)
    inw = (col[None, :] >= start[:, None]) & (col[None, :] < start[:, None] + 16)
    c["c_win"] = np.tile(np.where(inw, 0.0, NEG).astype(np.float32)[::-1], (2, 1))
    c["c_zero"] = np.zeros((120, 128), np.float32)
    return c


class Step:
    __slots__ = ("go", "after", "lane", "sem", "count", "named")

    def __init__(self, go, after, lane, sem=None):
        self.go, self.after, self.lane, self.sem, self.count, self.named = go, after, lane, sem, 0, sem is not None


def flat(xs):
    for x in xs:
        if x is None:
            continue
        if isinstance(x, (list, tuple)):
            yield from flat(x)
        else:
            yield x


class Lane:

    def __init__(self, name, sem):
        self.name, self.sem, self.queue = name, sem, []

    def __call__(self, go, *after):
        s = Step(go, list(flat(after)), self)
        for a in s.after:
            a.named = True
        self.queue.append(s)
        return s

    def dma(self, out, in_, sem, *after):
        s = Step(lambda e: e.dma_start(out, in_), list(flat(after)), self, sem)
        for a in s.after:
            a.named = True
        self.queue.append(s)
        sem.total += 16
        s.count = sem.total
        return s


class DmaSem:
    def __init__(self, sem):
        self.sem, self.total = sem, 0


def number(lanes):
    for lane in lanes:
        n = 0
        for s in lane.queue:
            if s.sem is None and s.named:
                n += 1
                s.count = n


def play(lane, eng):
    seen = {}
    for s in lane.queue:
        for a in s.after:
            sem = a.lane.sem if a.sem is None else a.sem.sem
            if seen.get(id(sem), 0) < a.count:
                eng.wait_ge(sem, a.count)
                seen[id(sem)] = a.count
        i = s.go(eng)
        if s.sem is not None:
            i.then_inc(s.sem.sem, 16)
        elif s.named:
            i.then_inc(lane.sem, 1)


class Ring:

    def __init__(self, bufs):
        self.bufs, self.free, self.at = bufs, [[] for _ in bufs], 0

    def get(self):
        i = self.at % len(self.bufs)
        self.at += 1
        free, self.free[i] = self.free[i], []
        return Buf(self, i, self.bufs[i], free)


class Buf:
    def __init__(self, ring, i, ap, free):
        self.ring, self.i, self.ap, self.free = ring, i, ap, free

    def done(self, *steps):
        self.ring.free[self.i] += list(flat(steps))


def build(nc, ins, out):
    ctx = ExitStack()
    with ctx:
        def sb(name, shape, dt=F32):
            return ctx.enter_context(nc.sbuf_tensor(name, shape, dt))[tuple(slice(None) for _ in shape)]

        def sem(name):
            return ctx.enter_context(nc.semaphore(name))

        PE, DVE, ACTL, POOL, SP = [Lane(n, sem("s_" + n)) for n in ("pe", "dve", "act", "pool", "sp")]
        lanes = [PE, DVE, ACTL, POOL, SP]
        names = [0]

        def dsem():
            names[0] += 1
            return DmaSem(sem(f"d{names[0]}"))

        bank = [ctx.enter_context(nc.psum_tensor(f"bank{i}", [128, 512], F32))[:, :] for i in range(8)]
        bank_free = [[] for _ in range(8)]

        class Banks(Ring):
            def __init__(self, ids):
                self.bufs, self.at, self.ids = [bank[i] for i in ids], 0, ids

            def get(self):
                i = self.ids[self.at % len(self.ids)]
                self.at += 1
                free, bank_free[i] = bank_free[i], []
                return BankBuf(i, free)

        class BankBuf:
            def __init__(self, i, free):
                self.i, self.ap, self.free = i, bank[i], free

            def done(self, *steps):
                bank_free[self.i] += list(flat(steps))

        def const(name, shape, dt=F32, src=None, eng=None):
            t = sb("k_" + name, shape, dt)
            s = (eng or SP).dma(t, ins[name] if src is None else src, dsem())
            return t, s

        h = sb("h", [128, NT, D])
        h_ready = []
        x_v = ins["x"].rearrange("a (i p) d -> (a p) i d", p=128)
        for i in range(NT):
            h_ready.append(SP.dma(h[:, i, :], x_v[:, i, :], dsem()))
        rows = sb("rows", [NROWS, 128])
        rows_s = dsem()
        rows_d = None
        views = {
            "mix_norm_g": ins["mix_norm_g"].rearrange("l (k p) -> (l k) p", p=128),
            "mlp_norm_g": ins["mlp_norm_g"].rearrange("l (k p) -> (l k) p", p=128),
            "norm_mix_2": ins["norm_mix_2"].rearrange("l (k p) -> (l k) p", p=128),
            "norm_mlp_2": ins["norm_mlp_2"].rearrange("l (k p) -> (l k) p", p=128),
            "hg_lb_logits_2": ins["hg_lb_logits_2"].rearrange("a l (k p) -> (a l k) p", p=128),
            "even_cmp_pe": ins["even_cmp_pe"].rearrange("o c (l2 l) d -> (o c l2) (l d)", l=2),
            "odd_subln_g": ins["odd_subln_g"],
        }
        ident, ident_d = const("c_ident", [128, 128])
        for n, k in ROW_NAMES:
            rows_d = SP.dma(rows[ROW_AT[n]:ROW_AT[n] + k, :], views[n], rows_s)
        identb = sb("identb", [128, 128], BF16)
        causal = sb("causal", [128, 128], BF16)
        cmpm = sb("cmpm", [128, 128], BF16)
        cosT, cos_d = const("c_cos", [128, T])
        sinT, sin_d = const("c_sin", [128, T])
        rotm, rot_d = const("c_rot", [128, 128])
        winm, win_d = const("c_win", [128, 64], eng=POOL)
        half = sb("half", [128, 16])
        half_m = DVE(lambda e: e.memset(half, -0.5))

        uT = sb("uT", [128, KT, T + META])
        W = Ring([sb(f"w{i}", [128, 4096]) for i in range(3)])
        W_sem = [dsem() for _ in range(3)]
        ARENA = 21632
        big = sb("big", [128, ARENA])
        cols = sb("cols", [128, 128])
        lev = sb("lev", [128, 14 * 128], U8)
        lev_f = POOL.dma(big[:, 0:14 * 128], ins["c_lev"], dsem())
        lev_d = POOL(lambda e: e.tensor_copy(lev, big[:, 0:14 * 128]), lev_f)
        small = Ring([sb(f"sm{i}", [128, 16]) for i in range(24)])
        w2k = Ring([sb(f"p{i}", [128, 528]) for i in range(5)])
        w2t = Ring([sb(f"t{i}", [128, 528]) for i in range(4)])
        tmp4 = Ring([sb(f"q{i}", [128, D]) for i in range(2)])
        c1 = SP.dma(big[:, 1792:1920], ins["c_causal"], dsem())
        c2 = SP.dma(big[:, 1920:2048], ins["c_cmp"], dsem())
        identb_d = POOL(lambda e: e.tensor_copy(identb, ident), ident_d)
        causal_d = POOL(lambda e: e.tensor_copy(causal, big[:, 1792:1920]), c1)
        cmpm_d = POOL(lambda e: e.tensor_copy(cmpm, big[:, 1920:2048]), c2)
        tmp_sem = [dsem(), dsem()]

        def slab(src, kts=8, ncols=512):
            b = W.get()
            v = b.ap[:, 0:kts * ncols].rearrange("p (k n) -> p k n", n=ncols)
            b.view = v
            b.ready = SP.dma(v, src, W_sem[b.i], b.free)
            return b

        def slab_of(parts, ncols):
            b = W.get()
            b.view = b.ap[:, 0:8 * ncols].rearrange("p (k n) -> p k n", n=ncols)
            for dst, src in parts:
                b.ready = SP.dma(dst(b.view), src, W_sem[b.i], b.free)
            return b

        def wsrc(name, r0, kts, c0, ncols):
            return ins[name][r0:r0 + kts * 128, c0:c0 + ncols].rearrange("(k p) n -> p k n", p=128)

        allb = Banks(list(range(8)))

        b = allb.get()
        s = PE(lambda e, b=b: e.transpose(b.ap[:, 0:NROWS], rows[:, :], ident[0:NROWS, 0:NROWS]), rows_d, ident_d)
        cols_r = DVE(lambda e, b=b: e.tensor_copy(cols[:, 0:NROWS], b.ap[:, 0:NROWS]), s)
        b.done(cols_r)

        def col(name, k):
            return cols[:, ROW_AT[name] + k:ROW_AT[name] + k + 1]

        def rstd_of(ss, n, scale, part=128):
            v = small.get()
            s1 = DVE(lambda e: e.tensor_scalar(v.ap[0:part, 0:n], ss.ap[0:part, 0:n], scale, EPS, ALU.mult, ALU.add),
                     ss.ready, v.free)
            ss.done(s1)
            r = small.get()
            r.ready = POOL(lambda e: e.tensor_tensor(r.ap[0:part, 0:n], v.ap[0:part, 0:n], half[0:part, 0:n], ALU.pow),
                           s1, half_m, r.free)
            v.done(r.ready)
            return r

        def sum_squares(src, ready, part=128):
            junk = tmp4.get()
            ss = small.get()
            ss.ready = ACTL(lambda e: e.activation(junk.ap[0:part, :], src, ACT.Square,
                                                   accum_out=ss.ap[0:part, 0:1]), ready, junk.free, ss.free)
            junk.done(ss.ready)
            return ss

        def evac(n, outp, inp, scale, *after):
            if n % 2:
                return ACTL(lambda e: e.activation(outp, inp, ACT.Copy, scale=scale), *after)
            return DVE(lambda e: e.tensor_scalar(outp, inp, scale, None, ALU.mult), *after)

        def norm_T(h_ready, gname, g0, uT_free, meta=None):
            scaled = []
            ready = [None] * NT
            xs = [big[:, ARENA - (i + 1) * D:ARENA - i * D] for i in range(NT)]
            for i in range(NT):
                r = rstd_of(sum_squares(h[:, i, :], h_ready[i]), 1, 1.0 / D)
                ready[i] = DVE(lambda e, i=i, r=r: e.tensor_scalar(xs[i], h[:, i, :], r.ap[:, 0:1], None, ALU.mult),
                               r.ready, h_ready[i], uT_free)
                r.done(ready[i])
            out_steps = []
            mready = []
            if meta is not None:
                mx = tmp4.get()
                hm_d = POOL.dma(mx.ap[0:META, :], ins["meta_tokens_2"], tmp_sem[mx.i], mx.free)
                r = rstd_of(sum_squares(mx.ap[0:META, :], hm_d, META), 1, 1.0 / D, META)
                ms = DVE(lambda e: e.tensor_scalar(mx.ap[0:META, :], mx.ap[0:META, :], r.ap[0:META, 0:1], None, ALU.mult),
                         r.ready)
                r.done(ms)
                mb = allb.get()
                for k in range(KT):
                    t = PE(lambda e, k=k: e.transpose(mb.ap[:, k * META:(k + 1) * META],
                                                      mx.ap[0:META, k * 128:(k + 1) * 128], ident[0:META, 0:META]),
                           ms, mb.free)
                mx.done(t)
                for k in range(KT):
                    mready.append(DVE(lambda e, k=k: e.tensor_scalar(
                        uT[:, k, T:T + META], mb.ap[:, k * META:(k + 1) * META], col(gname, g0 + k), None, ALU.mult),
                        t, uT_free, cols_r))
                mb.done(mready)
            for k in range(KT):
                b = allb.get()
                for i in range(NT):
                    t = PE(lambda e, i=i, k=k, b=b: e.transpose(b.ap[:, i * 128:(i + 1) * 128],
                                                                xs[i][:, k * 128:(k + 1) * 128], ident), ready[i], b.free, ident_d)
                s = evac(k, uT[:, k, 0:T], b.ap, col(gname, g0 + k), t, cols_r, uT_free)
                b.done(s)
                out_steps.append(s)
            return out_steps + mready

        def fm(bk, lhs, ready, n0=0, n=T, kts=KT, rhs=None):
            for k in range(kts):
                t = PE(lambda e, k=k: e.matmul(bk.ap[:, 0:n], lhs(k), uT[:, k, n0:n0 + n] if rhs is None else rhs(k),
                                               start=(k == 0), stop=(k == kts - 1)), ready, bk.free)
            return t

        def tm(bk, wv, i, ready, c0, ncols, o0=0, part=128, lhs=None, kts=KT):
            for k in range(kts):
                t = PE(lambda e, k=k: e.matmul(bk.ap[0:part, o0:o0 + ncols],
                                               uT[:, k, i * 128:i * 128 + part] if lhs is None else lhs(k),
                                               wv[:, k, c0:c0 + ncols],
                                               start=(k == 0), stop=(k == kts - 1)), ready, bk.free)
            return t

        def run_pipe(units, depth):
            for n in range(len(units) + depth - 1):
                for d in range(depth - 1, -1, -1):
                    if 0 <= n - d < len(units):
                        units[n - d][d]()

        def rope_unit(bk, lhs, ready, dest, scale, dfree):
            st = {}

            def s0():
                st["b"] = bk.get()
                st["t"] = fm(st["b"], lhs, ready)

            def s1():
                x = st["x"] = w2k.get()
                b = st["b"]
                st["c"] = ACTL(lambda e: e.activation(x.ap[:, 0:T], b.ap, ACT.Copy, scale=scale), st["t"], x.free)
                b.done(st["c"])

            def s2():
                x, y, t1 = st["x"], bk.get(), w2t.get()
                a = PE(lambda e: e.matmul(y.ap, rotm, x.ap[:, 0:T], start=True, stop=True), st["c"], y.free, rot_d)
                p = POOL(lambda e: e.tensor_tensor(t1.ap[:, 0:T], x.ap[:, 0:T], cosT, ALU.mult), st["c"], t1.free, cos_d)
                x.done(a, p)
                t2 = w2t.get()
                q = DVE(lambda e: e.tensor_tensor(t2.ap[:, 0:T], y.ap, sinT, ALU.mult), a, t2.free, sin_d)
                y.done(q)
                r = DVE(lambda e: e.tensor_tensor(dest, t1.ap[:, 0:T], t2.ap[:, 0:T], ALU.add), p, q, dfree)
                t1.done(r)
                t2.done(r)
                st["r"] = r
            return [s0, s1, s2], st

        def residual(name, lhsT, lready, kslabs=1):
            new = [None] * NT
            last = []
            for c in range(2):
                slabs = []
                bks = [allb.get() for _ in range(NT)]
                for g in range(kslabs):
                    w = slab(wsrc(name, g * 1024, 8, c * 512, 512))
                    for i in range(NT):
                        for k in range(KT):
                            t = PE(lambda e, k=k, i=i, g=g, w=w, bks=bks: e.matmul(
                                bks[i].ap, lhsT(g * 8 + k, i), w.view[:, k, :],
                                start=(g == 0 and k == 0), stop=(g == kslabs - 1 and k == 7)),
                                w.ready, bks[i].free, lready(g * 8 + k))
                        if g == kslabs - 1:
                            new[i] = DVE(lambda e, i=i, c=c, bks=bks: e.tensor_tensor(
                                h[:, i, c * 512:(c + 1) * 512], h[:, i, c * 512:(c + 1) * 512], bks[i].ap, ALU.add), t)
                            bks[i].done(new[i])
                    w.done(t)
                    last = t
            return new, last

        def mlp(up, down, uready, big_free):
            hT = [big[:, q * 4096:(q + 1) * 4096].rearrange("p (k n) -> p k n", n=T) for q in range(2)]
            free = [big_free, big_free]
            new = [None] * NT

            def up_quarter(q):
                hready = []
                for g in range(2):
                    w = slab(wsrc(up, 0, 8, (q * 2 + g) * 512, 512))
                    for f in range(4):
                        b = allb.get()
                        t = fm(b, lambda k, f=f, w=w: w.view[:, k, f * 128:(f + 1) * 128], [w.ready, uready])
                        r = w2k.get()
                        a = ACTL(lambda e, b=b, r=r: e.activation(r.ap[:, 0:T], b.ap, ACT.Relu), t, r.free)
                        b.done(a)
                        p = POOL(lambda e, r=r, n=g * 4 + f, q=q: e.tensor_tensor(
                            hT[q % 2][:, n, :], r.ap[:, 0:T], r.ap[:, 0:T], ALU.mult), a, free[q % 2])
                        r.done(p)
                        hready.append(p)
                    w.done(t)
                return hready, t

            def down_quarter(q, hready):
                for c in range(2):
                    w = slab(wsrc(down, q * 1024, 8, c * 512, 512))
                    for i in range(NT):
                        b = allb.get()
                        for k in range(KT):
                            t = PE(lambda e, k=k, i=i, w=w, b=b: e.matmul(
                                b.ap, hT[q % 2][:, k, i * 128:(i + 1) * 128], w.view[:, k, :],
                                start=(k == 0), stop=(k == 7)), w.ready, b.free, hready[k])
                        new[i] = DVE(lambda e, i=i, c=c, b=b: e.tensor_tensor(
                            h[:, i, c * 512:(c + 1) * 512], h[:, i, c * 512:(c + 1) * 512], b.ap, ALU.add), t, new[i])
                        b.done(new[i])
                    w.done(t)
                free[q % 2] = t
                return t
            hready, _ = up_quarter(0)
            for q in range(4):
                after, uread = up_quarter(q + 1) if q < 3 else (None, uread)
                last = down_quarter(q, hready)
                hready = after
            return new, last, uread

        A = {}
        at = [0]

        def region(name, shape, base=None):
            n = int(np.prod(shape[1:]))
            o = at[0]
            at[0] += n
            assert at[0] <= ARENA, (name, at[0])
            v = big[0:shape[0], o:o + n]
            if len(shape) == 3:
                v = v.rearrange("p (a b) -> p a b", b=shape[2])
            A[name] = v
            return v

        u0 = norm_T(h_ready, "mix_norm_g", 0, []) + [lev_d, causal_d, cmpm_d]
        EV = "even_w_in"
        qaT = region("qaT", [128, 4, T])
        kaT = region("kaT", [128, T])
        va = region("va", [128, 4, 64])
        qiT = region("qiT", [128, 2, T])
        kiT = region("kiT", [128, T])
        qbT = region("qbT", [128, 4, T])
        kcT = region("kcT", [128, T])
        ksT = region("ksT", [128, T])
        vsb = region("vsb", [128, 4, 128])
        oT = region("oT", [128, 8, T])
        kwT = region("kwT", [128, T])
        vcT = region("vcT", [128, T])
        vw = region("vw", [128, 4, 152])
        wi = sb("wi", [128, 16])
        gate = sb("gate", [128, 4, 24])
        pk = Banks([0, 1, 2, 3, 4, 5])
        pv2 = Banks([6, 7])
        xs_read = u0

        def piece(c0, n, at_):
            return (lambda v: v[:, :, at_:at_ + n]), wsrc(EV, 0, 8, c0, n)

        wB = slab_of([piece(896, 64, 0), piece(896, 68, 64), piece(640, 256, 132)], 388)
        wK = slab_of([piece(512, 64, 0), piece(512, 128, 64)], 192)
        wE_cols = 280
        units, sts = [], {}

        def add(name, lhs, w, dest, scale=1.0, dfree=()):
            u, st = rope_unit(pk, lhs, [w.ready, u0], dest, scale, list(dfree))
            units.append(u)
            sts[name] = st

        def sub(w, c0):
            return lambda k: w.view[:, k, c0:c0 + 128]

        add("ki", sub(wB, 0), wB, kiT)
        add("qi0", sub(wB, 132), wB, qiT[:, 0, :])
        add("qi1", sub(wB, 260), wB, qiT[:, 1, :])
        add("ka", sub(wK, 0), wK, kaT)
        run_pipe(units, 3)
        wi_r = va_r = None
        b = pk.get()
        for i in range(NT):
            t = tm(b, wB.view, i, [wB.ready, u0], 128, 4, i * 4)
        wi_r = DVE(lambda e, b=b: e.tensor_copy(wi[:, :], b.ap[:, 0:16]), t)
        b.done(wi_r)
        wB.done(t)
        b = pk.get()
        for i in range(NT):
            t = tm(b, wK.view, i, [wK.ready, u0], 128, 64, i * 64)
        va_r = DVE(lambda e, b=b: e.tensor_copy(va, b.ap[:, 0:256].rearrange("p (a b) -> p a b", b=64)), t)
        b.done(va_r)
        wK.done(t)

        sc = {i: region(f"sc{i}", [128, (i + 1) * 128]) for i in (1, 2, 3)}
        sel = sb("sel", [128, 3, T], BF16)
        sc_r = {}
        for i in (1, 2, 3):
            n = (i + 1) * 128
            for hh in range(4):
                b = pk.get()
                p0 = (hh % 2) * 64
                t = PE(lambda e, b=b, i=i, hh=hh, p0=p0, n=n: e.matmul(
                    b.ap[:, 0:n], qiT[p0:p0 + 64, hh // 2, i * 128:(i + 1) * 128], kiT[p0:p0 + 64, 0:n],
                    start=True, stop=True), sts[f"qi{hh // 2}"]["r"], sts["ki"]["r"], b.free)
                r = w2k.get()
                a = ACTL(lambda e, b=b, r=r, n=n: e.activation(r.ap[:, 0:n], b.ap[:, 0:n], ACT.Relu), t, r.free)
                b.done(a)
                wc = wi[:, i * 4 + hh:i * 4 + hh + 1]
                if hh == 0:
                    s = DVE(lambda e, r=r, i=i, n=n, wc=wc: e.tensor_scalar(sc[i][:, 0:n], r.ap[:, 0:n], wc, None, ALU.mult),
                            a, wi_r)
                else:
                    s = DVE(lambda e, r=r, i=i, n=n, wc=wc: e.scalar_tensor_tensor(
                        out=sc[i][:, 0:n], in0=r.ap[:, 0:n], scalar=wc, in1=sc[i][:, 0:n], op0=ALU.mult, op1=ALU.add),
                        a, wi_r, sc_r[i])
                r.done(s)
                sc_r[i] = s
            sc_r[i] = DVE(lambda e, i=i: e.tensor_tensor(sc[i][:, i * 128:(i + 1) * 128], sc[i][:, i * 128:(i + 1) * 128],
                                                         causal, ALU.add), sc_r[i], causal_d)

        m8 = sb("m8", [128, 3, 8])

        def topk():
            for _ in range(TAKE // 8):
                for i in (1, 2, 3):
                    n = (i + 1) * 128
                    s = DVE(lambda e, i=i, n=n: e.max(m8[:, i - 1, :], sc[i][:, 0:n]), sc_r[i])
                    sc_r[i] = DVE(lambda e, i=i, n=n: e.match_replace(sc[i][:, 0:n], m8[:, i - 1, :], sc[i][:, 0:n], TAKEN), s)
                    yield
            for i in (1, 2, 3):
                n = (i + 1) * 128
                sc_r[i] = DVE(lambda e, i=i, n=n: e.tensor_scalar(sel[:, i - 1, 0:n], sc[i][:, 0:n], -2e38, NEG,
                                                                  ALU.is_gt, ALU.mult), sc_r[i])

        taking = topk()

        def advance(g, n):
            for _ in range(n):
                if next(g, "end") == "end":
                    break

        units = []
        wA = slab(wsrc(EV, 0, 8, 0, 512))
        wD = slab(wsrc(EV, 0, 8, 1476, 512))
        for j in range(4):
            add(f"qa{j}", sub(wA, j * 128), wA, qaT[:, j, :], 0.125)
        add("kc", sub(wD, 0), wD, kcT)
        add("ks", sub(wD, 256), wD, ksT)
        run_pipe(units, 3)
        wA.done(sts["qa3"]["t"])
        b = pk.get()
        t = fm(b, sub(wD, 128), [wD.ready, u0])
        vc_r = ACTL(lambda e, b=b: e.activation(vcT, b.ap, ACT.Copy), t)
        b.done(vc_r)
        b = pk.get()
        for i in range(NT):
            t = tm(b, wD.view, i, [wD.ready, u0], 384, 128, i * 128)
        vs_r = DVE(lambda e, b=b: e.tensor_copy(vsb, b.ap.rearrange("p (a b) -> p a b", b=128)), t)
        b.done(vs_r)
        wD.done(t)
        X = [region(f"X{c}", [128, 2, T]) for c in range(2)]
        X_r = []
        for c, (src, r) in enumerate(((kcT, sts["kc"]["r"]), (vcT, vc_r))):
            xs = dsem()
            X_m = DVE(lambda e, c=c: e.memset(X[c][64:128, :, T - 1:T], 0.0), u0)
            for g in range(2):
                d1 = POOL.dma(X[c][0:64, g, :], src[g * 64:(g + 1) * 64, :], xs, r)
                d2 = POOL.dma(X[c][64:128, g, 0:T - 1], src[g * 64:(g + 1) * 64, 1:T], xs, r)
            X_r.append([d2, X_m])
        wC = W.get()
        wC.view = wC.ap.rearrange("p (k n) -> p k n", n=512)
        for g in range(2):
            for k in range(KT):
                wC.ready = SP.dma(wC.view[:, k, :].rearrange("p (j g d) -> p g j d", g=2, j=4)[:, g],
                                  ins[EV][k * 128:(k + 1) * 128, 964 + g * 256:964 + (g + 1) * 256].rearrange(
                                      "p (j d) -> p j d", j=4), W_sem[wC.i], wC.free)
        wE = slab(wsrc(EV, 0, 8, 1988, 280), 8, 280)
        units = []
        for j in range(4):
            add(f"qb{j}", sub(wC, j * 128), wC, qbT[:, j, :], 0.125)
        add("kw", sub(wE, 0), wE, kwT)
        run_pipe(units, 3)
        wC.done(sts["qb3"]["t"])
        for i in range(NT):
            b = pk.get()
            t = tm(b, wE.view, i, [wE.ready, u0], 128, 152)
            vw_r = DVE(lambda e, b=b, i=i: e.tensor_copy(vw[:, i, :], b.ap[:, 0:152]), t)
            b.done(vw_r)
        wE.done(t)
        g1 = ACTL(lambda e: e.activation(gate, vw[:, :, 128:152], ACT.Exp, scale=-1.0), vw_r)
        g2 = DVE(lambda e: e.tensor_scalar(gate, gate, 1.0, None, ALU.add), g1)
        gate_r = DVE(lambda e: e.reciprocal(gate, gate), g2)
        advance(taking, 10)

        cH = region("cH", [128, 4, 62])
        cG = region("cG", [128, 4, 62])
        cb = sb("cb", [128, 4])
        w2s = region("w2s", [128, 4, 64])
        w2_d = POOL.dma(w2s, ins["even_cmp_w2"].rearrange("o c (f p) d -> p (o c f) d", p=128), dsem(), u0)
        kcc = sb("kcc", [128, 32])
        vcc = sb("vcc", [32, 2, 64])
        hs = []
        for c in range(2):
            w = slab(ins["even_cmp_w1"][0, c].rearrange("(k p) n -> p k n", p=128), 16, 256)
            for f in range(2):
                b = pk.get()
                for lp in range(16):
                    a0, b0 = (2 * lp) // 16, (2 * lp) % 16
                    rhs = X[c].rearrange("p g (n s) -> p g n s", s=16)[:, :, a0:a0 + 31, b0]
                    t = PE(lambda e, b=b, w=w, f=f, lp=lp, rhs=rhs: e.matmul(
                        b.ap[:, 0:62], w.view[:, lp, f * 128:(f + 1) * 128], rhs,
                        start=(lp == 0), stop=(lp == 15)), w.ready, X_r[c], b.free)
                for lp in range(16):
                    t = PE(lambda e, b=b, w=w, f=f, lp=lp, c=c: e.matmul(
                        b.ap[:, 64:65], w.view[:, lp, f * 128:(f + 1) * 128], col("even_cmp_pe", c * 16 + lp),
                        start=(lp == 0), stop=(lp == 15)), cols_r)
                s1 = ACTL(lambda e, b=b, n=c * 2 + f: e.activation(cb[:, n:n + 1], b.ap[:, 64:65], ACT.Copy), t)
                s2 = ACTL(lambda e, b=b, n=c * 2 + f: e.activation(cH[:, n, :], b.ap[:, 0:62], ACT.Identity,
                                                                   bias=cb[:, n:n + 1]), s1)
                b.done(s2)
                hs.append(s2)
            w.done(t)
        s = POOL(lambda e: e.tensor_tensor(cG, cH, cH, ALU.mult), hs)
        s = POOL(lambda e: e.tensor_tensor(cG, cG, cH, ALU.mult), s)
        s = DVE(lambda e: e.scalar_tensor_tensor(out=cG, in0=cG, scalar=0.044715, in1=cH, op0=ALU.mult, op1=ALU.add), s)
        s = ACTL(lambda e: e.activation(cG, cG, ACT.Tanh, scale=math.sqrt(2.0 / math.pi)), s)
        s = DVE(lambda e: e.tensor_scalar(cG, cG, 0.5, 0.5, ALU.mult, ALU.add), s)
        cg_r = DVE(lambda e: e.tensor_tensor(cG, cG, cH, ALU.mult), s)
        b = pk.get()
        for g in range(2):
            for f in range(2):
                t = PE(lambda e, b=b, g=g, f=f: e.matmul(b.ap[g * 64:(g + 1) * 64, 0:31], w2s[:, f, :],
                                                         cG[:, f, g * 31:(g + 1) * 31], start=(f == 0), stop=(f == 1)),
                       cg_r, w2_d, b.free)
        kcc_r = DVE(lambda e, b=b: e.tensor_copy(kcc[:, 0:31], b.ap[:, 0:31]), t)
        b.done(kcc_r)
        b = pk.get()
        for g in range(2):
            for f in range(2):
                t = PE(lambda e, b=b, g=g, f=f: e.matmul(b.ap[0:31, g * 64:(g + 1) * 64], cG[:, 2 + f, g * 31:(g + 1) * 31],
                                                         w2s[:, 2 + f, :], start=(f == 0), stop=(f == 1)),
                       cg_r, w2_d, b.free)
        vcc_r = DVE(lambda e, b=b: e.tensor_copy(vcc[0:31], b.ap[0:31, 0:128].rearrange("p (a b) -> p a b", b=64)), t)
        b.done(vcc_r)

        sb_s = Banks([0, 1, 2])
        sb_p = Banks([3, 4, 5])
        sb_o = Banks([6, 7])

        def softmax_unit(qv, kv, n, masks, qready, vs, floor, gatev, obk, oreg, first, last, vready):
            st = {}
            nb = (n + 127) // 128

            def s0():
                b = st["b"] = sb_s.get()
                t = PE(lambda e: e.matmul(b.ap[:, 0:n], qv, kv, start=True, stop=not masks), qready, b.free)
                for m, (c0, c1, mv, mr) in enumerate(masks):
                    t = PE(lambda e, c0=c0, c1=c1, mv=mv, m=m: e.matmul(
                        b.ap[:, c0:c1], identb, mv, start=False, stop=(m == len(masks) - 1)), mr, identb_d)
                st["t"] = t

            def s1():
                b = st["b"]
                m = st["m"] = small.get()
                s = DVE(lambda e: e.tensor_reduce(m.ap[:, 0:1], b.ap[:, 0:n], AX.X, ALU.max, negate=True), st["t"], m.free)
                if floor:
                    s = DVE(lambda e: e.tensor_scalar(m.ap[:, 0:1], m.ap[:, 0:1], 1e28, None, ALU.min), s)
                p = st["p"] = w2k.get()
                st["e"] = ACTL(lambda e: e.activation(p.ap[:, 0:n], b.ap[:, 0:n], ACT.Exp, bias=m.ap[:, 0:1],
                                                      accum_out=m.ap[:, 1:2]), s, p.free)
                b.done(st["e"])

            def s2():
                m, p = st["m"], st["p"]
                s = st["e"]
                if floor:
                    s = DVE(lambda e: e.tensor_scalar(m.ap[:, 1:2], m.ap[:, 1:2], 1e-30, None, ALU.max), s)
                s = DVE(lambda e: e.reciprocal(m.ap[:, 2:3], m.ap[:, 1:2]), s)
                if gatev is None:
                    s = DVE(lambda e: e.tensor_scalar(p.ap[:, 0:n], p.ap[:, 0:n], m.ap[:, 2:3], None, ALU.mult), s)
                else:
                    s = DVE(lambda e: e.tensor_scalar(p.ap[:, 0:n], p.ap[:, 0:n], m.ap[:, 2:3], gatev, ALU.mult,
                                                      ALU.mult), s, gate_r)
                m.done(s)
                st["n"] = s

            def s3():
                p = st["p"]
                b = st["b2"] = sb_p.get()
                for k in range(nb):
                    w = min(128, n - k * 128)
                    t = PE(lambda e, k=k, w=w: e.transpose(b.ap[0:w, k * 128:(k + 1) * 128], p.ap[:, k * 128:k * 128 + w],
                                                           ident), st["n"], b.free)
                p.done(t)
                x = st["x"] = w2t.get()
                w = min(n, 128)
                s = ACTL(lambda e: e.activation(x.ap[0:w, 0:nb * 128], b.ap[0:w, 0:nb * 128], ACT.Copy), t, x.free)
                b.done(s)
                st["v"] = s

            def s4():
                x = st["x"]
                o = obk()
                for k in range(nb):
                    w = min(128, n - k * 128)
                    t = PE(lambda e, k=k, w=w: e.matmul(oreg(o), vs(k), x.ap[0:w, k * 128:(k + 1) * 128],
                                                        start=(first and k == 0), stop=(last and k == nb - 1)),
                           st["v"], vready, o.free)
                x.done(t)
                o.last = t
            return [s0, s1, s2, s3, s4]

        def pair_bank(flush):
            st = {}

            def get():
                if "b" not in st:
                    st["b"] = sb_o.get()
                return st["b"]
            return get, st

        units = []
        flushes = {}
        oT_r = [None] * 8
        for j in range(4):
            get, st = pair_bank(None)
            for i in range(NT):
                n = (i + 1) * 128
                for g in range(2):
                    p = slice(g * 64, g * 64 + 64)
                    qv = qbT[p, j, i * 128:(i + 1) * 128]
                    reg = lambda o, p=p, i=i: o.ap[p, i * 128:(i + 1) * 128]
                    gc = lambda x, i=i, g=g, j=j: gate[:, i, (g * 4 + j) * 3 + x:(g * 4 + j) * 3 + x + 1]
                    qr = sts[f"qb{j}"]["r"]
                    units.append(softmax_unit(qv, kcc[p, 0:31], 31, [(0, 31, cmpm[:, i * 32:i * 32 + 31], cmpm_d)],
                                              [qr, kcc_r], lambda k, g=g: vcc[0:31, g, :], True, gc(0), get, reg,
                                              True, False, vcc_r))
                    cm = [(i * 128, n, causal, causal_d)]
                    units.append(softmax_unit(qv, ksT[p, 0:n], n, cm, [qr, sts["ks"]["r"]],
                                              lambda k, g=g: vsb[:, k, g * 64:g * 64 + 64], False, gc(1), get, reg,
                                              False, False, vs_r))
                    units.append(softmax_unit(qv, kwT[p, 0:n], n, cm, [qr, sts["kw"]["r"]],
                                              lambda k, g=g: vw[:, k, g * 64:g * 64 + 64], False, gc(2), get, reg,
                                              False, True, vw_r))

            def flush(st=st, j=j):
                b = st["b"]
                oT_r[4 + j] = ACTL(lambda e: e.activation(oT[:, 4 + j, :], b.ap, ACT.Copy), b.last, u0)
                b.done(oT_r[4 + j])
            old = units[-1][4]
            units[-1][4] = lambda old=old, flush=flush: (old(), flush())
        for n, u in enumerate(units):
            if n % 2 == 0:
                old = u[2]
                u[2] = lambda old=old: (old(), advance(taking, 2))
        run_pipe(units, 5)
        advance(taking, 1000)
        nsa_done = oT_r[7]

        units = []
        for j in range(4):
            get, st = pair_bank(None)
            for i in range(NT):
                n = (i + 1) * 128
                for c in range(2):
                    p = slice(c * 64, c * 64 + 64)
                    if i < 1:
                        masks = [(i * 128, n, causal, causal_d)]
                    else:
                        masks = [(0, n, sel[:, i - 1, 0:n], sc_r[i])]
                    units.append(softmax_unit(qaT[p, j, i * 128:(i + 1) * 128], kaT[p, 0:n], n, masks,
                                              [sts[f"qa{j}"]["r"], sts["ka"]["r"]], lambda k: va[:, k, :], False, None,
                                              get, lambda o, p=p, i=i: o.ap[p, i * 128:(i + 1) * 128], True, True, va_r))

            def flush(st=st, j=j):
                b = st["b"]
                oT_r[j] = ACTL(lambda e: e.activation(oT[:, j, :], b.ap, ACT.Copy), b.last, u0)
                b.done(oT_r[j])
            old = units[-1][4]
            units[-1][4] = lambda old=old, flush=flush: (old(), flush())
        run_pipe(units, 5)

        def residual_even():
            new = [None] * NT
            for c in range(2):
                w = W.get()
                v = w.ap.rearrange("p (k n) -> p k n", n=512)
                src = ins["even_w_out"][:, c * 512:(c + 1) * 512]
                SP.dma(v[:, 0:4, :], src[0:512, :].rearrange("(k p) n -> p k n", p=128), W_sem[w.i], w.free)
                hi = src[512:1024, :].rearrange("(g j d) n -> g d j n", g=2, j=4)
                SP.dma(v[0:64, 4:8, :], hi[0], W_sem[w.i])
                w.ready = SP.dma(v[64:128, 4:8, :], hi[1], W_sem[w.i])
                for i in range(NT):
                    b = allb.get()
                    for k in range(KT):
                        t = PE(lambda e, k=k, i=i, v=v, b=b: e.matmul(b.ap, oT[:, k, i * 128:(i + 1) * 128], v[:, k, :],
                                                                      start=(k == 0), stop=(k == 7)),
                               w.ready, b.free, oT_r[k])
                    new[i] = DVE(lambda e, i=i, c=c, b=b: e.tensor_tensor(
                        h[:, i, c * 512:(c + 1) * 512], h[:, i, c * 512:(c + 1) * 512], b.ap, ALU.add), t)
                    b.done(new[i])
                w.done(t)
            return new, t

        hr, last = residual_even()
        u = norm_T(hr, "mlp_norm_g", 0, [last])
        hr, last, _ = mlp("mlp_up_0", "mlp_down_0", u, u)

        u0 = u = norm_T(hr, "mix_norm_g", 8, [last])
        at[0] = 0
        QT = region("QT", [128, 8, T])
        KTt = region("KTt", [128, 8, T])
        V = region("V", [128, 4, D])
        OQ = region("OQ", [128, 2, D])
        OT = uT
        O = {}
        units = []
        sts = {}
        V_r = []
        slabs = []
        for g in range(2):
            w = slab(wsrc("odd_w_in_0", 0, 8, 1024 + g * 512, 512))
            for f in range(4):
                add(f"k{g * 4 + f}", sub(w, f * 128), w, KTt[:, g * 4 + f, :], dfree=u)
            old = units[-1][0]
            units[-1][0] = lambda old=old, w=w, n=f"k{g * 4 + 3}": (old(), w.done(sts[n]["t"]))
            run_pipe(units, 3)
            units = []
        for g in range(2):
            w = slab(wsrc("odd_w_in_0", 0, 8, 2048 + g * 512, 512))
            for i in range(NT):
                b = pk.get()
                t = tm(b, w.view, i, [w.ready, u], 0, 512)
                s = evac(i, V[:, i, g * 512:(g + 1) * 512], b.ap, 1.0, t, u)
                b.done(s)
                V_r.append(s)
            w.done(t)
        for g in range(2):
            w = slab(wsrc("odd_w_in_0", 0, 8, g * 512, 512))
            for f in range(4):
                add(f"q{g * 4 + f}", sub(w, f * 128), w, QT[:, g * 4 + f, :], 0.125, dfree=u)
            old = units[-1][0]
            units[-1][0] = lambda old=old, w=w, n=f"q{g * 4 + 3}": (old(), w.done(sts[n]["t"]))
            run_pipe(units, 3)
            units = []
        uT_read = sts["q7"]["t"]

        lm = region("lm", [128, 128])
        lamb = region("lamb", [128, 256])
        lamb_d = POOL.dma(lamb, bass.AP(ins["odd_lambda"].tensor, 0, [[0, 128], [1, 256]]), dsem(), u)
        lv = region("lv", [128, 4])
        lvv = lamb.rearrange("p (a b d) -> p a b d", a=2, b=2)
        s = DVE(lambda e: e.tensor_tensor(lm.rearrange("p (a d) -> p a d", d=64), lvv[:, :, 0, :], lvv[:, :, 1, :], ALU.mult), lamb_d)
        s = DVE(lambda e: e.tensor_reduce(lv[:, 0:2], lm.rearrange("p (a d) -> p a d", d=64), AX.X, ALU.add), s)
        s = ACTL(lambda e: e.activation(lv[:, 0:2], lv[:, 0:2], ACT.Exp), s)
        s = DVE(lambda e: e.tensor_scalar(lv[:, 2:3], lv[:, 1:2], LAMBDA_INIT, None, ALU.subtract), s)
        lam_r = DVE(lambda e: e.tensor_tensor(lv[:, 2:3], lv[:, 2:3], lv[:, 0:1], ALU.subtract), s)
        subg = region("subg", [128, 1])
        subg_r = DVE(lambda e: e.tensor_scalar(subg, col("odd_subln_g", 0), 1.0 - LAMBDA_INIT, None, ALU.mult), cols_r, u)

        dS = Banks([0, 1, 2, 3])
        dP = Banks([4, 5])
        dO = Banks([6, 7])
        Oq = Ring([OQ[:, i, :] for i in range(2)])
        oT_s = []
        first_q = {"r": [last]}

        def diff_unit(hh, i, oq, ost):
            st = {}
            n = (i + 1) * 128
            Q = QT[:, hh, :]

            def s0():
                st["b"] = []
                for c in range(2):
                    b = dS.get()
                    p = slice(c * 64, c * 64 + 64)
                    PE(lambda e, b=b, p=p: e.matmul(b.ap[:, 0:n], Q[p, i * 128:(i + 1) * 128], KTt[p, hh, 0:n],
                                                    start=True, stop=False), sts[f"q{hh}"]["r"], sts[f"k{hh}"]["r"], b.free)
                    b.t = PE(lambda e, b=b: e.matmul(b.ap[:, i * 128:n], identb, causal, start=False, stop=True))
                    st["b"].append(b)

            def s1():
                m = st["m"] = small.get()
                st["p"], st["e"] = [], []
                for c in range(2):
                    b = st["b"][c]
                    s = DVE(lambda e, b=b, c=c: e.tensor_reduce(m.ap[:, c:c + 1], b.ap[:, 0:n], AX.X, ALU.max, negate=True),
                            b.t, m.free)
                    p = w2k.get()
                    x = ACTL(lambda e, b=b, c=c, p=p: e.activation(p.ap[:, 0:n], b.ap[:, 0:n], ACT.Exp, bias=m.ap[:, c:c + 1],
                                                                   accum_out=m.ap[:, 2 + c:3 + c]), s, p.free)
                    b.done(x)
                    st["p"].append(p)
                    st["e"].append(x)

            def s2():
                m = st["m"]
                p0, p1 = st["p"]
                s = DVE(lambda e: e.reciprocal(m.ap[:, 4:6], m.ap[:, 2:4]), st["e"])
                s = DVE(lambda e: e.tensor_scalar(p1.ap[:, 0:n], p1.ap[:, 0:n], m.ap[:, 5:6], lv[:, 2:3], ALU.mult, ALU.mult),
                        s, lam_r)
                s = DVE(lambda e: e.scalar_tensor_tensor(out=p0.ap[:, 0:n], in0=p0.ap[:, 0:n], scalar=m.ap[:, 4:5],
                                                         in1=p1.ap[:, 0:n], op0=ALU.mult, op1=ALU.add), s)
                m.done(s)
                p1.done(s)
                st["n"] = s

            def s3():
                p0 = st["p"][0]
                b = dP.get()
                for k in range(i + 1):
                    t = PE(lambda e, k=k: e.transpose(b.ap[:, k * 128:(k + 1) * 128], p0.ap[:, k * 128:(k + 1) * 128], ident),
                           st["n"], b.free)
                p0.done(t)
                x = st["x"] = w2t.get()
                s = ACTL(lambda e: e.activation(x.ap[:, 0:n], b.ap[:, 0:n], ACT.Copy), t, x.free)
                b.done(s)
                st["v"] = s

            def s4():
                x = st["x"]
                if hh % 4 == 0:
                    ost["b"] = dO.get()
                o = ost["b"]
                for k in range(i + 1):
                    t = PE(lambda e, k=k: e.matmul(o.ap[:, (hh % 4) * 128:(hh % 4 + 1) * 128], x.ap[:, k * 128:(k + 1) * 128],
                                                   V[:, k, hh * 128:(hh + 1) * 128], start=(k == 0), stop=(k == i)),
                           st["v"], V_r, o.free)
                x.done(t)
                if hh == 0:
                    ost["q"] = Oq.get()
                if hh % 4 == 3:
                    q = ost["q"]
                    hf = hh // 4
                    s = DVE(lambda e: e.tensor_copy(q.ap[:, hf * 512:(hf + 1) * 512], o.ap), t, q.free)
                    o.done(s)
                    ost[hf] = s
                if hh == 7:
                    q = ost["q"]
                    qv = q.ap.rearrange("p (a b) -> p a b", b=128)
                    sq = tmp4.get()
                    s = POOL(lambda e: e.tensor_tensor(sq.ap, q.ap, q.ap, ALU.mult), ost[0], ost[1], sq.free)
                    ss = small.get()
                    ss.ready = DVE(lambda e: e.tensor_reduce(ss.ap[:, 0:8], sq.ap.rearrange("p (a b) -> p a b", b=128), AX.X,
                                                             ALU.add), s, ss.free)
                    sq.done(ss.ready)
                    r = rstd_of(ss, 8, 1.0 / 128)
                    s = DVE(lambda e: e.tensor_tensor(qv, qv, r.ap[:, 0:8].unsqueeze(2).to_broadcast([128, 8, 128]), ALU.mult),
                            r.ready)
                    r.done(s)
                    ost["n"] = s
            return [s0, s1, s2, s3, s4]

        def turn_back(i, ost):
            q = ost["q"]
            for hf in range(2):
                b = dP.get()
                for k in range(4):
                    t = PE(lambda e, k=k, b=b, hf=hf: e.transpose(b.ap[:, k * 128:(k + 1) * 128],
                                                                  q.ap[:, (hf * 4 + k) * 128:(hf * 4 + k + 1) * 128], ident),
                           ost["n"], b.free)
                s = ACTL(lambda e, b=b, hf=hf: e.activation(
                    OT[:, hf * 4:hf * 4 + 4, i * 128:(i + 1) * 128], b.ap.rearrange("p (a b) -> p a b", b=128), ACT.Copy,
                    scale=subg), t, uT_read, subg_r)
                b.done(s)
                oT_s.append(s)
            q.done(t)

        units = []
        for i in range(NT):
            ost = {}
            for hh in range(8):
                u_ = diff_unit(hh, i, None, ost)
                units.append(u_)
            if i:
                old = units[-5][0]
                units[-5][0] = lambda old=old, i=i, prev=prev: (old(), turn_back(i - 1, prev))
            prev = ost
        run_pipe(units, 5)
        turn_back(3, prev)
        hr, last = residual("odd_w_out_0", lambda k, i: OT[:, k, i * 128:(i + 1) * 128], lambda k: oT_s)
        u = norm_T(hr, "mlp_norm_g", 8, [last])
        hr, last, _ = mlp("mlp_up_1", "mlp_down_1", u, u)
        def final_norm(name, after):
            g = big[:, 8192:8192 + D]
            gd = POOL.dma(g, bass.AP(ins[name].tensor, 0, [[0, 128], [1, D]]), dsem(), after)
            res = []
            for i in range(NT):
                r = rstd_of(sum_squares(h[:, i, :], hr[i]), 1, 1.0 / D)
                res.append(DVE(lambda e, i=i, r=r: e.scalar_tensor_tensor(
                    out=h[:, i, :], in0=h[:, i, :], scalar=r.ap[:, 0:1], in1=g, op0=ALU.mult, op1=ALU.mult), r.ready, gd))
                r.done(res[-1])
            return res

        hr = final_norm("final_norm_g", u)

        u = norm_T(hr, "norm_mix_2", 0, [last], meta=True)
        u0 = u
        at[0] = 0
        nq = region("nq", [128, 4, T])
        nk = region("nk", [128, 4, T + META])
        nv = region("nv", [128, 4, T])
        nbr = region("nbr", [128, 2, 896])
        at_hg = at[0]
        hv = region("hv", [128, 4, T])
        hsg = region("hsg", [128, 4, T])
        hq = region("hq", [128, 4, T])
        onT = region("onT", [128, 4, T])
        ohT = region("ohT", [128, 4, T])
        nvm = region("nvm", [META, T])
        hvm = region("hvm", [META, T])
        ST = region("ST", [128, 8, 128])
        oh = region("oh", [128, 4, 128])
        ohs = region("ohs", [128, 4, 128])

        def win(c0, n=512):
            return slab(wsrc("w_in_2_0", 0, 8, c0, n), 8, n)

        fb = Banks([0, 1, 2, 3])
        w = win(0)
        nq_r, nk_r, nv_r = [], [], []
        for f in range(4):
            b = fb.get()
            t = fm(b, sub(w, f * 128), [w.ready, u])
            s = evac(f, nq[:, f, :], b.ap[:, ::-1], 0.125, t, u)
            b.done(s)
            nq_r.append(s)
        w.done(t)
        w = win(512)
        for f in range(4):
            b = fb.get()
            t = fm(b, sub(w, f * 128), [w.ready, u])
            s = evac(f, nk[:, f, 0:T], b.ap, 1.0, t, u)
            b.done(s)
            b = fb.get()
            t = fm(b, sub(w, f * 128), [w.ready, u], T, META)
            s2 = evac(f, nk[:, f, T:T + META], b.ap[:, 0:META], 1.0, t, u)
            b.done(s2)
            nk_r.append([s, s2])
        w.done(t)

        def token_major(w, dest, destm, rr):
            for i in range(NT):
                b = fb.get()
                t = tm(b, w.view, i, [w.ready, u], 0, 512)
                s = evac(i, dest[:, i, :], b.ap, 1.0, t, u)
                b.done(s)
                rr.append(s)
            if destm is not None:
                b = fb.get()
                t = tm(b, w.view, 0, [w.ready, u], 0, 512, part=META, lhs=lambda k: uT[:, k, T:T + META])
                s = evac(0, destm, b.ap[0:META, :], 1.0, t)
                b.done(s)
                rr.append(s)
            w.done(t)

        token_major(win(1024), nv, nvm, nv_r)

        pad = nc.dram_tensor("pad", (8, 15, 128), F32, kind="Internal").ap()
        pz = dsem()
        s = POOL.dma(pad.rearrange("h a b -> (h a) b"), ins["c_zero"], pz)
        s = POOL.dma(pad[:, :, 48:79], ins["na_rpb_2"].rearrange("o h a b -> (o h) a b"), pz, s)
        nb_ring = Ring([nbr[:, i, :] for i in range(2)])
        nb_sem = [dsem(), dsem()]

        def bias(hh):
            b = nb_ring.get()
            for e2 in range(2):
                src = bass.AP(pad.tensor, hh * 15 * 128 + e2 * 128, [[1, 64], [128, 14], [1, 64]])
                d = POOL.dma(b.ap[e2 * 64:(e2 + 1) * 64, :].rearrange("p (a b) -> p a b", b=64), src, nb_sem[b.i], b.free, s, u)
            b.ready = POOL(lambda e: e.tensor_tensor(b.ap.rearrange("p (a b) -> p a b", b=64),
                                                     b.ap.rearrange("p (a b) -> p a b", b=64),
                                                     winm.unsqueeze(1).to_broadcast([128, 14, 64]), ALU.add), d, win_d)
            return b

        nS = [(0, 1), (2, 3)]
        nSat = [0]
        nP = Banks([4, 5])
        nO = Banks([6, 7])
        on_r = [None] * 4
        bias_of = {}

        def na_unit(hh, i, get, last):
            st = {}
            p = slice((hh % 2) * 64, (hh % 2) * 64 + 64)

            def s0():
                if i == 0:
                    bias_of[hh] = bias(hh)
                b0, b1 = fb.get(), fb.get()
                t0 = PE(lambda e: e.matmul(b0.ap, nq[p, hh // 2, T - (i + 1) * 128:T - i * 128], nk[p, hh // 2, 0:T],
                                           start=True, stop=True), nq_r[hh // 2], nk_r[hh // 2], b0.free)
                t1 = PE(lambda e: e.matmul(b1.ap[:, 0:META], nq[p, hh // 2, T - (i + 1) * 128:T - i * 128],
                                           nk[p, hh // 2, T:T + META], start=True, stop=True), b1.free)
                st["b"], st["t"] = (b0, b1), (t0, t1)

            def s1():
                b0, b1 = st["b"]
                q = st["q"] = w2k.get()
                bb = bias_of[hh]
                o = (6 - 2 * i) * 64
                x0 = DVE(lambda e: e.tensor_tensor(q.ap[:, 0:T], b0.ap, bb.ap[:, o:o + T], ALU.add), st["t"][0],
                         bb.ready, q.free)
                x1 = DVE(lambda e: e.tensor_copy(q.ap[:, T:T + META], b1.ap[:, 0:META]), st["t"][1])
                b0.done(x0)
                b1.done(x1)
                bb.done(x0)
                m = st["m"] = small.get()
                x = DVE(lambda e: e.tensor_reduce(m.ap[:, 0:1], q.ap, AX.X, ALU.max, negate=True), x0, x1, m.free)
                st["e"] = ACTL(lambda e: e.activation(q.ap, q.ap, ACT.Exp, bias=m.ap[:, 0:1], accum_out=m.ap[:, 1:2]), x)

            def s2():
                m, q = st["m"], st["q"]
                x = DVE(lambda e: e.reciprocal(m.ap[:, 2:3], m.ap[:, 1:2]), st["e"])
                st["n"] = DVE(lambda e: e.tensor_scalar(q.ap, q.ap, m.ap[:, 2:3], None, ALU.mult), x)
                m.done(st["n"])

            def s3():
                q = st["q"]
                b, b2 = nP.get(), nP.get()
                for k in range(4):
                    t = PE(lambda e, k=k: e.transpose(b.ap[:, k * 128:(k + 1) * 128], q.ap[:, k * 128:(k + 1) * 128], ident),
                           st["n"], b.free)
                t2 = PE(lambda e: e.transpose(b2.ap[0:META, 0:128], q.ap[:, T:T + META], ident), b2.free)
                q.done(t2)
                x, y = st["x"], st["y"] = w2t.get(), w2t.get()
                s = ACTL(lambda e: e.activation(x.ap[:, 0:T], b.ap, ACT.Copy), t, x.free)
                s2_ = DVE(lambda e: e.tensor_copy(y.ap[0:META, 0:128], b2.ap[0:META, 0:128]), t2, y.free)
                b.done(s)
                b2.done(s2_)
                st["v"] = (s, s2_)

            def s4():
                x, y = st["x"], st["y"]
                o = get()
                for k in range(4):
                    PE(lambda e, k=k: e.matmul(o.ap[p, T - (i + 1) * 128:T - i * 128], nv[:, k, hh * 64:hh * 64 + 64],
                                               x.ap[:, k * 128:(k + 1) * 128], start=(k == 0), stop=False),
                       st["v"], nv_r, o.free)
                t = PE(lambda e: e.matmul(o.ap[p, T - (i + 1) * 128:T - i * 128], nvm[:, hh * 64:hh * 64 + 64],
                                          y.ap[0:META, 0:128], start=False, stop=True))
                x.done(t)
                y.done(t)
                if last:
                    on_r[hh // 2] = ACTL(lambda e: e.activation(onT[:, hh // 2, :], o.ap[:, ::-1], ACT.Copy), t, u)
                    o.done(on_r[hh // 2])
            return [s0, s1, s2, s3, s4]

        na_units = []
        for j in range(4):
            st_ = {}

            def get(st_=st_):
                if "b" not in st_:
                    st_["b"] = nO.get()
                return st_["b"]
            for c in range(2):
                for i in range(NT):
                    na_units.append(na_unit(2 * j + c, i, get, c == 1 and i == 3))
        run_pipe(na_units, 5)

        lb = sb("lb", [128, 2, 2, 4])
        hgain = ohs.rearrange("p c t -> p (c t)")
        hgain_d = POOL.dma(hgain, bass.AP(ins["hg_norm_2"].tensor, 0, [[0, 128], [1, T]]), dsem(), u)
        lg = cols[:, ROW_AT["hg_lb_logits_2"]:ROW_AT["hg_lb_logits_2"] + 16].rearrange("p (a l k) -> p a l k", a=2, l=2)
        s1 = DVE(lambda e: e.tensor_tensor(lb[:, :, 0, :], lg[:, :, 1, :], lg[:, :, 0, :], ALU.subtract), cols_r)
        s2 = DVE(lambda e: e.tensor_tensor(lb[:, :, 1, :], lg[:, :, 0, :], lg[:, :, 1, :], ALU.subtract), cols_r)
        s3 = ACTL(lambda e: e.activation(lb, lb, ACT.Exp), s1, s2)
        s4 = DVE(lambda e: e.tensor_scalar(lb, lb, 1.0, None, ALU.add), s3)
        lb_r = DVE(lambda e: e.reciprocal(lb, lb), s4)

        hv_r = []
        token_major(win(3072), hv, hvm, hv_r)
        w = win(3584)
        hg_r = []
        for i in range(NT):
            b = fb.get()
            t = tm(b, w.view, i, [w.ready, u], 0, 512)
            x = w2k.get()
            a = ACTL(lambda e, b=b, x=x: e.activation(x.ap[:, 0:T], b.ap, ACT.Exp, scale=-1.0), t, x.free)
            a = DVE(lambda e, x=x: e.tensor_scalar(x.ap[:, 0:T], x.ap[:, 0:T], 1.0, None, ALU.add), a)
            a = DVE(lambda e, x=x: e.reciprocal(x.ap[:, 0:T], x.ap[:, 0:T]), a)
            a = DVE(lambda e, b=b, x=x: e.tensor_tensor(x.ap[:, 0:T], x.ap[:, 0:T], b.ap, ALU.mult), a)
            b.done(a)
            a = POOL(lambda e, i=i, x=x: e.tensor_tensor(hsg[:, i, :], x.ap[:, 0:T], hgain, ALU.mult), a, hgain_d, u)
            x.done(a)
            hg_r.append(a)
        w.done(t)
        w = win(1536)
        hq_r = []
        for f in range(4):
            b = fb.get()
            t = fm(b, sub(w, f * 128), [w.ready, u])
            x = w2k.get()
            a = ACTL(lambda e, b=b, x=x: e.activation(x.ap[:, 0:T], b.ap, ACT.Exp, scale=-1.0), t, x.free)
            a = DVE(lambda e, x=x: e.tensor_scalar(x.ap[:, 0:T], x.ap[:, 0:T], 1.0, None, ALU.add), a)
            a = DVE(lambda e, x=x: e.reciprocal(x.ap[:, 0:T], x.ap[:, 0:T]), a)
            a = DVE(lambda e, b=b, x=x, f=f: e.tensor_tensor(hq[:, f, :], x.ap[:, 0:T], b.ap, ALU.mult), a, u)
            b.done(a)
            x.done(a)
            hq_r.append(a)
        w.done(t)

        at[0] = 0
        FK = [[region(f"fk{d}{c}", [128, T + META]) for c in range(2)] for d in range(2)]
        SX = [region(f"sx{d}", [128, T + META]) for d in range(2)]
        Qt = [region(f"qt{d}", [128, T]) for d in range(2)]
        Kt = [region(f"kt{d}", [128, T + META]) for d in range(2)]
        AT = region("AT", [128, T])
        Kh = [Ring([region(f"kh{d}", [128, T + 128])]) for d in range(2)]
        assert at[0] <= at_hg
        wz = [win(2048), win(2560)]
        zr = {}
        free = {"fk": [on_r, on_r], "sx": [on_r, on_r], "qt": [on_r, on_r], "kt": [on_r, on_r], "AT": on_r, "ST": u,
                "oh": None}
        pz_b = Banks([0, 1])
        pA = Banks([2, 3, 4])
        pT = Banks([5])
        pKV = Banks([6])
        pOo = Banks([7])
        oh_r = [None] * 4
        LEV = (1, 2, 4, 8, 16, 32, 64)
        for hd in range(4):
            k_r, f_r = [None, None], [None, None]
            for d in range(2):
                f_, k_ = FK[d]
                parts = [(0, T)] + ([(T, META)] if d == 0 else [])
                ff, kk = [], []
                for c0, n in parts:
                    b = pz_b.get()
                    t = fm(b, sub(wz[d], hd * 128), [wz[d].ready, u], c0, n)
                    a1 = ACTL(lambda e, b=b, n=n, c0=c0, f_=f_: e.activation(f_[:, c0:c0 + n], b.ap[:, 0:n], ACT.Exp, scale=-1.0),
                              t, free["fk"][d])
                    a2 = ACTL(lambda e, b=b, n=n, c0=c0, k_=k_: e.activation(k_[:, c0:c0 + n], b.ap[:, 0:n], ACT.Exp),
                              t, free["fk"][d])
                    b.done(a2)
                    s = DVE(lambda e, n=n, c0=c0, f_=f_: e.tensor_scalar(f_[:, c0:c0 + n], f_[:, c0:c0 + n], 1.0, None, ALU.add), a1)
                    s = DVE(lambda e, n=n, c0=c0, f_=f_: e.reciprocal(f_[:, c0:c0 + n], f_[:, c0:c0 + n]), s)
                    ff.append(DVE(lambda e, n=n, c0=c0, f_=f_, d=d, hd=hd: e.tensor_scalar(
                        f_[:, c0:c0 + n], f_[:, c0:c0 + n], lb[:, d, 1, hd:hd + 1], lb[:, d, 0, hd:hd + 1], ALU.mult, ALU.add),
                        s, lb_r))
                    s = DVE(lambda e, n=n, c0=c0, k_=k_: e.tensor_scalar(k_[:, c0:c0 + n], k_[:, c0:c0 + n], 1.0, None, ALU.add), a2)
                    s = DVE(lambda e, n=n, c0=c0, k_=k_: e.reciprocal(k_[:, c0:c0 + n], k_[:, c0:c0 + n]), s)
                    kk.append(DVE(lambda e, n=n, c0=c0, k_=k_, d=d, hd=hd: e.tensor_scalar(
                        k_[:, c0:c0 + n], k_[:, c0:c0 + n], lb[:, d, 1, hd:hd + 1], None, ALU.mult), s, lb_r))
                zr[d] = t
                f_r[d], k_r[d] = ff, kk
            if hd == 3:
                wz[0].done(zr[0])
                wz[1].done(zr[1])
            s = POOL(lambda e: e.tensor_tensor(Kt[0][:, 0:T], FK[0][1][:, 0:T], FK[1][1][:, 0:T], ALU.add), k_r,
                     free["kt"][0])
            b = pA.get()
            for c in range(4):
                t = PE(lambda e, c=c, b=b, hd=hd: e.matmul(b.ap[:, c * 128:(c + 1) * 128], Kt[0][:, c * 128:(c + 1) * 128],
                                                           hq[:, hd, c * 128:(c + 1) * 128], start=True, stop=True),
                       s, hq_r[hd], b.free)
            at_r = DVE(lambda e, b=b: e.tensor_tensor(AT.rearrange("p (c t) -> p c t", t=128), b.ap.rearrange(
                "p (c t) -> p c t", t=128), ident.unsqueeze(1).to_broadcast([128, 4, 128]), ALU.mult), t, free["AT"])
            b.done(at_r)
            free["kt"][0] = t
            sx_r = [POOL(lambda e, d=d: e.memset(SX[d], 1.0), free["sx"][d]) for d in range(2)]
            q_r = [POOL(lambda e, d=d, hd=hd: e.tensor_copy(Qt[d], hq[:, hd, :]), hq_r[hd], free["qt"][d]) for d in range(2)]
            kt_r = [POOL(lambda e, d=d: e.tensor_copy(Kt[d][:, 0:T], FK[d][1][:, 0:T]), k_r[d], free["kt"][d]) for d in range(2)]
            p_r = [f_r[0], f_r[1]]
            for li, m in enumerate(LEV):
                for d in range(2):
                    L = T + META if (d == 0 and m <= 8) else T

                    def hv2(x, L=L, m=m):
                        return x[:, 0:L].rearrange("p (n two m) -> p n two m", two=2, m=m)
                    P_, S_, k_ = FK[d][0], SX[d], FK[d][1]
                    qs, ks = (1, 0) if d == 0 else (0, 1)
                    qsrc = hq[:, hd, :].rearrange("p (n two m) -> p n two m", two=2, m=m)
                    q_s = POOL(lambda e, m=m, P_=P_, d=d, qs=qs, qsrc=qsrc: e.tensor_tensor(
                        Qt[d].rearrange("p (n two m) -> p n two m", two=2, m=m)[:, :, qs, :], qsrc[:, :, qs, :],
                        P_[:, 0:T].rearrange("p (n two m) -> p n two m", two=2, m=m)[:, :, qs, :], ALU.mult),
                        p_r[d], q_r[d], free["qt"][d])
                    k_s = POOL(lambda e, m=m, S_=S_, k_=k_, d=d, ks=ks: e.tensor_tensor(
                        Kt[d][:, 0:T].rearrange("p (n two m) -> p n two m", two=2, m=m)[:, :, ks, :],
                        k_[:, 0:T].rearrange("p (n two m) -> p n two m", two=2, m=m)[:, :, ks, :],
                        S_[:, 0:T].rearrange("p (n two m) -> p n two m", two=2, m=m)[:, :, ks, :], ALU.mult),
                        sx_r[d], kt_r[d], k_r[d], free["kt"][d])
                    b = pA.get()
                    for c in range(4):
                        t = PE(lambda e, c=c, b=b, d=d: e.matmul(b.ap[:, c * 128:(c + 1) * 128], Kt[d][:, c * 128:(c + 1) * 128],
                                                                 Qt[d][:, c * 128:(c + 1) * 128], start=True, stop=True),
                               q_s, k_s, b.free)
                    free["qt"][d] = free["kt"][d] = t
                    mk = lev[:, (d * 7 + li) * 128:(d * 7 + li + 1) * 128].unsqueeze(1).to_broadcast([128, 4, 128])
                    at_r = DVE(lambda e, b=b, mk=mk: e.copy_predicated(
                        AT.rearrange("p (c t) -> p c t", t=128), mk, b.ap.rearrange("p (c t) -> p c t", t=128)),
                        t, at_r, lev_d)
                    b.done(at_r)
                    nb = L // (2 * m)
                    e0 = m - 1 if d == 0 else 0
                    s = DVE(lambda e, P_=P_, S_=S_, ks=ks, qs=qs, hv2=hv2, nb=nb, m=m, e0=e0: e.tensor_tensor(
                        hv2(S_)[:, :, ks, :], hv2(S_)[:, :, ks, :],
                        hv2(P_)[:, :, qs, e0:e0 + 1].to_broadcast([128, nb, m]), ALU.mult), p_r[d], sx_r[d], k_s)
                    sx_r[d] = s
                    p_r[d] = DVE(lambda e, P_=P_, ks=ks, qs=qs, hv2=hv2, nb=nb, m=m, e0=e0: e.tensor_tensor(
                        hv2(P_)[:, :, qs, :], hv2(P_)[:, :, qs, :],
                        hv2(P_)[:, :, ks, e0:e0 + 1].to_broadcast([128, nb, m]), ALU.mult), s, q_s)
                    q_r[d] = q_s
                    kt_r[d] = k_s
            kh_r = [None, None]
            for d in range(2):
                n = T + META if d == 0 else T
                kb = Kh[d].get()
                s = POOL(lambda e, d=d, n=n: e.tensor_tensor(Kt[d][:, 0:n], FK[d][1][:, 0:n], SX[d][:, 0:n], ALU.mult),
                         sx_r[d], k_r[d], free["kt"][d])
                q_s = POOL(lambda e, d=d, hd=hd: e.tensor_tensor(Qt[d], hq[:, hd, :], FK[d][0][:, 0:T], ALU.mult),
                           p_r[d], free["qt"][d])
                b = pT.get()
                for c in range(4):
                    t = PE(lambda e, c=c, b=b, d=d: e.transpose(b.ap[:, c * 128:(c + 1) * 128], Kt[d][:, c * 128:(c + 1) * 128],
                                                                ident), s, b.free)
                x = ACTL(lambda e, b=b, kb=kb: e.activation(kb.ap[:, 0:T], b.ap, ACT.Copy), t, kb.free)
                b.done(x)
                kh_r[d] = [x]
                if d == 0:
                    b = pT.get()
                    t = PE(lambda e, b=b, d=d: e.transpose(b.ap[0:META, 0:128], Kt[d][:, T:T + META], ident), b.free)
                    x = ACTL(lambda e, b=b, kb=kb: e.activation(kb.ap[0:META, T:T + 128], b.ap[0:META, 0:128], ACT.Copy), t)
                    b.done(x)
                    kh_r[d].append(x)
                free["kt"][d] = t
                Kh[d].cur = kb
                free["sx"][d] = s
                q_r[d] = q_s
            st_r = [None] * 8
            b = pKV.get()
            kf, kbk = Kh[0].cur.ap, Kh[1].cur.ap
            t = PE(lambda e, b=b, hd=hd, kf=kf: e.matmul(b.ap[:, 0:128], kf[0:META, T:T + 128], hvm[:, hd * 128:(hd + 1) * 128],
                                                         start=True, stop=True), kh_r[0], hv_r, b.free)
            st_r[0] = DVE(lambda e, b=b: e.tensor_copy(ST[:, 0, :], b.ap[:, 0:128]), t, free["ST"])
            b.done(st_r[0])
            for c in range(3):
                b = pKV.get()
                t = PE(lambda e, b=b, hd=hd, c=c, kf=kf: e.matmul(b.ap[:, 0:128], kf[:, c * 128:(c + 1) * 128],
                                                                  hv[:, c, hd * 128:(hd + 1) * 128], start=True, stop=True),
                       kh_r[0], hv_r, b.free)
                st_r[c + 1] = DVE(lambda e, b=b, c=c: e.scalar_tensor_tensor(
                    out=ST[:, c + 1, :], in0=ST[:, c, :], scalar=FK[0][0][:, c * 128 + 127:c * 128 + 128], in1=b.ap[:, 0:128],
                    op0=ALU.mult, op1=ALU.add), t, st_r[c], p_r[0], free["ST"])
                b.done(st_r[c + 1])
            Kh[0].cur.done(t)
            for c in (3, 2, 1):
                b = pKV.get()
                t = PE(lambda e, b=b, hd=hd, c=c, kbk=kbk: e.matmul(b.ap[:, 0:128], kbk[:, c * 128:(c + 1) * 128],
                                                                    hv[:, c, hd * 128:(hd + 1) * 128], start=True, stop=True),
                       kh_r[1], hv_r, b.free)
                if c == 3:
                    st_r[6] = DVE(lambda e, b=b: e.tensor_copy(ST[:, 6, :], b.ap[:, 0:128]), t, free["ST"])
                else:
                    st_r[c + 3] = DVE(lambda e, b=b, c=c: e.scalar_tensor_tensor(
                        out=ST[:, c + 3, :], in0=ST[:, c + 4, :], scalar=FK[1][0][:, c * 128:c * 128 + 1], in1=b.ap[:, 0:128],
                        op0=ALU.mult, op1=ALU.add), t, st_r[c + 4], p_r[1], free["ST"])
                b.done(st_r[c + 3])
            Kh[1].cur.done(t)
            free["fk"] = [[st_r[1:4], q_r[0], kt_r[0], free["sx"][0]], [st_r[4:7], q_r[1], kt_r[1], free["sx"][1]]]
            b = pOo.get()
            for c in range(4):
                o = b.ap[:, c * 128:(c + 1) * 128]
                cs = slice(c * 128, (c + 1) * 128)
                PE(lambda e, o=o, cs=cs, c=c, hd=hd: e.matmul(o, AT[:, cs], hv[:, c, hd * 128:(hd + 1) * 128], start=True,
                                                              stop=False), at_r, b.free)
                t = PE(lambda e, o=o, cs=cs, c=c: e.matmul(o, Qt[0][:, cs], ST[:, c, :], start=False, stop=(c == 3)),
                       q_r[0], st_r[c])
                if c < 3:
                    t = PE(lambda e, o=o, cs=cs, c=c: e.matmul(o, Qt[1][:, cs], ST[:, 4 + c, :], start=False, stop=True),
                           q_r[1], st_r[4 + c])
            free["AT"] = free["ST"] = t
            free["qt"] = [t, t]
            x = ACTL(lambda e, b=b: e.activation(oh, b.ap.rearrange("p (c t) -> p c t", t=128), ACT.Copy), t, free["oh"])
            b.done(x)
            s = POOL(lambda e: e.tensor_tensor(ohs, oh, oh, ALU.mult), x, hg_r)
            ss = small.get()
            ss.ready = DVE(lambda e, ss=ss: e.tensor_reduce(ss.ap[:, 0:4], ohs, AX.X, ALU.add), s, ss.free)
            r = rstd_of(ss, 4, 1.0 / 128)
            s = DVE(lambda e, r=r: e.tensor_tensor(oh, oh, r.ap[:, 0:4].unsqueeze(2).to_broadcast([128, 4, 128]), ALU.mult),
                    r.ready)
            r.done(s)
            s = DVE(lambda e, hd=hd: e.tensor_tensor(oh, oh, hsg[:, :, hd * 128:(hd + 1) * 128], ALU.mult), s, hg_r)
            b = pT.get()
            for c in range(4):
                t = PE(lambda e, c=c, b=b: e.transpose(b.ap[:, c * 128:(c + 1) * 128], oh[:, c, :], ident), s, b.free)
            free["oh"] = t
            oh_r[hd] = ACTL(lambda e, b=b, hd=hd: e.activation(ohT[:, hd, :], b.ap, ACT.Copy), t)
            b.done(oh_r[hd])

        mixT = big[:, 0:4096].rearrange("p (k n) -> p k n", n=T)
        mix_free = [on_r, oh_r, nk_r]
        mix_r = []
        parts = {}
        for br, (c0, wname, oT_, orr) in enumerate(((4096, "w_na_out_2_0", onT, on_r), (5120, "w_hg_out_2_0", ohT, oh_r))):
            wo = slab(wsrc(wname, 0, 4, 0, 1024), 4, 1024)
            for g in range(2):
                w = win(c0 + g * 512)
                for f in range(4):
                    ft = g * 4 + f
                    bg = allb.get()
                    t = fm(bg, sub(w, f * 128), [w.ready, u])
                    by = allb.get()
                    ty = fm(by, lambda k, ft=ft, wo=wo: wo.view[:, k, ft * 128:(ft + 1) * 128], [wo.ready, orr], kts=4,
                            rhs=lambda k, oT_=oT_: oT_[:, k, :])
                    x = w2k.get()
                    a = ACTL(lambda e, bg=bg, x=x: e.activation(x.ap[:, 0:T], bg.ap, ACT.Exp, scale=-1.0), t, x.free)
                    bg.done(a)
                    a = DVE(lambda e, x=x: e.tensor_scalar(x.ap[:, 0:T], x.ap[:, 0:T], 1.0, None, ALU.add), a)
                    a = DVE(lambda e, x=x: e.reciprocal(x.ap[:, 0:T], x.ap[:, 0:T]), a)
                    if br == 0:
                        a = DVE(lambda e, x=x, by=by, ft=ft: e.tensor_tensor(mixT[:, ft, :], x.ap[:, 0:T], by.ap, ALU.mult),
                                a, ty, mix_free)
                        by.done(a)
                        x.done(a)
                        parts[ft] = a
                    else:
                        a = DVE(lambda e, x=x, by=by: e.tensor_tensor(x.ap[:, 0:T], x.ap[:, 0:T], by.ap, ALU.mult), a, ty)
                        by.done(a)
                        a = POOL(lambda e, x=x, ft=ft: e.tensor_tensor(mixT[:, ft, :], mixT[:, ft, :], x.ap[:, 0:T], ALU.add),
                                 a, parts[ft])
                        x.done(a)
                        mix_r.append(a)
                w.done(t)
            wo.done(ty)
        hr, last = residual("w_o_2_0", lambda k, i: mixT[:, k, i * 128:(i + 1) * 128], lambda k: mix_r[k])
        u = norm_T(hr, "norm_mlp_2", 0, [last])
        hr, last, _ = mlp("w_up_2_0", "w_down_2_0", u, u)
        out_v = out.rearrange("a (i p) d -> (a p) i d", p=128)
        hr = final_norm("norm_final_2", u)
        stores = [SP.dma(out_v[:, i, :], h[:, i, :], dsem(), hr[i]) for i in range(NT)]
        number(lanes)

        block = ctx.enter_context(nc.Block())

        @block.sync
        def _(e):
            play(SP, e)
            for s in stores:
                e.wait_ge(s.sem.sem, s.count)

        @block.gpsimd
        def _(e):
            play(POOL, e)

        @block.scalar
        def _(e):
            play(ACTL, e)

        @block.tensor
        def _(e):
            play(PE, e)

        @block.vector
        def _(e):
            play(DVE, e)


_INS = ["x", "mix_norm_g", "mlp_norm_g", "even_w_in", "even_cmp_pe", "even_cmp_w1", "even_cmp_w2", "even_w_out",
        "odd_w_in", "odd_lambda", "odd_subln_g", "odd_w_out", "mlp_w_up", "mlp_w_down", "final_norm_g",
        "meta_tokens_2", "w_in_2", "w_na_out_2", "w_hg_out_2", "w_o_2", "w_up_2", "w_down_2", "norm_mix_2",
        "norm_mlp_2", "norm_final_2", "hg_norm_2", "na_rpb_2", "hg_lb_logits_2"]


def kernel(**inputs):
    import concourse.bacc as bacc
    from concourse.bass_utils import run_bass_kernel_spmd

    nc = bacc.Bacc("TRN2", target_bir_lowering=False, num_devices=1)
    arrays = {n: np.ascontiguousarray(inputs[n]) for n in _INS}
    arrays.update(shape_constants())
    ins = {}
    for n, a in arrays.items():
        ins[n] = nc.dram_tensor(n, a.shape, mybir.dt.from_np(a.dtype), kind="ExternalInput").ap()
    for n in ("even_w_in", "even_w_out"):
        ins[n] = ins[n][0]
    for n in ("odd_w_in", "odd_w_out", "w_in_2", "w_na_out_2", "w_hg_out_2", "w_o_2", "w_up_2", "w_down_2"):
        ins[n + "_0"] = ins[n][0]
    for k in range(2):
        ins[f"mlp_up_{k}"] = ins["mlp_w_up"][k]
        ins[f"mlp_down_{k}"] = ins["mlp_w_down"][k]
    out = nc.dram_tensor("out", (1, T, D), F32, kind="ExternalOutput").ap()
    build(nc, ins, out)
    r = run_bass_kernel_spmd(nc, [arrays], core_ids=[0])
    return r.results[0]["out"]
```

```python
import math
from contextlib import ExitStack

import numpy as np

import concourse.bass as bass
from concourse import mybir

F32 = mybir.dt.float32
BF16 = mybir.dt.bfloat16
U8 = mybir.dt.uint8
R32 = mybir.dt.float32r
ALU = mybir.AluOpType
ACT = mybir.ActivationFunctionType
AX = mybir.AxisListType

T = 512
D = 1024
NT = 4
KT = 8
META = 16
EPS = 1e-6
TAKE = 128
NEG = -1e30
TAKEN = -3e38
LAMBDA_INIT = 0.8 - 0.6 * math.exp(-0.3)

ROW_NAMES = [("mix_norm_g", 16), ("mlp_norm_g", 16), ("norm_mix_2", 8), ("norm_mlp_2", 8),
             ("hg_lb_logits_2", 16), ("even_cmp_pe", 32), ("odd_subln_g", 1)]
ROW_AT = {}
for _n, _k in ROW_NAMES:
    ROW_AT[_n] = sum(k for _, k in ROW_NAMES[:len(ROW_AT)])
NROWS = sum(k for _, k in ROW_NAMES)


def shape_constants():
    c = {}
    inv = (1.0 / (np.float32(10000.0) ** (np.arange(0, 64, 2, dtype=np.float32) / np.float32(64)))).astype(np.float32)
    ang = np.arange(T, dtype=np.float32)[None, :] * inv[:, None]
    c["c_cos"] = np.tile(np.cos(ang), (4, 1)).astype(np.float32)
    c["c_sin"] = np.tile(np.sin(ang), (4, 1)).astype(np.float32)
    rot = np.zeros((128, 128), np.float32)
    for b in (0, 64):
        for d in range(32):
            rot[b + 32 + d, b + d] = -1.0
            rot[b + d, b + 32 + d] = 1.0
    c["c_rot"] = rot
    c["c_ident"] = np.eye(128, dtype=np.float32)
    q = np.arange(128)
    c["c_causal"] = np.where(q[None, :] <= q[:, None], 0.0, NEG).astype(np.float32)
    n = np.arange(32)
    end = n * 16 + 31
    t = np.arange(T).reshape(NT, 128).transpose(1, 0)
    c["c_cmp"] = np.where(end[None, None, :] <= t[:, :, None], 0.0, NEG).astype(np.float32).reshape(128, 128)
    masks = []
    for m in (1, 2, 4, 8, 16, 32, 64):
        same = (q[:, None] // (2 * m)) == (q[None, :] // (2 * m))
        left = (q // m) % 2 == 0
        masks.append(same & left[:, None] & ~left[None, :])
    for m in range(7):
        masks.append(masks[m].T)
    c["c_lev"] = np.concatenate([m.astype(np.float32) for m in masks], axis=1)
    col = np.arange(64)
    start = np.clip(col - 8, 0, 48)
    inw = (col[None, :] >= start[:, None]) & (col[None, :] < start[:, None] + 16)
    c["c_win"] = np.tile(np.where(inw, 0.0, NEG).astype(np.float32)[::-1], (2, 1))
    c["c_zero"] = np.zeros((120, 128), np.float32)
    return c


class Step:
    __slots__ = ("go", "after", "lane", "sem", "count", "named")

    def __init__(self, go, after, lane, sem=None):
        self.go, self.after, self.lane, self.sem, self.count, self.named = go, after, lane, sem, 0, sem is not None


def flat(xs):
    for x in xs:
        if x is None:
            continue
        if isinstance(x, (list, tuple)):
            yield from flat(x)
        else:
            yield x


class Lane:

    def __init__(self, name, sem):
        self.name, self.sem, self.queue = name, sem, []

    def __call__(self, go, *after):
        s = Step(go, list(flat(after)), self)
        for a in s.after:
            a.named = True
        self.queue.append(s)
        return s

    def dma(self, out, in_, sem, *after):
        s = Step(lambda e: e.dma_start(out, in_), list(flat(after)), self, sem)
        for a in s.after:
            a.named = True
        self.queue.append(s)
        sem.total += 16
        s.count = sem.total
        return s


class DmaSem:
    def __init__(self, sem):
        self.sem, self.total = sem, 0


def number(lanes):
    for lane in lanes:
        n = 0
        for s in lane.queue:
            if s.sem is None and s.named:
                n += 1
                s.count = n


def play(lane, eng):
    seen = {}
    for s in lane.queue:
        for a in s.after:
            sem = a.lane.sem if a.sem is None else a.sem.sem
            if seen.get(id(sem), 0) < a.count:
                eng.wait_ge(sem, a.count)
                seen[id(sem)] = a.count
        i = s.go(eng)
        if s.sem is not None:
            i.then_inc(s.sem.sem, 16)
        elif s.named:
            i.then_inc(lane.sem, 1)


class Ring:

    def __init__(self, bufs):
        self.bufs, self.free, self.at = bufs, [[] for _ in bufs], 0

    def get(self):
        i = self.at % len(self.bufs)
        self.at += 1
        free, self.free[i] = self.free[i], []
        return Buf(self, i, self.bufs[i], free)


class Buf:
    def __init__(self, ring, i, ap, free):
        self.ring, self.i, self.ap, self.free = ring, i, ap, free

    def done(self, *steps):
        self.ring.free[self.i] += list(flat(steps))


def build(nc, ins, out):
    ctx = ExitStack()
    with ctx:
        def sb(name, shape, dt=F32):
            return ctx.enter_context(nc.sbuf_tensor(name, shape, dt))[tuple(slice(None) for _ in shape)]

        def sem(name):
            return ctx.enter_context(nc.semaphore(name))

        PE, DVE, ACTL, POOL, SP = [Lane(n, sem("s_" + n)) for n in ("pe", "dve", "act", "pool", "sp")]
        lanes = [PE, DVE, ACTL, POOL, SP]
        names = [0]

        def dsem():
            names[0] += 1
            return DmaSem(sem(f"d{names[0]}"))

        bank = [ctx.enter_context(nc.psum_tensor(f"bank{i}", [128, 512], F32))[:, :] for i in range(8)]
        bank_free = [[] for _ in range(8)]

        class Banks(Ring):
            def __init__(self, ids):
                self.bufs, self.at, self.ids = [bank[i] for i in ids], 0, ids

            def get(self):
                i = self.ids[self.at % len(self.ids)]
                self.at += 1
                free, bank_free[i] = bank_free[i], []
                return BankBuf(i, free)

        class BankBuf:
            def __init__(self, i, free):
                self.i, self.ap, self.free = i, bank[i], free

            def done(self, *steps):
                bank_free[self.i] += list(flat(steps))

        def const(name, shape, dt=F32, src=None, eng=None):
            t = sb("k_" + name, shape, dt)
            s = (eng or SP).dma(t, ins[name] if src is None else src, dsem())
            return t, s

        h = sb("h", [128, NT, D])
        h_ready = []
        x_v = ins["x"].rearrange("a (i p) d -> (a p) i d", p=128)
        for i in range(NT):
            h_ready.append(SP.dma(h[:, i, :], x_v[:, i, :], dsem()))
        rows = sb("rows", [NROWS, 128])
        rows_s = dsem()
        rows_d = None
        views = {
            "mix_norm_g": ins["mix_norm_g"].rearrange("l (k p) -> (l k) p", p=128),
            "mlp_norm_g": ins["mlp_norm_g"].rearrange("l (k p) -> (l k) p", p=128),
            "norm_mix_2": ins["norm_mix_2"].rearrange("l (k p) -> (l k) p", p=128),
            "norm_mlp_2": ins["norm_mlp_2"].rearrange("l (k p) -> (l k) p", p=128),
            "hg_lb_logits_2": ins["hg_lb_logits_2"].rearrange("a l (k p) -> (a l k) p", p=128),
            "even_cmp_pe": ins["even_cmp_pe"].rearrange("o c (l2 l) d -> (o c l2) (l d)", l=2),
            "odd_subln_g": ins["odd_subln_g"],
        }
        ident, ident_d = const("c_ident", [128, 128])
        for n, k in ROW_NAMES:
            rows_d = SP.dma(rows[ROW_AT[n]:ROW_AT[n] + k, :], views[n], rows_s)
        identb = sb("identb", [128, 128], BF16)
        causal = sb("causal", [128, 128], BF16)
        cmpm = sb("cmpm", [128, 128], BF16)
        cosT, cos_d = const("c_cos", [128, T])
        sinT, sin_d = const("c_sin", [128, T])
        rotm, rot_d = const("c_rot", [128, 128])
        winm, win_d = const("c_win", [128, 64], eng=POOL)
        half = sb("half", [128, 16])
        half_m = DVE(lambda e: e.memset(half, -0.5))

        uTh = sb("uTh", [128, KT, T + META], R32)
        uTl = sb("uTl", [128, KT, T + META], R32)
        STG = Ring([sb(f"stg{i}", [128, 2048]) for i in range(2)])
        stg_sem = [dsem() for _ in range(2)]
        WH = [sb(f"wh{i}", [128, 2048], R32) for i in range(2)]
        WL = [sb(f"wl{i}", [128, 2048], R32) for i in range(2)]
        WR = Ring([0, 1])
        ARENA = 17920
        arena_at = nc.sbuf_base
        big = sb("big", [128, ARENA])
        hTr = nc.alloc_sbuf_tensor_at("hTr", [128, 16384], R32, offset=arena_at)[:, :]
        cols = sb("cols", [128, 128])
        lev = sb("lev", [128, 14 * 128], U8)
        lev_f = POOL.dma(big[:, 0:14 * 128], ins["c_lev"], dsem())
        lev_d = POOL(lambda e: e.tensor_copy(lev, big[:, 0:14 * 128]), lev_f)
        small = Ring([sb(f"sm{i}", [128, 16]) for i in range(24)])
        w2k = Ring([sb(f"p{i}", [128, 528]) for i in range(5)])
        w2t = Ring([sb(f"t{i}", [128, 528]) for i in range(4)])
        tmp4 = Ring([sb(f"q{i}", [128, D]) for i in range(2)])
        c1 = SP.dma(big[:, 1792:1920], ins["c_causal"], dsem())
        c2 = SP.dma(big[:, 1920:2048], ins["c_cmp"], dsem())
        identb_d = POOL(lambda e: e.tensor_copy(identb, ident), ident_d)
        causal_d = POOL(lambda e: e.tensor_copy(causal, big[:, 1792:1920]), c1)
        cmpm_d = POOL(lambda e: e.tensor_copy(cmpm, big[:, 1920:2048]), c2)
        tmp_sem = [dsem(), dsem()]

        class Piece:
            pass

        stg_user = [None, None]

        def load(spec):
            p = Piece()
            p.key, p.kts, p.ncols, parts, p.raw_only = spec
            p.st = STG.get()
            stg_user[p.st.i] = p
            p.let_go = False
            p.raw = p.st.ap[:, 0:p.kts * p.ncols].rearrange("p (k n) -> p k n", n=p.ncols)
            for dst, src in parts:
                p.loaded = SP.dma(dst(p.raw), src, stg_sem[p.st.i], p.st.free)
            return p

        def split(p):
            if p.raw_only:
                def done(*steps):
                    p.st.done(*steps)
                    p.let_go = True
                    weights.fill()
                p.ready, p.done = p.loaded, done
                return
            b = WR.get()
            n = p.kts * p.ncols
            hi, lo, st = WH[b.i][:, 0:n], WL[b.i][:, 0:n], p.st.ap[:, 0:n]
            a = ACTL(lambda e: e.activation(hi, st, ACT.Copy), p.loaded, b.free)
            d = DVE(lambda e: e.tensor_tensor(lo, st, hi.bitcast(F32), ALU.subtract), a)
            p.st.done(a, d)
            p.let_go = True
            p.ready = [a, d]
            p.h = hi.rearrange("p (k n) -> p k n", n=p.ncols)
            p.l = lo.rearrange("p (k n) -> p k n", n=p.ncols)
            p.done = b.done

        class Stream:

            def __init__(self, specs):
                self.specs, self.loaded, self.split, self.ahead = specs, [], [], 1

            def fill(self):
                more = True
                while more:
                    more = False
                    user = stg_user[STG.at % 2]
                    if len(self.loaded) < 2 and self.specs and (user is None or user.let_go):
                        self.loaded.append(load(self.specs.pop(0)))
                        more = True
                    if len(self.split) < self.ahead and self.loaded:
                        p = self.loaded.pop(0)
                        split(p)
                        self.split.append(p)
                        more = True

            def take(self, key):
                self.ahead = 2
                self.fill()
                p = self.split.pop(0)
                self.ahead = 1
                assert p.key == key, (p.key, key)
                return p

        def whole(v):
            return v

        def wsrc(name, r0, kts, c0, ncols):
            return ins[name][r0:r0 + kts * 128, c0:c0 + ncols].rearrange("(k p) n -> p k n", p=128)

        def fm_piece(key, name, c0, raw=False):
            return (key, 8, 256, [(whole, wsrc(name, 0, 8, c0, 256))], raw)

        def tm_piece(key, name, k0, c0, n=512, kts=4, raw=False):
            return (key, kts, n, [(whole, wsrc(name, k0 * 128, kts, c0, n))], raw)

        def at_cols(c0, n, dst):
            return (lambda v: v[:, :, dst:dst + n]), wsrc("even_w_in", 0, 8, c0, n)

        def group_cols(j0):
            return [((lambda v, k=k, g=g: v[:, k, :].rearrange("p (j g d) -> p g j d", g=2, j=2)[:, g]),
                     ins["even_w_in"][k * 128:(k + 1) * 128, 964 + g * 256 + j0 * 64:964 + g * 256 + (j0 + 2) * 64]
                     .rearrange("p (j d) -> p j d", j=2)) for g in range(2) for k in range(KT)]

        def cmp_w1(c, hf):
            return ("w1", 8, 256, [(whole, ins["even_cmp_w1"][0, c][hf * 1024:(hf + 1) * 1024, :].rearrange(
                "(k p) n -> p k n", p=128))], True)

        def even_out(c, hf):
            src = ins["even_w_out"][:, c * 512:(c + 1) * 512]
            if hf == 0:
                return ("out", 4, 512, [(whole, src[0:512, :].rearrange("(k p) n -> p k n", p=128))], False)
            hi = src[512:1024, :].rearrange("(g j d) n -> g d j n", g=2, j=4)
            return ("out", 4, 512, [((lambda v, g=g: v[g * 64:(g + 1) * 64]), hi[g]) for g in range(2)], False)

        def mlp_pieces(up, down):
            def ups(q):
                return [fm_piece("up", up, q * 1024 + g * 256) for g in range(4)]

            def downs(q):
                return [tm_piece("down", down, q * 8 + g * 4, c * 512) for c in range(2) for g in range(2)]
            return ups(0) + ups(1) + downs(0) + ups(2) + downs(1) + ups(3) + downs(2) + downs(3)

        def out_pieces(name):
            return [tm_piece("out", name, g * 4, c * 512) for c in range(2) for g in range(2)]

        specs = [
            ("P1", 8, 256, [at_cols(896, 64, 0), at_cols(896, 64, 64), at_cols(640, 128, 128)], False),
            ("P2", 8, 256, [at_cols(768, 128, 0), at_cols(512, 64, 128), at_cols(512, 64, 192)], False),
            ("P3", 8, 68, [at_cols(576, 64, 0), at_cols(960, 4, 64)], False),
            fm_piece("qa", "even_w_in", 0), fm_piece("qa", "even_w_in", 256),
            fm_piece("kvc", "even_w_in", 1476),
            ("ksw", 8, 256, [at_cols(1732, 128, 0), at_cols(1988, 128, 128)], False),
            ("vs", 8, 152, [at_cols(1860, 128, 0), at_cols(2244, 24, 128)], False),
            ("vw", 8, 128, [at_cols(2116, 128, 0)], False),
            ("qb", 8, 256, group_cols(0), False), ("qb", 8, 256, group_cols(2), False),
            cmp_w1(0, 0), cmp_w1(0, 1), cmp_w1(1, 0), cmp_w1(1, 1),
            even_out(0, 0), even_out(0, 1), even_out(1, 0), even_out(1, 1)]
        specs += mlp_pieces("mlp_up_0", "mlp_down_0")
        specs += [fm_piece("k", "odd_w_in_0", 1024 + g * 256) for g in range(4)]
        specs += [tm_piece("v", "odd_w_in_0", k0, 2048 + c * 512) for c in range(2) for k0 in (0, 4)]
        specs += [fm_piece("q", "odd_w_in_0", g * 256) for g in range(4)]
        specs += out_pieces("odd_w_out_0") + mlp_pieces("mlp_up_1", "mlp_down_1")
        W2 = "w_in_2_0"
        specs += [fm_piece("nq", W2, 0), fm_piece("nq", W2, 256), fm_piece("nk", W2, 512), fm_piece("nk", W2, 768)]
        specs += [tm_piece("tok", W2, k0, c) for c in (1024, 3072, 3584) for k0 in (0, 4)]
        specs += [fm_piece("hq", W2, 1536), fm_piece("hq", W2, 1792)]
        specs += [("z", 8, 256, [((lambda v: v[:, :, 0:128]), wsrc(W2, 0, 8, 2048 + d * 128, 128)),
                                 ((lambda v: v[:, :, 128:256]), wsrc(W2, 0, 8, 2560 + d * 128, 128))], False)
                  for d in range(4)]
        for c0, wname in ((4096, "w_na_out_2_0"), (5120, "w_hg_out_2_0")):
            for g in range(2):
                specs += [tm_piece("y", wname, 0, g * 512, raw=True), fm_piece("gate", W2, c0 + g * 512),
                          fm_piece("gate", W2, c0 + g * 512 + 256)]
        specs += out_pieces("w_o_2_0") + mlp_pieces("w_up_2_0", "w_down_2_0")
        weights = Stream(specs)

        allb = Banks(list(range(8)))

        b = allb.get()
        s = PE(lambda e, b=b: e.transpose(b.ap[:, 0:NROWS], rows[:, :], ident[0:NROWS, 0:NROWS]), rows_d, ident_d)
        cols_r = DVE(lambda e, b=b: e.tensor_copy(cols[:, 0:NROWS], b.ap[:, 0:NROWS]), s)
        b.done(cols_r)

        def col(name, k):
            return cols[:, ROW_AT[name] + k:ROW_AT[name] + k + 1]

        def rstd_of(ss, n, scale, part=128):
            v = small.get()
            s1 = DVE(lambda e: e.tensor_scalar(v.ap[0:part, 0:n], ss.ap[0:part, 0:n], scale, EPS, ALU.mult, ALU.add),
                     ss.ready, v.free)
            ss.done(s1)
            r = small.get()
            r.ready = POOL(lambda e: e.tensor_tensor(r.ap[0:part, 0:n], v.ap[0:part, 0:n], half[0:part, 0:n], ALU.pow),
                           s1, half_m, r.free)
            v.done(r.ready)
            return r

        def sum_squares(src, ready, part=128):
            junk = tmp4.get()
            ss = small.get()
            ss.ready = ACTL(lambda e: e.activation(junk.ap[0:part, :], src, ACT.Square,
                                                   accum_out=ss.ap[0:part, 0:1]), ready, junk.free, ss.free)
            junk.done(ss.ready)
            return ss

        def evac(n, outp, inp, scale, *after):
            if n % 2:
                return ACTL(lambda e: e.activation(outp, inp, ACT.Copy, scale=scale), *after)
            return DVE(lambda e: e.tensor_scalar(outp, inp, scale, None, ALU.mult), *after)

        def parts_of(hi, lo, src, scale, *after):
            a = ACTL(lambda e: e.activation(hi, src, ACT.Copy, scale=scale), *after)
            d = DVE(lambda e: e.scalar_tensor_tensor(out=lo, in0=src, scalar=scale, in1=hi.bitcast(F32), op0=ALU.mult,
                                                     op1=ALU.subtract), a)
            return [a, d]

        def norm_T(h_ready, gname, g0, uT_free, meta=None):
            scaled = []
            ready = [None] * NT
            xs = [big[:, ARENA - (i + 1) * D:ARENA - i * D] for i in range(NT)]
            for i in range(NT):
                r = rstd_of(sum_squares(h[:, i, :], h_ready[i]), 1, 1.0 / D)
                ready[i] = DVE(lambda e, i=i, r=r: e.tensor_scalar(xs[i], h[:, i, :], r.ap[:, 0:1], None, ALU.mult),
                               r.ready, h_ready[i], uT_free)
                r.done(ready[i])
            out_steps = []
            mready = []
            if meta is not None:
                mx = tmp4.get()
                hm_d = POOL.dma(mx.ap[0:META, :], ins["meta_tokens_2"], tmp_sem[mx.i], mx.free)
                r = rstd_of(sum_squares(mx.ap[0:META, :], hm_d, META), 1, 1.0 / D, META)
                ms = DVE(lambda e: e.tensor_scalar(mx.ap[0:META, :], mx.ap[0:META, :], r.ap[0:META, 0:1], None, ALU.mult),
                         r.ready)
                r.done(ms)
                mb = allb.get()
                for k in range(KT):
                    t = PE(lambda e, k=k: e.transpose(mb.ap[:, k * META:(k + 1) * META],
                                                      mx.ap[0:META, k * 128:(k + 1) * 128], ident[0:META, 0:META]),
                           ms, mb.free)
                mx.done(t)
                y = w2k.get()
                yv = y.ap[:, 0:KT * META].rearrange("p (k n) -> p k n", n=META)
                gc = cols[:, ROW_AT[gname] + g0:ROW_AT[gname] + g0 + KT].unsqueeze(2).to_broadcast([128, KT, META])
                ym = DVE(lambda e: e.tensor_tensor(yv, mb.ap[:, 0:KT * META].rearrange("p (k n) -> p k n", n=META), gc,
                                                   ALU.mult), t, cols_r, y.free)
                mready = parts_of(uTh[:, :, T:T + META], uTl[:, :, T:T + META], yv, 1.0, ym, uT_free)
                y.done(mready)
                mready.append(ym)
                mb.done(mready)
            for k in range(KT):
                b = allb.get()
                for i in range(NT):
                    t = PE(lambda e, i=i, k=k, b=b: e.transpose(b.ap[:, i * 128:(i + 1) * 128],
                                                                xs[i][:, k * 128:(k + 1) * 128], ident), ready[i], b.free, ident_d)
                s = parts_of(uTh[:, k, 0:T], uTl[:, k, 0:T], b.ap, col(gname, g0 + k), t, cols_r, uT_free)
                b.done(s)
                out_steps += s
            return out_steps + mready

        def products(outp, pairs, start, stop, *after):
            n = len(pairs)
            for k, (lh, ll, rh, rl) in enumerate(pairs):
                for m, (x, y) in enumerate(((lh, rh), (lh, rl), (ll, rh))):
                    t = PE(lambda e, x=x, y=y, k=k, m=m: e.matmul(outp, x, y, start=(start and k == 0 and m == 0),
                                                                  stop=(stop and k == n - 1 and m == 2)), *after)
            return t

        def fm(bk, w, c0, ready, n0=0, n=T):
            return products(bk.ap[:, 0:n], [(w.h[:, k, c0:c0 + 128], w.l[:, k, c0:c0 + 128],
                                             uTh[:, k, n0:n0 + n], uTl[:, k, n0:n0 + n]) for k in range(KT)],
                            True, True, w.ready, ready, bk.free)

        def tm(outp, w, t0, part, c0, ncols, k0, start, stop, *after):
            return products(outp, [(uTh[:, k0 + k, t0:t0 + part], uTl[:, k0 + k, t0:t0 + part],
                                    w.h[:, k, c0:c0 + ncols], w.l[:, k, c0:c0 + ncols]) for k in range(w.kts)],
                            start, stop, w.ready, *after)

        def run_pipe(units, depth):
            for n in range(len(units) + depth - 1):
                for d in range(depth - 1, -1, -1):
                    if 0 <= n - d < len(units):
                        units[n - d][d]()

        def rope_unit(bk, key, half, dest, scale, ready, dfree):
            st = {}

            def s0():
                st["b"] = bk.get()
                if half == 0:
                    taken[0] = weights.take(key)
                st["t"] = fm(st["b"], taken[0], half * 128, ready)
                if half == 1:
                    taken[0].done(st["t"])

            def s1():
                x = st["x"] = w2k.get()
                b = st["b"]
                st["c"] = ACTL(lambda e: e.activation(x.ap[:, 0:T], b.ap, ACT.Copy, scale=scale), st["t"], x.free)
                b.done(st["c"])

            def s2():
                x, y, t1 = st["x"], bk.get(), w2t.get()
                a = PE(lambda e: e.matmul(y.ap, rotm, x.ap[:, 0:T], start=True, stop=True), st["c"], y.free, rot_d)
                p = POOL(lambda e: e.tensor_tensor(t1.ap[:, 0:T], x.ap[:, 0:T], cosT, ALU.mult), st["c"], t1.free, cos_d)
                x.done(a, p)
                t2 = w2t.get()
                q = DVE(lambda e: e.tensor_tensor(t2.ap[:, 0:T], y.ap, sinT, ALU.mult), a, t2.free, sin_d)
                y.done(q)
                r = DVE(lambda e: e.tensor_tensor(dest, t1.ap[:, 0:T], t2.ap[:, 0:T], ALU.add), p, q, dfree)
                t1.done(r)
                t2.done(r)
                st["r"] = r
            return [s0, s1, s2], st

        def add_products(lhs, nk, lready, key="out"):
            new = [None] * NT
            for c in range(2):
                bks = [allb.get() for _ in range(NT)]
                for g in range(nk // 4):
                    w = weights.take(key)
                    for i in range(NT):
                        t = products(bks[i].ap, [(*lhs(g * 4 + k, i), w.h[:, k, :], w.l[:, k, :]) for k in range(4)],
                                     g == 0, g == nk // 4 - 1, w.ready, bks[i].free,
                                     [lready(g * 4 + k) for k in range(4)])
                        if g == nk // 4 - 1:
                            new[i] = DVE(lambda e, i=i, c=c, bks=bks: e.tensor_tensor(
                                h[:, i, c * 512:(c + 1) * 512], h[:, i, c * 512:(c + 1) * 512], bks[i].ap, ALU.add), t,
                                h_last[i])
                            h_last[i] = new[i]
                            bks[i].done(new[i])
                    w.done(t)
            return list(new), t

        h_last = [None] * NT
        taken = [None]

        def from_uT(k, i):
            return uTh[:, k, i * 128:(i + 1) * 128], uTl[:, k, i * 128:(i + 1) * 128]

        def mlp(uready, big_free):
            hT = [[hTr[:, (q * 2 + x) * 4096:(q * 2 + x + 1) * 4096].rearrange("p (k n) -> p k n", n=T)
                   for x in range(2)] for q in range(2)]
            free = [big_free, big_free]

            def up_quarter(q):
                hready = []
                for g in range(4):
                    w = weights.take("up")
                    for f in range(2):
                        b = allb.get()
                        t = fm(b, w, f * 128, uready)
                        r = w2k.get()
                        a = ACTL(lambda e, b=b, r=r: e.activation(r.ap[:, 0:T], b.ap, ACT.Relu), t, r.free)
                        b.done(a)
                        p = POOL(lambda e, r=r: e.tensor_tensor(r.ap[:, 0:T], r.ap[:, 0:T], r.ap[:, 0:T], ALU.mult), a)
                        hi, lo = (hT[q % 2][x][:, g * 2 + f, :] for x in range(2))
                        a = ACTL(lambda e, r=r, hi=hi: e.activation(hi, r.ap[:, 0:T], ACT.Copy), p, free[q % 2])
                        d = DVE(lambda e, r=r, hi=hi, lo=lo: e.tensor_tensor(lo, r.ap[:, 0:T], hi.bitcast(F32),
                                                                             ALU.subtract), a)
                        r.done(d)
                        hready.append([a, d])
                    w.done(t)
                return hready, t

            def down_quarter(q, hready):
                new, t = add_products(lambda k, i: tuple(hT[q % 2][x][:, k, i * 128:(i + 1) * 128] for x in range(2)),
                                      8, lambda k: hready[k], "down")
                free[q % 2] = t
                return new, t
            hready, _ = up_quarter(0)
            for q in range(4):
                after, uread = up_quarter(q + 1) if q < 3 else (None, uread)
                new, last = down_quarter(q, hready)
                hready = after
            return new, last, uread

        A = {}
        at = [0]

        def region(name, shape, base=None):
            n = int(np.prod(shape[1:]))
            o = at[0]
            at[0] += n
            assert at[0] <= ARENA, (name, at[0])
            v = big[0:shape[0], o:o + n]
            if len(shape) == 3:
                v = v.rearrange("p (a b) -> p a b", b=shape[2])
            A[name] = v
            return v

        u0 = norm_T(h_ready, "mix_norm_g", 0, []) + [lev_d, causal_d, cmpm_d]
        EV = "even_w_in"
        qaT = region("qaT", [128, 4, T])
        kaT = region("kaT", [128, T])
        va = region("va", [128, 4, 64])
        qiT = region("qiT", [128, 2, T])
        kiT = region("kiT", [128, T])
        qbT = region("qbT", [128, 4, T])
        kcT = region("kcT", [128, T])
        ksT = region("ksT", [128, T])
        vsb = region("vsb", [128, 4, 128])
        kwT = region("kwT", [128, T])
        vcT = region("vcT", [128, T])
        vw = region("vw", [128, 4, 128])
        wi = sb("wi", [128, 16])
        gate = sb("gate", [128, 4, 24])
        pk = Banks([0, 1, 2, 3, 4, 5])
        pv2 = Banks([6, 7])
        xs_read = u0

        units, sts = [], {}

        def add(name, key, half, dest, scale=1.0, dfree=()):
            u, st = rope_unit(pk, key, half, dest, scale, u0, list(dfree))
            units.append(u)
            sts[name] = st

        add("ki", "P1", 0, kiT)
        add("qi0", "P1", 1, qiT[:, 0, :])
        add("qi1", "P2", 0, qiT[:, 1, :])
        add("ka", "P2", 1, kaT)
        run_pipe(units, 3)
        w = weights.take("P3")
        b = pk.get()
        for i in range(NT):
            t = tm(b.ap[:, i * 128:i * 128 + 68], w, i * 128, 128, 0, 68, 0, True, True, u0, b.free)
        w.done(t)
        wi_r = DVE(lambda e, b=b: e.tensor_copy(wi.rearrange("p (a b) -> p a b", b=4),
                                                b.ap.rearrange("p (a b) -> p a b", b=128)[:, :, 64:68]), t)
        va_r = DVE(lambda e, b=b: e.tensor_copy(va, b.ap.rearrange("p (a b) -> p a b", b=128)[:, :, 0:64]), t, u0)
        b.done(wi_r, va_r)

        sc = {i: region(f"sc{i}", [128, (i + 1) * 128]) for i in (1, 2, 3)}
        sel = sb("sel", [128, 3, T], BF16)
        sc_r = {}
        for i in (1, 2, 3):
            n = (i + 1) * 128
            for hh in range(4):
                b = pk.get()
                p0 = (hh % 2) * 64
                t = PE(lambda e, b=b, i=i, hh=hh, p0=p0, n=n: e.matmul(
                    b.ap[:, 0:n], qiT[p0:p0 + 64, hh // 2, i * 128:(i + 1) * 128], kiT[p0:p0 + 64, 0:n],
                    start=True, stop=True), sts[f"qi{hh // 2}"]["r"], sts["ki"]["r"], b.free)
                r = w2k.get()
                a = ACTL(lambda e, b=b, r=r, n=n: e.activation(r.ap[:, 0:n], b.ap[:, 0:n], ACT.Relu), t, r.free)
                b.done(a)
                wc = wi[:, i * 4 + hh:i * 4 + hh + 1]
                if hh == 0:
                    s = DVE(lambda e, r=r, i=i, n=n, wc=wc: e.tensor_scalar(sc[i][:, 0:n], r.ap[:, 0:n], wc, None, ALU.mult),
                            a, wi_r)
                else:
                    s = DVE(lambda e, r=r, i=i, n=n, wc=wc: e.scalar_tensor_tensor(
                        out=sc[i][:, 0:n], in0=r.ap[:, 0:n], scalar=wc, in1=sc[i][:, 0:n], op0=ALU.mult, op1=ALU.add),
                        a, wi_r, sc_r[i])
                r.done(s)
                sc_r[i] = s
            sc_r[i] = DVE(lambda e, i=i: e.tensor_tensor(sc[i][:, i * 128:(i + 1) * 128], sc[i][:, i * 128:(i + 1) * 128],
                                                         causal, ALU.add), sc_r[i], causal_d)

        m8 = sb("m8", [128, 3, 8])

        def topk():
            for _ in range(TAKE // 8):
                for i in (1, 2, 3):
                    n = (i + 1) * 128
                    s = DVE(lambda e, i=i, n=n: e.max(m8[:, i - 1, :], sc[i][:, 0:n]), sc_r[i])
                    sc_r[i] = DVE(lambda e, i=i, n=n: e.match_replace(sc[i][:, 0:n], m8[:, i - 1, :], sc[i][:, 0:n], TAKEN), s)
                    yield
            for i in (1, 2, 3):
                n = (i + 1) * 128
                sc_r[i] = DVE(lambda e, i=i, n=n: e.tensor_scalar(sel[:, i - 1, 0:n], sc[i][:, 0:n], -2e38, NEG,
                                                                  ALU.is_gt, ALU.mult), sc_r[i])

        taking = topk()

        def advance(g, n):
            for _ in range(n):
                if next(g, "end") == "end":
                    break

        units = []
        for j in range(4):
            add(f"qa{j}", "qa", j % 2, qaT[:, j, :], 0.125)
        add("kc", "kvc", 0, kcT)
        run_pipe(units, 3)
        b = pk.get()
        t = fm(b, taken[0], 128, u0)
        taken[0].done(t)
        vc_r = ACTL(lambda e, b=b: e.activation(vcT, b.ap, ACT.Copy), t)
        b.done(vc_r)
        X = [region(f"X{c}", [128, 2, T]) for c in range(2)]
        X_r = []
        for c, (src, r) in enumerate(((kcT, sts["kc"]["r"]), (vcT, vc_r))):
            xs = dsem()
            X_m = DVE(lambda e, c=c: e.memset(X[c][64:128, :, T - 1:T], 0.0), u0)
            for g in range(2):
                d1 = POOL.dma(X[c][0:64, g, :], src[g * 64:(g + 1) * 64, :], xs, r)
                d2 = POOL.dma(X[c][64:128, g, 0:T - 1], src[g * 64:(g + 1) * 64, 1:T], xs, r)
            X_r.append([d2, X_m])
        units = []
        add("ks", "ksw", 0, ksT)
        add("kw", "ksw", 1, kwT)
        run_pipe(units, 3)
        w = weights.take("vs")
        vs_r, gb_r = [], []
        for i in range(NT):
            b = pk.get()
            t = tm(b.ap[:, 0:152], w, i * 128, 128, 0, 152, 0, True, True, u0, b.free)
            vs_r.append(DVE(lambda e, b=b, i=i: e.tensor_copy(vsb[:, i, :], b.ap[:, 0:128]), t))
            gb_r.append(ACTL(lambda e, b=b, i=i: e.activation(gate[:, i, :], b.ap[:, 128:152], ACT.Exp, scale=-1.0), vs_r[-1]))
            b.done(vs_r[-1], gb_r[-1])
        w.done(t)
        w = weights.take("vw")
        b = pk.get()
        for i in range(NT):
            t = tm(b.ap[:, i * 128:(i + 1) * 128], w, i * 128, 128, 0, 128, 0, True, True, u0, b.free)
        vw_r = DVE(lambda e, b=b: e.tensor_copy(vw, b.ap.rearrange("p (a b) -> p a b", b=128)), t)
        b.done(vw_r)
        w.done(t)
        units = []
        for j in range(4):
            add(f"qb{j}", "qb", j % 2, qbT[:, j, :], 0.125)
        run_pipe(units, 3)
        g2 = DVE(lambda e: e.tensor_scalar(gate, gate, 1.0, None, ALU.add), gb_r)
        gate_r = DVE(lambda e: e.reciprocal(gate, gate), g2)
        advance(taking, 10)

        cH = region("cH", [128, 4, 62])
        cG = region("cG", [128, 4, 62])
        cb = sb("cb", [128, 4])
        w2s = region("w2s", [128, 4, 64])
        w2_d = POOL.dma(w2s, ins["even_cmp_w2"].rearrange("o c (f p) d -> p (o c f) d", p=128), dsem(), u0)
        kcc = region("kcc", [128, 32])
        vcc = region("vcc", [32, 2, 64])
        hs = []
        for c in range(2):
            bks = [pk.get() for _ in range(4)]
            for hf in range(2):
                w = weights.take("w1")
                for f in range(2):
                    for lq in range(8):
                        lp = hf * 8 + lq
                        a0, b0 = (2 * lp) // 16, (2 * lp) % 16
                        rhs = X[c].rearrange("p g (n s) -> p g n s", s=16)[:, :, a0:a0 + 31, b0]
                        wv = w.raw[:, lq, f * 128:(f + 1) * 128]
                        PE(lambda e, b=bks[f], wv=wv, lp=lp, rhs=rhs: e.matmul(
                            b.ap[:, 0:62], wv, rhs, start=(lp == 0), stop=(lp == 15)), w.ready, X_r[c], bks[f].free)
                        t = PE(lambda e, b=bks[2 + f], wv=wv, lp=lp, c=c: e.matmul(
                            b.ap[:, 0:1], wv, col("even_cmp_pe", c * 16 + lp), start=(lp == 0), stop=(lp == 15)),
                            cols_r, bks[2 + f].free)
                w.done(t)
            for f in range(2):
                s1 = ACTL(lambda e, b=bks[2 + f], n=c * 2 + f: e.activation(cb[:, n:n + 1], b.ap[:, 0:1], ACT.Copy), t)
                s2 = ACTL(lambda e, b=bks[f], n=c * 2 + f: e.activation(cH[:, n, :], b.ap[:, 0:62], ACT.Identity,
                                                                        bias=cb[:, n:n + 1]), s1)
                bks[f].done(s2)
                bks[2 + f].done(s1)
                hs.append(s2)
        s = POOL(lambda e: e.tensor_tensor(cG, cH, cH, ALU.mult), hs)
        s = POOL(lambda e: e.tensor_tensor(cG, cG, cH, ALU.mult), s)
        s = DVE(lambda e: e.scalar_tensor_tensor(out=cG, in0=cG, scalar=0.044715, in1=cH, op0=ALU.mult, op1=ALU.add), s)
        s = ACTL(lambda e: e.activation(cG, cG, ACT.Tanh, scale=math.sqrt(2.0 / math.pi)), s)
        s = DVE(lambda e: e.tensor_scalar(cG, cG, 0.5, 0.5, ALU.mult, ALU.add), s)
        cg_r = DVE(lambda e: e.tensor_tensor(cG, cG, cH, ALU.mult), s)
        b = pk.get()
        for g in range(2):
            for f in range(2):
                t = PE(lambda e, b=b, g=g, f=f: e.matmul(b.ap[g * 64:(g + 1) * 64, 0:31], w2s[:, f, :],
                                                         cG[:, f, g * 31:(g + 1) * 31], start=(f == 0), stop=(f == 1)),
                       cg_r, w2_d, b.free)
        kcc_r = DVE(lambda e, b=b: e.tensor_copy(kcc[:, 0:31], b.ap[:, 0:31]), t)
        b.done(kcc_r)
        b = pk.get()
        for g in range(2):
            for f in range(2):
                t = PE(lambda e, b=b, g=g, f=f: e.matmul(b.ap[0:31, g * 64:(g + 1) * 64], cG[:, 2 + f, g * 31:(g + 1) * 31],
                                                         w2s[:, 2 + f, :], start=(f == 0), stop=(f == 1)),
                       cg_r, w2_d, b.free)
        vcc_r = DVE(lambda e, b=b: e.tensor_copy(vcc[0:31], b.ap[0:31, 0:128].rearrange("p (a b) -> p a b", b=64)), t)
        b.done(vcc_r)

        sb_s = Banks([0, 1, 2])
        sb_p = Banks([3, 4, 5])
        sb_o = Banks([6, 7])

        def softmax_unit(qv, kv, n, masks, qready, vs, floor, gatev, obk, oreg, first, last, vready):
            st = {}
            nb = (n + 127) // 128

            def s0():
                b = st["b"] = sb_s.get()
                t = PE(lambda e: e.matmul(b.ap[:, 0:n], qv, kv, start=True, stop=not masks), qready, b.free)
                for m, (c0, c1, mv, mr) in enumerate(masks):
                    t = PE(lambda e, c0=c0, c1=c1, mv=mv, m=m: e.matmul(
                        b.ap[:, c0:c1], identb, mv, start=False, stop=(m == len(masks) - 1)), mr, identb_d)
                st["t"] = t

            def s1():
                b = st["b"]
                m = st["m"] = small.get()
                s = DVE(lambda e: e.tensor_reduce(m.ap[:, 0:1], b.ap[:, 0:n], AX.X, ALU.max, negate=True), st["t"], m.free)
                if floor:
                    s = DVE(lambda e: e.tensor_scalar(m.ap[:, 0:1], m.ap[:, 0:1], 1e28, None, ALU.min), s)
                p = st["p"] = w2k.get()
                st["e"] = ACTL(lambda e: e.activation(p.ap[:, 0:n], b.ap[:, 0:n], ACT.Exp, bias=m.ap[:, 0:1],
                                                      accum_out=m.ap[:, 1:2]), s, p.free)
                b.done(st["e"])

            def s2():
                m, p = st["m"], st["p"]
                s = st["e"]
                if floor:
                    s = DVE(lambda e: e.tensor_scalar(m.ap[:, 1:2], m.ap[:, 1:2], 1e-30, None, ALU.max), s)
                s = DVE(lambda e: e.reciprocal(m.ap[:, 2:3], m.ap[:, 1:2]), s)
                if gatev is None:
                    s = DVE(lambda e: e.tensor_scalar(p.ap[:, 0:n], p.ap[:, 0:n], m.ap[:, 2:3], None, ALU.mult), s)
                else:
                    s = DVE(lambda e: e.tensor_scalar(p.ap[:, 0:n], p.ap[:, 0:n], m.ap[:, 2:3], gatev, ALU.mult,
                                                      ALU.mult), s, gate_r)
                m.done(s)
                st["n"] = s

            def s3():
                p = st["p"]
                b = st["b2"] = sb_p.get()
                for k in range(nb):
                    w = min(128, n - k * 128)
                    t = PE(lambda e, k=k, w=w: e.transpose(b.ap[0:w, k * 128:(k + 1) * 128], p.ap[:, k * 128:k * 128 + w],
                                                           ident), st["n"], b.free)
                p.done(t)
                x = st["x"] = w2t.get()
                w = min(n, 128)
                s = ACTL(lambda e: e.activation(x.ap[0:w, 0:nb * 128], b.ap[0:w, 0:nb * 128], ACT.Copy), t, x.free)
                b.done(s)
                st["v"] = s

            def s4():
                x = st["x"]
                o = obk()
                for k in range(nb):
                    w = min(128, n - k * 128)
                    t = PE(lambda e, k=k, w=w: e.matmul(oreg(o), vs(k), x.ap[0:w, k * 128:(k + 1) * 128],
                                                        start=(first and k == 0), stop=(last and k == nb - 1)),
                           st["v"], vready, o.free)
                x.done(t)
                o.last = t
            return [s0, s1, s2, s3, s4]

        def pair_bank(flush):
            st = {}

            def get():
                if "b" not in st:
                    st["b"] = sb_o.get()
                return st["b"]
            return get, st

        units = []
        flushes = {}
        oT_r = [None] * 8
        for j in range(4):
            get, st = pair_bank(None)
            for i in range(NT):
                n = (i + 1) * 128
                for g in range(2):
                    p = slice(g * 64, g * 64 + 64)
                    qv = qbT[p, j, i * 128:(i + 1) * 128]
                    reg = lambda o, p=p, i=i: o.ap[p, i * 128:(i + 1) * 128]
                    gc = lambda x, i=i, g=g, j=j: gate[:, i, (g * 4 + j) * 3 + x:(g * 4 + j) * 3 + x + 1]
                    qr = sts[f"qb{j}"]["r"]
                    units.append(softmax_unit(qv, kcc[p, 0:31], 31, [(0, 31, cmpm[:, i * 32:i * 32 + 31], cmpm_d)],
                                              [qr, kcc_r], lambda k, g=g: vcc[0:31, g, :], True, gc(0), get, reg,
                                              True, False, vcc_r))
                    cm = [(i * 128, n, causal, causal_d)]
                    units.append(softmax_unit(qv, ksT[p, 0:n], n, cm, [qr, sts["ks"]["r"]],
                                              lambda k, g=g: vsb[:, k, g * 64:g * 64 + 64], False, gc(1), get, reg,
                                              False, False, vs_r))
                    units.append(softmax_unit(qv, kwT[p, 0:n], n, cm, [qr, sts["kw"]["r"]],
                                              lambda k, g=g: vw[:, k, g * 64:g * 64 + 64], False, gc(2), get, reg,
                                              False, True, vw_r))

            def flush(st=st, j=j):
                b = st["b"]
                oT_r[4 + j] = parts_of(uTh[:, 4 + j, 0:T], uTl[:, 4 + j, 0:T], b.ap, 1.0, b.last)
                b.done(oT_r[4 + j])
            old = units[-1][4]
            units[-1][4] = lambda old=old, flush=flush: (old(), flush())
        for n, u in enumerate(units):
            if n % 2 == 0:
                old = u[2]
                u[2] = lambda old=old: (old(), advance(taking, 2))
        run_pipe(units, 5)
        advance(taking, 1000)
        nsa_done = oT_r[7]

        units = []
        for j in range(4):
            get, st = pair_bank(None)
            for i in range(NT):
                n = (i + 1) * 128
                for c in range(2):
                    p = slice(c * 64, c * 64 + 64)
                    if i < 1:
                        masks = [(i * 128, n, causal, causal_d)]
                    else:
                        masks = [(0, n, sel[:, i - 1, 0:n], sc_r[i])]
                    units.append(softmax_unit(qaT[p, j, i * 128:(i + 1) * 128], kaT[p, 0:n], n, masks,
                                              [sts[f"qa{j}"]["r"], sts["ka"]["r"]], lambda k: va[:, k, :], False, None,
                                              get, lambda o, p=p, i=i: o.ap[p, i * 128:(i + 1) * 128], True, True, va_r))

            def flush(st=st, j=j):
                b = st["b"]
                oT_r[j] = parts_of(uTh[:, j, 0:T], uTl[:, j, 0:T], b.ap, 1.0, b.last)
                b.done(oT_r[j])
            old = units[-1][4]
            units[-1][4] = lambda old=old, flush=flush: (old(), flush())
        run_pipe(units, 5)

        hr, last = add_products(from_uT, 8, lambda k: oT_r[k])
        u = norm_T(hr, "mlp_norm_g", 0, [last])
        hr, last, _ = mlp(u, u)

        u0 = u = norm_T(hr, "mix_norm_g", 8, [last])
        at[0] = 0
        QT = region("QT", [128, 8, T])
        KTt = region("KTt", [128, 8, T])
        V = region("V", [128, 4, D])
        OQ = region("OQ", [128, 2, D])
        O = {}
        units = []
        sts = {}
        V_r = []
        for g in range(8):
            add(f"k{g}", "k", g % 2, KTt[:, g, :], dfree=u)
        run_pipe(units, 3)
        for c in range(2):
            bks = [pk.get() for _ in range(NT)]
            for k0 in (0, 4):
                w = weights.take("v")
                for i in range(NT):
                    t = tm(bks[i].ap, w, i * 128, 128, 0, 512, k0, k0 == 0, k0 == 4, u, bks[i].free)
                    if k0 == 4:
                        s = evac(i, V[:, i, c * 512:(c + 1) * 512], bks[i].ap, 1.0, t, u)
                        bks[i].done(s)
                        V_r.append(s)
                w.done(t)
        units = []
        for g in range(8):
            add(f"q{g}", "q", g % 2, QT[:, g, :], 0.125, dfree=u)
        run_pipe(units, 3)
        uT_read = sts["q7"]["t"]

        lm = region("lm", [128, 128])
        lamb = region("lamb", [128, 256])
        lamb_d = POOL.dma(lamb, bass.AP(ins["odd_lambda"].tensor, 0, [[0, 128], [1, 256]]), dsem(), u)
        lv = region("lv", [128, 4])
        lvv = lamb.rearrange("p (a b d) -> p a b d", a=2, b=2)
        s = DVE(lambda e: e.tensor_tensor(lm.rearrange("p (a d) -> p a d", d=64), lvv[:, :, 0, :], lvv[:, :, 1, :], ALU.mult), lamb_d)
        s = DVE(lambda e: e.tensor_reduce(lv[:, 0:2], lm.rearrange("p (a d) -> p a d", d=64), AX.X, ALU.add), s)
        s = ACTL(lambda e: e.activation(lv[:, 0:2], lv[:, 0:2], ACT.Exp), s)
        s = DVE(lambda e: e.tensor_scalar(lv[:, 2:3], lv[:, 1:2], LAMBDA_INIT, None, ALU.subtract), s)
        lam_r = DVE(lambda e: e.tensor_tensor(lv[:, 2:3], lv[:, 2:3], lv[:, 0:1], ALU.subtract), s)
        subg = region("subg", [128, 1])
        subg_r = DVE(lambda e: e.tensor_scalar(subg, col("odd_subln_g", 0), 1.0 - LAMBDA_INIT, None, ALU.mult), cols_r, u)

        dS = Banks([0, 1, 2, 3])
        dP = Banks([4, 5])
        dO = Banks([6, 7])
        Oq = Ring([OQ[:, i, :] for i in range(2)])
        oT_s = []
        first_q = {"r": [last]}

        def diff_unit(hh, i, oq, ost):
            st = {}
            n = (i + 1) * 128
            Q = QT[:, hh, :]

            def s0():
                st["b"] = []
                for c in range(2):
                    b = dS.get()
                    p = slice(c * 64, c * 64 + 64)
                    PE(lambda e, b=b, p=p: e.matmul(b.ap[:, 0:n], Q[p, i * 128:(i + 1) * 128], KTt[p, hh, 0:n],
                                                    start=True, stop=False), sts[f"q{hh}"]["r"], sts[f"k{hh}"]["r"], b.free)
                    b.t = PE(lambda e, b=b: e.matmul(b.ap[:, i * 128:n], identb, causal, start=False, stop=True))
                    st["b"].append(b)

            def s1():
                m = st["m"] = small.get()
                st["p"], st["e"] = [], []
                for c in range(2):
                    b = st["b"][c]
                    s = DVE(lambda e, b=b, c=c: e.tensor_reduce(m.ap[:, c:c + 1], b.ap[:, 0:n], AX.X, ALU.max, negate=True),
                            b.t, m.free)
                    p = w2k.get()
                    x = ACTL(lambda e, b=b, c=c, p=p: e.activation(p.ap[:, 0:n], b.ap[:, 0:n], ACT.Exp, bias=m.ap[:, c:c + 1],
                                                                   accum_out=m.ap[:, 2 + c:3 + c]), s, p.free)
                    b.done(x)
                    st["p"].append(p)
                    st["e"].append(x)

            def s2():
                m = st["m"]
                p0, p1 = st["p"]
                s = DVE(lambda e: e.reciprocal(m.ap[:, 4:6], m.ap[:, 2:4]), st["e"])
                s = DVE(lambda e: e.tensor_scalar(p1.ap[:, 0:n], p1.ap[:, 0:n], m.ap[:, 5:6], lv[:, 2:3], ALU.mult, ALU.mult),
                        s, lam_r)
                s = DVE(lambda e: e.scalar_tensor_tensor(out=p0.ap[:, 0:n], in0=p0.ap[:, 0:n], scalar=m.ap[:, 4:5],
                                                         in1=p1.ap[:, 0:n], op0=ALU.mult, op1=ALU.add), s)
                m.done(s)
                p1.done(s)
                st["n"] = s

            def s3():
                p0 = st["p"][0]
                b = dP.get()
                for k in range(i + 1):
                    t = PE(lambda e, k=k: e.transpose(b.ap[:, k * 128:(k + 1) * 128], p0.ap[:, k * 128:(k + 1) * 128], ident),
                           st["n"], b.free)
                p0.done(t)
                x = st["x"] = w2t.get()
                s = ACTL(lambda e: e.activation(x.ap[:, 0:n], b.ap[:, 0:n], ACT.Copy), t, x.free)
                b.done(s)
                st["v"] = s

            def s4():
                x = st["x"]
                if hh % 4 == 0:
                    ost["b"] = dO.get()
                o = ost["b"]
                for k in range(i + 1):
                    t = PE(lambda e, k=k: e.matmul(o.ap[:, (hh % 4) * 128:(hh % 4 + 1) * 128], x.ap[:, k * 128:(k + 1) * 128],
                                                   V[:, k, hh * 128:(hh + 1) * 128], start=(k == 0), stop=(k == i)),
                           st["v"], V_r, o.free)
                x.done(t)
                if hh == 0:
                    ost["q"] = Oq.get()
                if hh % 4 == 3:
                    q = ost["q"]
                    hf = hh // 4
                    s = DVE(lambda e: e.tensor_copy(q.ap[:, hf * 512:(hf + 1) * 512], o.ap), t, q.free)
                    o.done(s)
                    ost[hf] = s
                if hh == 7:
                    q = ost["q"]
                    qv = q.ap.rearrange("p (a b) -> p a b", b=128)
                    sq = tmp4.get()
                    s = POOL(lambda e: e.tensor_tensor(sq.ap, q.ap, q.ap, ALU.mult), ost[0], ost[1], sq.free)
                    ss = small.get()
                    ss.ready = DVE(lambda e: e.tensor_reduce(ss.ap[:, 0:8], sq.ap.rearrange("p (a b) -> p a b", b=128), AX.X,
                                                             ALU.add), s, ss.free)
                    sq.done(ss.ready)
                    r = rstd_of(ss, 8, 1.0 / 128)
                    s = DVE(lambda e: e.tensor_tensor(qv, qv, r.ap[:, 0:8].unsqueeze(2).to_broadcast([128, 8, 128]), ALU.mult),
                            r.ready)
                    r.done(s)
                    ost["n"] = s
            return [s0, s1, s2, s3, s4]

        def turn_back(i, ost):
            q = ost["q"]
            for hf in range(2):
                b = dP.get()
                for k in range(4):
                    t = PE(lambda e, k=k, b=b, hf=hf: e.transpose(b.ap[:, k * 128:(k + 1) * 128],
                                                                  q.ap[:, (hf * 4 + k) * 128:(hf * 4 + k + 1) * 128], ident),
                           ost["n"], b.free)
                v = (slice(None), slice(hf * 4, hf * 4 + 4), slice(i * 128, (i + 1) * 128))
                s = parts_of(uTh[v], uTl[v], b.ap.rearrange("p (a b) -> p a b", b=128), subg, t, uT_read, subg_r)
                b.done(s)
                oT_s.append(s)
            q.done(t)

        units = []
        for i in range(NT):
            ost = {}
            for hh in range(8):
                u_ = diff_unit(hh, i, None, ost)
                units.append(u_)
            if i:
                old = units[-5][0]
                units[-5][0] = lambda old=old, i=i, prev=prev: (old(), turn_back(i - 1, prev))
            prev = ost
        run_pipe(units, 5)
        turn_back(3, prev)
        hr, last = add_products(from_uT, 8, lambda k: oT_s)
        u = norm_T(hr, "mlp_norm_g", 8, [last])
        hr, last, _ = mlp(u, u)
        def final_norm(name, after):
            g = big[:, ARENA - D:ARENA]
            gd = POOL.dma(g, bass.AP(ins[name].tensor, 0, [[0, 128], [1, D]]), dsem(), after)
            res = []
            for i in range(NT):
                r = rstd_of(sum_squares(h[:, i, :], hr[i]), 1, 1.0 / D)
                res.append(DVE(lambda e, i=i, r=r: e.scalar_tensor_tensor(
                    out=h[:, i, :], in0=h[:, i, :], scalar=r.ap[:, 0:1], in1=g, op0=ALU.mult, op1=ALU.mult), r.ready, gd))
                r.done(res[-1])
            return res

        hr = final_norm("final_norm_g", u)

        u = norm_T(hr, "norm_mix_2", 0, [last], meta=True)
        u0 = u
        at[0] = 0
        nq = region("nq", [128, 4, T])
        onT = nq
        at_hg = at[0]
        nk = region("nk", [128, 4, T + META])
        nv = region("nv", [128, 4, T])
        nbr = region("nbr", [128, 2, 896])
        at[0] = max(at[0], at_hg + 7040)
        end_hg = at[0]
        hv = region("hv", [128, 4, T])
        hsg = region("hsg", [128, 4, T])
        hq = region("hq", [128, 4, T])
        ohT = hq
        nvm = region("nvm", [META, T])
        hvm = region("hvm", [META, T])
        ST = region("ST", [128, 8, 128])
        oh = region("oh", [128, 4, 128])

        fb = Banks([0, 1, 2, 3])
        nq_r, nk_r, nv_r = [], [], []
        for f in range(4):
            if f % 2 == 0:
                w = weights.take("nq")
            b = fb.get()
            t = fm(b, w, f % 2 * 128, u)
            s = evac(f, nq[:, f, :], b.ap[:, ::-1], 0.125, t, u)
            b.done(s)
            nq_r.append(s)
            if f % 2:
                w.done(t)
        for f in range(4):
            if f % 2 == 0:
                w = weights.take("nk")
            b = fb.get()
            t = fm(b, w, f % 2 * 128, u)
            s = evac(f, nk[:, f, 0:T], b.ap, 1.0, t, u)
            b.done(s)
            b = fb.get()
            t = fm(b, w, f % 2 * 128, u, T, META)
            s2 = evac(f, nk[:, f, T:T + META], b.ap[:, 0:META], 1.0, t, u)
            b.done(s2)
            nk_r.append([s, s2])
            if f % 2:
                w.done(t)

        def token_major(fin, finm):
            bks = [allb.get() for _ in range(NT + (finm is not None))]
            for k0 in (0, 4):
                w = weights.take("tok")
                for i, b in enumerate(bks):
                    part = 128 if i < NT else META
                    t = tm(b.ap[0:part, :], w, i * 128, part, 0, 512, k0, k0 == 0, k0 == 4, u, b.free)
                    if k0 == 4:
                        (fin if i < NT else finm)(i, b, t)
                w.done(t)

        def keep(dest, rr):
            def fin(i, b, t):
                d = dest[:, i, :] if i < NT else dest
                s = evac(i, d, b.ap[0:128 if i < NT else META, :], 1.0, t, u)
                b.done(s)
                rr.append(s)
            return fin

        token_major(keep(nv, nv_r), keep(nvm, nv_r))

        pad = nc.dram_tensor("pad", (8, 15, 128), F32, kind="Internal").ap()
        pz = dsem()
        s = POOL.dma(pad.rearrange("h a b -> (h a) b"), ins["c_zero"], pz)
        s = POOL.dma(pad[:, :, 48:79], ins["na_rpb_2"].rearrange("o h a b -> (o h) a b"), pz, s)
        nb_ring = Ring([nbr[:, i, :] for i in range(2)])
        nb_sem = [dsem(), dsem()]

        def bias(hh):
            b = nb_ring.get()
            for e2 in range(2):
                src = bass.AP(pad.tensor, hh * 15 * 128 + e2 * 128, [[1, 64], [128, 14], [1, 64]])
                d = POOL.dma(b.ap[e2 * 64:(e2 + 1) * 64, :].rearrange("p (a b) -> p a b", b=64), src, nb_sem[b.i], b.free, s, u)
            b.ready = POOL(lambda e: e.tensor_tensor(b.ap.rearrange("p (a b) -> p a b", b=64),
                                                     b.ap.rearrange("p (a b) -> p a b", b=64),
                                                     winm.unsqueeze(1).to_broadcast([128, 14, 64]), ALU.add), d, win_d)
            return b

        nS = [(0, 1), (2, 3)]
        nSat = [0]
        nP = Banks([4, 5])
        nO = Banks([6, 7])
        on_r = [None] * 4
        bias_of = {}

        def na_unit(hh, i, get, last):
            st = {}
            p = slice((hh % 2) * 64, (hh % 2) * 64 + 64)

            def s0():
                if i == 0:
                    bias_of[hh] = bias(hh)
                b0, b1 = fb.get(), fb.get()
                t0 = PE(lambda e: e.matmul(b0.ap, nq[p, hh // 2, T - (i + 1) * 128:T - i * 128], nk[p, hh // 2, 0:T],
                                           start=True, stop=True), nq_r[hh // 2], nk_r[hh // 2], b0.free)
                t1 = PE(lambda e: e.matmul(b1.ap[:, 0:META], nq[p, hh // 2, T - (i + 1) * 128:T - i * 128],
                                           nk[p, hh // 2, T:T + META], start=True, stop=True), b1.free)
                st["b"], st["t"] = (b0, b1), (t0, t1)

            def s1():
                b0, b1 = st["b"]
                q = st["q"] = w2k.get()
                bb = bias_of[hh]
                o = (6 - 2 * i) * 64
                x0 = DVE(lambda e: e.tensor_tensor(q.ap[:, 0:T], b0.ap, bb.ap[:, o:o + T], ALU.add), st["t"][0],
                         bb.ready, q.free)
                x1 = DVE(lambda e: e.tensor_copy(q.ap[:, T:T + META], b1.ap[:, 0:META]), st["t"][1])
                b0.done(x0)
                b1.done(x1)
                bb.done(x0)
                m = st["m"] = small.get()
                x = DVE(lambda e: e.tensor_reduce(m.ap[:, 0:1], q.ap, AX.X, ALU.max, negate=True), x0, x1, m.free)
                st["e"] = ACTL(lambda e: e.activation(q.ap, q.ap, ACT.Exp, bias=m.ap[:, 0:1], accum_out=m.ap[:, 1:2]), x)

            def s2():
                m, q = st["m"], st["q"]
                x = DVE(lambda e: e.reciprocal(m.ap[:, 2:3], m.ap[:, 1:2]), st["e"])
                st["n"] = DVE(lambda e: e.tensor_scalar(q.ap, q.ap, m.ap[:, 2:3], None, ALU.mult), x)
                m.done(st["n"])

            def s3():
                q = st["q"]
                b, b2 = nP.get(), nP.get()
                for k in range(4):
                    t = PE(lambda e, k=k: e.transpose(b.ap[:, k * 128:(k + 1) * 128], q.ap[:, k * 128:(k + 1) * 128], ident),
                           st["n"], b.free)
                t2 = PE(lambda e: e.transpose(b2.ap[0:META, 0:128], q.ap[:, T:T + META], ident), b2.free)
                q.done(t2)
                x, y = st["x"], st["y"] = w2t.get(), w2t.get()
                s = ACTL(lambda e: e.activation(x.ap[:, 0:T], b.ap, ACT.Copy), t, x.free)
                s2_ = DVE(lambda e: e.tensor_copy(y.ap[0:META, 0:128], b2.ap[0:META, 0:128]), t2, y.free)
                b.done(s)
                b2.done(s2_)
                st["v"] = (s, s2_)

            def s4():
                x, y = st["x"], st["y"]
                o = get()
                for k in range(4):
                    PE(lambda e, k=k: e.matmul(o.ap[p, T - (i + 1) * 128:T - i * 128], nv[:, k, hh * 64:hh * 64 + 64],
                                               x.ap[:, k * 128:(k + 1) * 128], start=(k == 0), stop=False),
                       st["v"], nv_r, o.free)
                t = PE(lambda e: e.matmul(o.ap[p, T - (i + 1) * 128:T - i * 128], nvm[:, hh * 64:hh * 64 + 64],
                                          y.ap[0:META, 0:128], start=False, stop=True))
                x.done(t)
                y.done(t)
                if last:
                    on_r[hh // 2] = ACTL(lambda e: e.activation(onT[:, hh // 2, :], o.ap[:, ::-1], ACT.Copy), t, u)
                    o.done(on_r[hh // 2])
            return [s0, s1, s2, s3, s4]

        na_units = []
        for j in range(4):
            st_ = {}

            def get(st_=st_):
                if "b" not in st_:
                    st_["b"] = nO.get()
                return st_["b"]
            for c in range(2):
                for i in range(NT):
                    na_units.append(na_unit(2 * j + c, i, get, c == 1 and i == 3))
        run_pipe(na_units, 5)

        lb = sb("lb", [128, 2, 2, 4])
        lg = cols[:, ROW_AT["hg_lb_logits_2"]:ROW_AT["hg_lb_logits_2"] + 16].rearrange("p (a l k) -> p a l k", a=2, l=2)
        s1 = DVE(lambda e: e.tensor_tensor(lb[:, :, 0, :], lg[:, :, 1, :], lg[:, :, 0, :], ALU.subtract), cols_r)
        s2 = DVE(lambda e: e.tensor_tensor(lb[:, :, 1, :], lg[:, :, 0, :], lg[:, :, 1, :], ALU.subtract), cols_r)
        s3 = ACTL(lambda e: e.activation(lb, lb, ACT.Exp), s1, s2)
        s4 = DVE(lambda e: e.tensor_scalar(lb, lb, 1.0, None, ALU.add), s3)
        lb_r = DVE(lambda e: e.reciprocal(lb, lb), s4)

        hv_r = []
        token_major(keep(hv, hv_r), keep(hvm, hv_r))
        hg_r = []
        hgain = tmp4.get()
        hgain_d = POOL.dma(hgain.ap[:, 0:T], bass.AP(ins["hg_norm_2"].tensor, 0, [[0, 128], [1, T]]), tmp_sem[hgain.i],
                           hgain.free)

        def silu_gain(i, b, t):
            x = w2k.get()
            a = ACTL(lambda e: e.activation(x.ap[:, 0:T], b.ap, ACT.Exp, scale=-1.0), t, x.free)
            a = DVE(lambda e: e.tensor_scalar(x.ap[:, 0:T], x.ap[:, 0:T], 1.0, None, ALU.add), a)
            a = DVE(lambda e: e.reciprocal(x.ap[:, 0:T], x.ap[:, 0:T]), a)
            a = DVE(lambda e: e.tensor_tensor(x.ap[:, 0:T], x.ap[:, 0:T], b.ap, ALU.mult), a)
            b.done(a)
            a = POOL(lambda e: e.tensor_tensor(hsg[:, i, :], x.ap[:, 0:T], hgain.ap[:, 0:T], ALU.mult), a, hgain_d, u)
            x.done(a)
            hg_r.append(a)

        token_major(silu_gain, None)
        hgain.done(hg_r)
        hq_r = []
        for f in range(4):
            if f % 2 == 0:
                w = weights.take("hq")
            b = fb.get()
            t = fm(b, w, f % 2 * 128, u)
            x = w2k.get()
            a = ACTL(lambda e, b=b, x=x: e.activation(x.ap[:, 0:T], b.ap, ACT.Exp, scale=-1.0), t, x.free)
            a = DVE(lambda e, x=x: e.tensor_scalar(x.ap[:, 0:T], x.ap[:, 0:T], 1.0, None, ALU.add), a)
            a = DVE(lambda e, x=x: e.reciprocal(x.ap[:, 0:T], x.ap[:, 0:T]), a)
            a = DVE(lambda e, b=b, x=x, f=f: e.tensor_tensor(hq[:, f, :], x.ap[:, 0:T], b.ap, ALU.mult), a, u)
            b.done(a)
            x.done(a)
            hq_r.append(a)
            if f % 2:
                w.done(t)

        at[0] = at_hg
        FK = [[region(f"fk{d}{c}", [128, T + META]) for c in range(2)] for d in range(2)]
        SX = [region(f"sx{d}", [128, T + META]) for d in range(2)]
        Qt = [region(f"qt{d}", [128, T]) for d in range(2)]
        Kt = [region(f"kt{d}", [128, T + META]) for d in range(2)]
        AT = region("AT", [128, T])
        Kh = [Ring([region(f"kh{d}", [128, T + 128])]) for d in range(2)]
        assert at[0] <= end_hg
        free = {"fk": [on_r, on_r], "sx": [on_r, on_r], "qt": [on_r, on_r], "kt": [on_r, on_r], "AT": on_r, "ST": u,
                "oh": None}
        pz_b = Banks([0, 1])
        pA = Banks([2, 3, 4])
        pT = Banks([5])
        pKV = Banks([6])
        pOo = Banks([7])
        oh_r = [None] * 4
        LEV = (1, 2, 4, 8, 16, 32, 64)
        for hd in range(4):
            k_r, f_r = [None, None], [None, None]
            w = weights.take("z")
            for d in range(2):
                f_, k_ = FK[d]
                parts = [(0, T)] + ([(T, META)] if d == 0 else [])
                ff, kk = [], []
                for c0, n in parts:
                    b = pz_b.get()
                    t = fm(b, w, d * 128, u, c0, n)
                    a1 = ACTL(lambda e, b=b, n=n, c0=c0, f_=f_: e.activation(f_[:, c0:c0 + n], b.ap[:, 0:n], ACT.Exp, scale=-1.0),
                              t, free["fk"][d])
                    a2 = ACTL(lambda e, b=b, n=n, c0=c0, k_=k_: e.activation(k_[:, c0:c0 + n], b.ap[:, 0:n], ACT.Exp),
                              t, free["fk"][d])
                    b.done(a2)
                    s = DVE(lambda e, n=n, c0=c0, f_=f_: e.tensor_scalar(f_[:, c0:c0 + n], f_[:, c0:c0 + n], 1.0, None, ALU.add), a1)
                    s = DVE(lambda e, n=n, c0=c0, f_=f_: e.reciprocal(f_[:, c0:c0 + n], f_[:, c0:c0 + n]), s)
                    ff.append(DVE(lambda e, n=n, c0=c0, f_=f_, d=d, hd=hd: e.tensor_scalar(
                        f_[:, c0:c0 + n], f_[:, c0:c0 + n], lb[:, d, 1, hd:hd + 1], lb[:, d, 0, hd:hd + 1], ALU.mult, ALU.add),
                        s, lb_r))
                    s = DVE(lambda e, n=n, c0=c0, k_=k_: e.tensor_scalar(k_[:, c0:c0 + n], k_[:, c0:c0 + n], 1.0, None, ALU.add), a2)
                    s = DVE(lambda e, n=n, c0=c0, k_=k_: e.reciprocal(k_[:, c0:c0 + n], k_[:, c0:c0 + n]), s)
                    kk.append(DVE(lambda e, n=n, c0=c0, k_=k_, d=d, hd=hd: e.tensor_scalar(
                        k_[:, c0:c0 + n], k_[:, c0:c0 + n], lb[:, d, 1, hd:hd + 1], None, ALU.mult), s, lb_r))
                w.done(t)
                f_r[d], k_r[d] = ff, kk
            s = POOL(lambda e: e.tensor_tensor(Kt[0][:, 0:T], FK[0][1][:, 0:T], FK[1][1][:, 0:T], ALU.add), k_r,
                     free["kt"][0])
            b = pA.get()
            for c in range(4):
                t = PE(lambda e, c=c, b=b, hd=hd: e.matmul(b.ap[:, c * 128:(c + 1) * 128], Kt[0][:, c * 128:(c + 1) * 128],
                                                           hq[:, hd, c * 128:(c + 1) * 128], start=True, stop=True),
                       s, hq_r[hd], b.free)
            at_r = DVE(lambda e, b=b: e.tensor_tensor(AT.rearrange("p (c t) -> p c t", t=128), b.ap.rearrange(
                "p (c t) -> p c t", t=128), ident.unsqueeze(1).to_broadcast([128, 4, 128]), ALU.mult), t, free["AT"])
            b.done(at_r)
            free["kt"][0] = t
            sx_r = [POOL(lambda e, d=d: e.memset(SX[d], 1.0), free["sx"][d]) for d in range(2)]
            q_r = [POOL(lambda e, d=d, hd=hd: e.tensor_copy(Qt[d], hq[:, hd, :]), hq_r[hd], free["qt"][d]) for d in range(2)]
            kt_r = [POOL(lambda e, d=d: e.tensor_copy(Kt[d][:, 0:T], FK[d][1][:, 0:T]), k_r[d], free["kt"][d]) for d in range(2)]
            p_r = [f_r[0], f_r[1]]
            for li, m in enumerate(LEV):
                for d in range(2):
                    L = T + META if (d == 0 and m <= 8) else T

                    def hv2(x, L=L, m=m):
                        return x[:, 0:L].rearrange("p (n two m) -> p n two m", two=2, m=m)
                    P_, S_, k_ = FK[d][0], SX[d], FK[d][1]
                    qs, ks = (1, 0) if d == 0 else (0, 1)
                    qsrc = hq[:, hd, :].rearrange("p (n two m) -> p n two m", two=2, m=m)
                    q_s = POOL(lambda e, m=m, P_=P_, d=d, qs=qs, qsrc=qsrc: e.tensor_tensor(
                        Qt[d].rearrange("p (n two m) -> p n two m", two=2, m=m)[:, :, qs, :], qsrc[:, :, qs, :],
                        P_[:, 0:T].rearrange("p (n two m) -> p n two m", two=2, m=m)[:, :, qs, :], ALU.mult),
                        p_r[d], q_r[d], free["qt"][d])
                    k_s = POOL(lambda e, m=m, S_=S_, k_=k_, d=d, ks=ks: e.tensor_tensor(
                        Kt[d][:, 0:T].rearrange("p (n two m) -> p n two m", two=2, m=m)[:, :, ks, :],
                        k_[:, 0:T].rearrange("p (n two m) -> p n two m", two=2, m=m)[:, :, ks, :],
                        S_[:, 0:T].rearrange("p (n two m) -> p n two m", two=2, m=m)[:, :, ks, :], ALU.mult),
                        sx_r[d], kt_r[d], k_r[d], free["kt"][d])
                    b = pA.get()
                    for c in range(4):
                        t = PE(lambda e, c=c, b=b, d=d: e.matmul(b.ap[:, c * 128:(c + 1) * 128], Kt[d][:, c * 128:(c + 1) * 128],
                                                                 Qt[d][:, c * 128:(c + 1) * 128], start=True, stop=True),
                               q_s, k_s, b.free)
                    free["qt"][d] = free["kt"][d] = t
                    mk = lev[:, (d * 7 + li) * 128:(d * 7 + li + 1) * 128].unsqueeze(1).to_broadcast([128, 4, 128])
                    at_r = DVE(lambda e, b=b, mk=mk: e.copy_predicated(
                        AT.rearrange("p (c t) -> p c t", t=128), mk, b.ap.rearrange("p (c t) -> p c t", t=128)),
                        t, at_r, lev_d)
                    b.done(at_r)
                    nb = L // (2 * m)
                    e0 = m - 1 if d == 0 else 0
                    s = DVE(lambda e, P_=P_, S_=S_, ks=ks, qs=qs, hv2=hv2, nb=nb, m=m, e0=e0: e.tensor_tensor(
                        hv2(S_)[:, :, ks, :], hv2(S_)[:, :, ks, :],
                        hv2(P_)[:, :, qs, e0:e0 + 1].to_broadcast([128, nb, m]), ALU.mult), p_r[d], sx_r[d], k_s)
                    sx_r[d] = s
                    p_r[d] = DVE(lambda e, P_=P_, ks=ks, qs=qs, hv2=hv2, nb=nb, m=m, e0=e0: e.tensor_tensor(
                        hv2(P_)[:, :, qs, :], hv2(P_)[:, :, qs, :],
                        hv2(P_)[:, :, ks, e0:e0 + 1].to_broadcast([128, nb, m]), ALU.mult), s, q_s)
                    q_r[d] = q_s
                    kt_r[d] = k_s
            kh_r = [None, None]
            for d in range(2):
                n = T + META if d == 0 else T
                kb = Kh[d].get()
                s = POOL(lambda e, d=d, n=n: e.tensor_tensor(Kt[d][:, 0:n], FK[d][1][:, 0:n], SX[d][:, 0:n], ALU.mult),
                         sx_r[d], k_r[d], free["kt"][d])
                q_s = POOL(lambda e, d=d, hd=hd: e.tensor_tensor(Qt[d], hq[:, hd, :], FK[d][0][:, 0:T], ALU.mult),
                           p_r[d], free["qt"][d])
                b = pT.get()
                for c in range(4):
                    t = PE(lambda e, c=c, b=b, d=d: e.transpose(b.ap[:, c * 128:(c + 1) * 128], Kt[d][:, c * 128:(c + 1) * 128],
                                                                ident), s, b.free)
                x = ACTL(lambda e, b=b, kb=kb: e.activation(kb.ap[:, 0:T], b.ap, ACT.Copy), t, kb.free)
                b.done(x)
                kh_r[d] = [x]
                if d == 0:
                    b = pT.get()
                    t = PE(lambda e, b=b, d=d: e.transpose(b.ap[0:META, 0:128], Kt[d][:, T:T + META], ident), b.free)
                    x = ACTL(lambda e, b=b, kb=kb: e.activation(kb.ap[0:META, T:T + 128], b.ap[0:META, 0:128], ACT.Copy), t)
                    b.done(x)
                    kh_r[d].append(x)
                free["kt"][d] = t
                Kh[d].cur = kb
                free["sx"][d] = s
                q_r[d] = q_s
            st_r = [None] * 8
            b = pKV.get()
            kf, kbk = Kh[0].cur.ap, Kh[1].cur.ap
            t = PE(lambda e, b=b, hd=hd, kf=kf: e.matmul(b.ap[:, 0:128], kf[0:META, T:T + 128], hvm[:, hd * 128:(hd + 1) * 128],
                                                         start=True, stop=True), kh_r[0], hv_r, b.free)
            st_r[0] = DVE(lambda e, b=b: e.tensor_copy(ST[:, 0, :], b.ap[:, 0:128]), t, free["ST"])
            b.done(st_r[0])
            for c in range(3):
                b = pKV.get()
                t = PE(lambda e, b=b, hd=hd, c=c, kf=kf: e.matmul(b.ap[:, 0:128], kf[:, c * 128:(c + 1) * 128],
                                                                  hv[:, c, hd * 128:(hd + 1) * 128], start=True, stop=True),
                       kh_r[0], hv_r, b.free)
                st_r[c + 1] = DVE(lambda e, b=b, c=c: e.scalar_tensor_tensor(
                    out=ST[:, c + 1, :], in0=ST[:, c, :], scalar=FK[0][0][:, c * 128 + 127:c * 128 + 128], in1=b.ap[:, 0:128],
                    op0=ALU.mult, op1=ALU.add), t, st_r[c], p_r[0], free["ST"])
                b.done(st_r[c + 1])
            Kh[0].cur.done(t)
            for c in (3, 2, 1):
                b = pKV.get()
                t = PE(lambda e, b=b, hd=hd, c=c, kbk=kbk: e.matmul(b.ap[:, 0:128], kbk[:, c * 128:(c + 1) * 128],
                                                                    hv[:, c, hd * 128:(hd + 1) * 128], start=True, stop=True),
                       kh_r[1], hv_r, b.free)
                if c == 3:
                    st_r[6] = DVE(lambda e, b=b: e.tensor_copy(ST[:, 6, :], b.ap[:, 0:128]), t, free["ST"])
                else:
                    st_r[c + 3] = DVE(lambda e, b=b, c=c: e.scalar_tensor_tensor(
                        out=ST[:, c + 3, :], in0=ST[:, c + 4, :], scalar=FK[1][0][:, c * 128:c * 128 + 1], in1=b.ap[:, 0:128],
                        op0=ALU.mult, op1=ALU.add), t, st_r[c + 4], p_r[1], free["ST"])
                b.done(st_r[c + 3])
            Kh[1].cur.done(t)
            free["fk"] = [[st_r[1:4], q_r[0], kt_r[0], free["sx"][0]], [st_r[4:7], q_r[1], kt_r[1], free["sx"][1]]]
            b = pOo.get()
            for c in range(4):
                o = b.ap[:, c * 128:(c + 1) * 128]
                cs = slice(c * 128, (c + 1) * 128)
                PE(lambda e, o=o, cs=cs, c=c, hd=hd: e.matmul(o, AT[:, cs], hv[:, c, hd * 128:(hd + 1) * 128], start=True,
                                                              stop=False), at_r, b.free)
                t = PE(lambda e, o=o, cs=cs, c=c: e.matmul(o, Qt[0][:, cs], ST[:, c, :], start=False, stop=(c == 3)),
                       q_r[0], st_r[c])
                if c < 3:
                    t = PE(lambda e, o=o, cs=cs, c=c: e.matmul(o, Qt[1][:, cs], ST[:, 4 + c, :], start=False, stop=True),
                           q_r[1], st_r[4 + c])
            free["AT"] = free["ST"] = t
            free["qt"] = [t, t]
            x = ACTL(lambda e, b=b: e.activation(oh, b.ap.rearrange("p (c t) -> p c t", t=128), ACT.Copy), t, free["oh"])
            b.done(x)
            sq = w2k.get()
            s = POOL(lambda e, sq=sq: e.tensor_tensor(sq.ap[:, 0:T].rearrange("p (c t) -> p c t", t=128), oh, oh, ALU.mult),
                     x, sq.free)
            ss = small.get()
            ss.ready = DVE(lambda e, ss=ss, sq=sq: e.tensor_reduce(
                ss.ap[:, 0:4], sq.ap[:, 0:T].rearrange("p (c t) -> p c t", t=128), AX.X, ALU.add), s, ss.free)
            sq.done(ss.ready)
            r = rstd_of(ss, 4, 1.0 / 128)
            s = DVE(lambda e, r=r: e.tensor_tensor(oh, oh, r.ap[:, 0:4].unsqueeze(2).to_broadcast([128, 4, 128]), ALU.mult),
                    r.ready)
            r.done(s)
            s = DVE(lambda e, hd=hd: e.tensor_tensor(oh, oh, hsg[:, :, hd * 128:(hd + 1) * 128], ALU.mult), s, hg_r)
            b = pT.get()
            for c in range(4):
                t = PE(lambda e, c=c, b=b: e.transpose(b.ap[:, c * 128:(c + 1) * 128], oh[:, c, :], ident), s, b.free)
            free["oh"] = t
            oh_r[hd] = ACTL(lambda e, b=b, hd=hd: e.activation(ohT[:, hd, :], b.ap, ACT.Copy), t)
            b.done(oh_r[hd])

        mixT = big[:, 2048:6144].rearrange("p (k n) -> p k n", n=T)
        mix_free = [on_r, oh_r, nk_r]
        parts = {}
        mix_r = []
        for br, (oT_, orr) in enumerate(((onT, on_r), (ohT, oh_r))):
            for g in range(2):
                w = weights.take("y")
                bys = []
                for f in range(4):
                    by = allb.get()
                    for k in range(4):
                        ty = PE(lambda e, k=k, by=by, w=w, f=f, oT_=oT_: e.matmul(
                            by.ap, w.raw[:, k, f * 128:(f + 1) * 128], oT_[:, k, :], start=(k == 0), stop=(k == 3)),
                            w.ready, orr, by.free)
                    bys.append((by, ty))
                w.done(ty)
                for f in range(4):
                    ft = g * 4 + f
                    if f % 2 == 0:
                        w = weights.take("gate")
                    bg = allb.get()
                    t = fm(bg, w, f % 2 * 128, u)
                    if f % 2:
                        w.done(t)
                    by, ty = bys[f]
                    x = w2k.get()
                    a = ACTL(lambda e, bg=bg, x=x: e.activation(x.ap[:, 0:T], bg.ap, ACT.Exp, scale=-1.0), t, x.free)
                    bg.done(a)
                    a = DVE(lambda e, x=x: e.tensor_scalar(x.ap[:, 0:T], x.ap[:, 0:T], 1.0, None, ALU.add), a)
                    a = DVE(lambda e, x=x: e.reciprocal(x.ap[:, 0:T], x.ap[:, 0:T]), a)
                    if br == 0:
                        a = DVE(lambda e, x=x, by=by, ft=ft: e.tensor_tensor(mixT[:, ft, :], x.ap[:, 0:T], by.ap, ALU.mult),
                                a, ty, mix_free)
                        by.done(a)
                        x.done(a)
                        parts[ft] = a
                    else:
                        a = DVE(lambda e, x=x, by=by: e.tensor_tensor(x.ap[:, 0:T], x.ap[:, 0:T], by.ap, ALU.mult), a, ty)
                        by.done(a)
                        a = POOL(lambda e, x=x, ft=ft: e.tensor_tensor(mixT[:, ft, :], mixT[:, ft, :], x.ap[:, 0:T], ALU.add),
                                 a, parts[ft])
                        x.done(a)
                        parts[ft] = a
        for k in range(KT):
            mix_r.append(parts_of(uTh[:, k, 0:T], uTl[:, k, 0:T], mixT[:, k, :], 1.0, parts[k], t))
        hr, last = add_products(from_uT, 8, lambda k: mix_r[k])
        u = norm_T(hr, "norm_mlp_2", 0, [last])
        hr, last, _ = mlp(u, u)
        out_v = out.rearrange("a (i p) d -> (a p) i d", p=128)
        hr = final_norm("norm_final_2", u)
        stores = [SP.dma(out_v[:, i, :], h[:, i, :], dsem(), hr[i]) for i in range(NT)]
        number(lanes)

        block = ctx.enter_context(nc.Block())

        @block.sync
        def _(e):
            play(SP, e)
            for s in stores:
                e.wait_ge(s.sem.sem, s.count)

        @block.gpsimd
        def _(e):
            play(POOL, e)

        @block.scalar
        def _(e):
            play(ACTL, e)

        @block.tensor
        def _(e):
            play(PE, e)

        @block.vector
        def _(e):
            play(DVE, e)


_INS = ["x", "mix_norm_g", "mlp_norm_g", "even_w_in", "even_cmp_pe", "even_cmp_w1", "even_cmp_w2", "even_w_out",
        "odd_w_in", "odd_lambda", "odd_subln_g", "odd_w_out", "mlp_w_up", "mlp_w_down", "final_norm_g",
        "meta_tokens_2", "w_in_2", "w_na_out_2", "w_hg_out_2", "w_o_2", "w_up_2", "w_down_2", "norm_mix_2",
        "norm_mlp_2", "norm_final_2", "hg_norm_2", "na_rpb_2", "hg_lb_logits_2"]


def kernel(**inputs):
    import concourse.bacc as bacc
    from concourse.bass_utils import run_bass_kernel_spmd

    nc = bacc.Bacc("TRN2", target_bir_lowering=False, num_devices=1)
    arrays = {n: np.ascontiguousarray(inputs[n]) for n in _INS}
    arrays.update(shape_constants())
    ins = {}
    for n, a in arrays.items():
        ins[n] = nc.dram_tensor(n, a.shape, mybir.dt.from_np(a.dtype), kind="ExternalInput").ap()
    for n in ("even_w_in", "even_w_out"):
        ins[n] = ins[n][0]
    for n in ("odd_w_in", "odd_w_out", "w_in_2", "w_na_out_2", "w_hg_out_2", "w_o_2", "w_up_2", "w_down_2"):
        ins[n + "_0"] = ins[n][0]
    for k in range(2):
        ins[f"mlp_up_{k}"] = ins["mlp_w_up"][k]
        ins[f"mlp_down_{k}"] = ins["mlp_w_down"][k]
    out = nc.dram_tensor("out", (1, T, D), F32, kind="ExternalOutput").ap()
    build(nc, ins, out)
    r = run_bass_kernel_spmd(nc, [arrays], core_ids=[0])
    return r.results[0]["out"]
```

```python
import math
from contextlib import ExitStack

import numpy as np

import concourse.bass as bass
from concourse import mybir

F32 = mybir.dt.float32
BF16 = mybir.dt.bfloat16
U8 = mybir.dt.uint8
R32 = mybir.dt.float32r
ALU = mybir.AluOpType
ACT = mybir.ActivationFunctionType
AX = mybir.AxisListType

T = 512
D = 1024
NT = 4
KT = 8
META = 16
EPS = 1e-6
TAKE = 128
NEG = -1e30
TAKEN = -3e38
ROPE_LAGS = (0, 1, 3)
ATT_LAGS = (0, 1, 3, 4, 6)
NA_LAGS = (0, 1, 3, 4, 5)
LAMBDA_INIT = 0.8 - 0.6 * math.exp(-0.3)

ROW_NAMES = [("mix_norm_g", 16), ("mlp_norm_g", 16), ("norm_mix_2", 8), ("norm_mlp_2", 8),
             ("hg_lb_logits_2", 16), ("even_cmp_pe", 32), ("odd_subln_g", 1)]
ROW_AT = {}
for _n, _k in ROW_NAMES:
    ROW_AT[_n] = sum(k for _, k in ROW_NAMES[:len(ROW_AT)])
NROWS = sum(k for _, k in ROW_NAMES)


def shape_constants():
    c = {}
    inv = (1.0 / (np.float32(10000.0) ** (np.arange(0, 64, 2, dtype=np.float32) / np.float32(64)))).astype(np.float32)
    ang = np.arange(T, dtype=np.float32)[None, :] * inv[:, None]
    c["c_cos"] = np.tile(np.cos(ang), (4, 1)).astype(np.float32)
    c["c_sin"] = np.tile(np.sin(ang), (4, 1)).astype(np.float32)
    rot = np.zeros((128, 128), np.float32)
    for b in (0, 64):
        for d in range(32):
            rot[b + 32 + d, b + d] = -1.0
            rot[b + d, b + 32 + d] = 1.0
    c["c_rot"] = rot
    c["c_ident"] = np.eye(128, dtype=np.float32)
    q = np.arange(128)
    c["c_causal"] = np.where(q[None, :] <= q[:, None], 0.0, NEG).astype(np.float32)
    n = np.arange(32)
    end = n * 16 + 31
    t = np.arange(T).reshape(NT, 128).transpose(1, 0)
    c["c_cmp"] = np.where(end[None, None, :] <= t[:, :, None], 0.0, NEG).astype(np.float32).reshape(128, 128)
    masks = []
    for m in (1, 2, 4, 8, 16, 32, 64):
        same = (q[:, None] // (2 * m)) == (q[None, :] // (2 * m))
        left = (q // m) % 2 == 0
        masks.append(same & left[:, None] & ~left[None, :])
    for m in range(7):
        masks.append(masks[m].T)
    c["c_lev"] = np.concatenate([m.astype(np.float32) for m in masks], axis=1)
    col = np.arange(64)
    start = np.clip(col - 8, 0, 48)
    inw = (col[None, :] >= start[:, None]) & (col[None, :] < start[:, None] + 16)
    c["c_win"] = np.tile(np.where(inw, 0.0, NEG).astype(np.float32)[::-1], (2, 1))
    c["c_zero"] = np.zeros((120, 128), np.float32)
    return c


class Step:
    __slots__ = ("go", "after", "lane", "sem", "count", "named")

    def __init__(self, go, after, lane, sem=None):
        self.go, self.after, self.lane, self.sem, self.count, self.named = go, after, lane, sem, 0, sem is not None


def flat(xs):
    for x in xs:
        if x is None:
            continue
        if isinstance(x, (list, tuple)):
            yield from flat(x)
        else:
            yield x


class Lane:

    def __init__(self, name, sem):
        self.name, self.sem, self.queue = name, sem, []

    def __call__(self, go, *after):
        s = Step(go, list(flat(after)), self)
        for a in s.after:
            a.named = True
        self.queue.append(s)
        return s

    def dma(self, out, in_, sem, *after):
        s = Step(lambda e: e.dma_start(out, in_), list(flat(after)), self, sem)
        for a in s.after:
            a.named = True
        self.queue.append(s)
        sem.total += 16
        s.count = sem.total
        return s


class DmaSem:
    def __init__(self, sem):
        self.sem, self.total = sem, 0


def number(lanes):
    for lane in lanes:
        n = 0
        for s in lane.queue:
            if s.sem is None and s.named:
                n += 1
                s.count = n


def play(lane, eng):
    seen = {}
    for s in lane.queue:
        for a in s.after:
            sem = a.lane.sem if a.sem is None else a.sem.sem
            if seen.get(id(sem), 0) < a.count:
                eng.wait_ge(sem, a.count)
                seen[id(sem)] = a.count
        i = s.go(eng)
        if s.sem is not None:
            i.then_inc(s.sem.sem, 16)
        elif s.named:
            i.then_inc(lane.sem, 1)


class Ring:

    def __init__(self, bufs):
        self.bufs, self.free, self.at, self.held = bufs, [[] for _ in bufs], 0, set()

    def get(self):
        i = self.at % len(self.bufs)
        self.at += 1
        assert i not in self.held, "a buffer is asked for before its last reader is known"
        self.held.add(i)
        free, self.free[i] = self.free[i], []
        return Buf(self, i, self.bufs[i], free)

    def more(self, bufs, after):
        self.bufs = self.bufs + bufs
        self.free = self.free + [list(flat([after])) for _ in bufs]

    def less(self, n):
        assert not self.held
        used = self.free[-n:]
        self.bufs, self.free, self.at = self.bufs[:-n], self.free[:-n], 0
        return used


class Buf:
    def __init__(self, ring, i, ap, free):
        self.ring, self.i, self.ap, self.free = ring, i, ap, free

    def done(self, *steps):
        self.ring.held.discard(self.i)
        self.ring.free[self.i] += list(flat(steps))


def build(nc, ins, out):
    ctx = ExitStack()
    with ctx:
        def sb(name, shape, dt=F32):
            return ctx.enter_context(nc.sbuf_tensor(name, shape, dt))[tuple(slice(None) for _ in shape)]

        def sem(name):
            return ctx.enter_context(nc.semaphore(name))

        PE, DVE, ACTL, POOL, SP = [Lane(n, sem("s_" + n)) for n in ("pe", "dve", "act", "pool", "sp")]
        lanes = [PE, DVE, ACTL, POOL, SP]
        names = [0]

        def dsem():
            names[0] += 1
            return DmaSem(sem(f"d{names[0]}"))

        bank = [ctx.enter_context(nc.psum_tensor(f"bank{i}", [128, 512], F32))[:, :] for i in range(8)]
        bank_free = [[] for _ in range(8)]

        class Banks(Ring):
            def __init__(self, ids):
                self.bufs, self.at, self.ids = [bank[i] for i in ids], 0, ids

            def get(self):
                i = self.ids[self.at % len(self.ids)]
                self.at += 1
                free, bank_free[i] = bank_free[i], []
                return BankBuf(i, free)

        class BankBuf:
            def __init__(self, i, free):
                self.i, self.ap, self.free = i, bank[i], free

            def done(self, *steps):
                bank_free[self.i] += list(flat(steps))

        def const(name, shape, dt=F32, src=None, eng=None):
            t = sb("k_" + name, shape, dt)
            s = (eng or SP).dma(t, ins[name] if src is None else src, dsem())
            return t, s

        h = sb("h", [128, NT, D])
        h_ready = []
        x_v = ins["x"].rearrange("a (i p) d -> (a p) i d", p=128)
        for i in range(NT):
            h_ready.append(SP.dma(h[:, i, :], x_v[:, i, :], dsem()))
        rows = sb("rows", [NROWS, 128])
        rows_s = dsem()
        rows_d = None
        views = {
            "mix_norm_g": ins["mix_norm_g"].rearrange("l (k p) -> (l k) p", p=128),
            "mlp_norm_g": ins["mlp_norm_g"].rearrange("l (k p) -> (l k) p", p=128),
            "norm_mix_2": ins["norm_mix_2"].rearrange("l (k p) -> (l k) p", p=128),
            "norm_mlp_2": ins["norm_mlp_2"].rearrange("l (k p) -> (l k) p", p=128),
            "hg_lb_logits_2": ins["hg_lb_logits_2"].rearrange("a l (k p) -> (a l k) p", p=128),
            "even_cmp_pe": ins["even_cmp_pe"].rearrange("o c (l2 l) d -> (o c l2) (l d)", l=2),
            "odd_subln_g": ins["odd_subln_g"],
        }
        ident, ident_d = const("c_ident", [128, 128])
        for n, k in ROW_NAMES:
            rows_d = SP.dma(rows[ROW_AT[n]:ROW_AT[n] + k, :], views[n], rows_s)
        identb = sb("identb", [128, 128], BF16)
        causal = sb("causal", [128, 128], BF16)
        cmpm = sb("cmpm", [128, 128], BF16)
        cosT, cos_d = const("c_cos", [128, T])
        sinT, sin_d = const("c_sin", [128, T])
        rotm, rot_d = const("c_rot", [128, 128])
        winm, win_d = const("c_win", [128, 64], eng=POOL)
        half = sb("half", [128, 16])
        half_m = DVE(lambda e: e.memset(half, -0.5))

        uTh = sb("uTh", [128, KT, T + META], R32)
        uTl = sb("uTl", [128, KT, T + META], R32)
        STG = Ring([sb(f"stg{i}", [128, 2048]) for i in range(2)])
        stg_sem = [dsem() for _ in range(2)]
        WH = [sb(f"wh{i}", [128, 2048], R32) for i in range(2)]
        WL = [sb(f"wl{i}", [128, 2048], R32) for i in range(2)]
        WR = Ring([0, 1])
        ARENA = 17920
        arena_at = nc.sbuf_base
        big = sb("big", [128, ARENA])
        hTr = nc.alloc_sbuf_tensor_at("hTr", [128, 16384], R32, offset=arena_at)[:, :]
        cols = sb("cols", [128, 128])
        lev = sb("lev", [128, 14 * 128], U8)
        small = Ring([sb(f"sm{i}", [128, 16]) for i in range(24)])
        w2k = Ring([sb(f"p{i}", [128, 528]) for i in range(5)])
        w2t = Ring([sb(f"t{i}", [128, 528]) for i in range(4)])
        tmp4 = Ring([sb(f"q{i}", [128, D]) for i in range(2)])
        tmp_sem = [dsem(), dsem()]

        class Piece:
            pass

        stg_user = [None, None]

        def load(spec):
            p = Piece()
            p.key, p.kts, p.ncols, parts, p.raw_only = spec
            p.st = STG.get()
            stg_user[p.st.i] = p
            p.let_go = False
            p.raw = p.st.ap[:, 0:p.kts * p.ncols].rearrange("p (k n) -> p k n", n=p.ncols)
            for dst, src in parts:
                p.loaded = SP.dma(dst(p.raw), src, stg_sem[p.st.i], p.st.free)
            return p

        def split(p):
            if p.raw_only:
                def done(*steps):
                    p.st.done(*steps)
                    p.let_go = True
                    weights.fill()
                p.ready, p.done = p.loaded, done
                return
            b = WR.get()
            n = p.kts * p.ncols
            hi, lo, st = WH[b.i][:, 0:n], WL[b.i][:, 0:n], p.st.ap[:, 0:n]
            a = ACTL(lambda e: e.activation(hi, st, ACT.Copy), p.loaded, b.free)
            d = DVE(lambda e: e.tensor_tensor(lo, st, hi.bitcast(F32), ALU.subtract), a)
            p.st.done(a, d)
            p.let_go = True
            p.ready = [a, d]
            p.h = hi.rearrange("p (k n) -> p k n", n=p.ncols)
            p.l = lo.rearrange("p (k n) -> p k n", n=p.ncols)
            p.done = b.done

        class Stream:

            def __init__(self, specs):
                self.specs, self.loaded, self.split, self.ahead = specs, [], [], 1

            def fill(self):
                more = True
                while more:
                    more = False
                    user = stg_user[STG.at % 2]
                    if len(self.loaded) < 2 and self.specs and (user is None or user.let_go):
                        self.loaded.append(load(self.specs.pop(0)))
                        more = True
                    if len(self.split) < self.ahead and self.loaded:
                        p = self.loaded.pop(0)
                        split(p)
                        self.split.append(p)
                        more = True

            def take(self, key):
                self.ahead = 2
                self.fill()
                p = self.split.pop(0)
                self.ahead = 1
                assert p.key == key, (p.key, key)
                return p

        def whole(v):
            return v

        def wsrc(name, r0, kts, c0, ncols):
            return ins[name][r0:r0 + kts * 128, c0:c0 + ncols].rearrange("(k p) n -> p k n", p=128)

        def fm_piece(key, name, c0, raw=False):
            return (key, 8, 256, [(whole, wsrc(name, 0, 8, c0, 256))], raw)

        def tm_piece(key, name, k0, c0, n=512, kts=4, raw=False):
            return (key, kts, n, [(whole, wsrc(name, k0 * 128, kts, c0, n))], raw)

        def at_cols(c0, n, dst):
            return (lambda v: v[:, :, dst:dst + n]), wsrc("even_w_in", 0, 8, c0, n)

        def group_cols(j0):
            return [((lambda v, k=k, g=g: v[:, k, :].rearrange("p (j g d) -> p g j d", g=2, j=2)[:, g]),
                     ins["even_w_in"][k * 128:(k + 1) * 128, 964 + g * 256 + j0 * 64:964 + g * 256 + (j0 + 2) * 64]
                     .rearrange("p (j d) -> p j d", j=2)) for g in range(2) for k in range(KT)]

        def cmp_w1(c, hf):
            return ("w1", 8, 256, [(whole, ins["even_cmp_w1"][0, c][hf * 1024:(hf + 1) * 1024, :].rearrange(
                "(k p) n -> p k n", p=128))], True)

        def even_out(c, hf):
            src = ins["even_w_out"][:, c * 512:(c + 1) * 512]
            if hf == 0:
                return ("out", 4, 512, [(whole, src[0:512, :].rearrange("(k p) n -> p k n", p=128))], False)
            hi = src[512:1024, :].rearrange("(g j d) n -> g d j n", g=2, j=4)
            return ("out", 4, 512, [((lambda v, g=g: v[g * 64:(g + 1) * 64]), hi[g]) for g in range(2)], False)

        def mlp_pieces(up, down):
            def ups(q):
                return [fm_piece("up", up, q * 1024 + g * 256) for g in range(4)]

            def downs(q):
                return [tm_piece("down", down, q * 8 + g * 4, c * 512) for c in range(2) for g in range(2)]
            return ups(0) + ups(1) + downs(0) + ups(2) + downs(1) + ups(3) + downs(2) + downs(3)

        def out_pieces(name):
            return [tm_piece("out", name, g * 4, c * 512) for c in range(2) for g in range(2)]

        specs = [
            ("P1", 8, 256, [at_cols(896, 64, 0), at_cols(896, 64, 64), at_cols(640, 128, 128)], False),
            ("P2", 8, 256, [at_cols(768, 128, 0), at_cols(512, 64, 128), at_cols(512, 64, 192)], False),
            ("P3", 8, 68, [at_cols(576, 64, 0), at_cols(960, 4, 64)], False),
            fm_piece("qa", "even_w_in", 0), fm_piece("qa", "even_w_in", 256),
            fm_piece("kvc", "even_w_in", 1476),
            ("ksw", 8, 256, [at_cols(1732, 128, 0), at_cols(1988, 128, 128)], False),
            ("vs", 8, 152, [at_cols(1860, 128, 0), at_cols(2244, 24, 128)], False),
            ("vw", 8, 128, [at_cols(2116, 128, 0)], False),
            ("qb", 8, 256, group_cols(0), False), ("qb", 8, 256, group_cols(2), False),
            cmp_w1(0, 0), cmp_w1(0, 1), cmp_w1(1, 0), cmp_w1(1, 1),
            even_out(0, 0), even_out(0, 1), even_out(1, 0), even_out(1, 1)]
        specs += mlp_pieces("mlp_up_0", "mlp_down_0")
        specs += [fm_piece("k", "odd_w_in_0", 1024 + g * 256) for g in range(4)]
        specs += [tm_piece("v", "odd_w_in_0", k0, 2048 + c * 512) for c in range(2) for k0 in (0, 4)]
        specs += [fm_piece("q", "odd_w_in_0", g * 256) for g in range(4)]
        specs += out_pieces("odd_w_out_0") + mlp_pieces("mlp_up_1", "mlp_down_1")
        W2 = "w_in_2_0"
        specs += [fm_piece("nq", W2, 0), fm_piece("nq", W2, 256), fm_piece("nk", W2, 512), fm_piece("nk", W2, 768)]
        specs += [tm_piece("tok", W2, k0, c) for c in (1024, 3072, 3584) for k0 in (0, 4)]
        specs += [fm_piece("hq", W2, 1536), fm_piece("hq", W2, 1792)]
        specs += [("z", 8, 256, [((lambda v: v[:, :, 0:128]), wsrc(W2, 0, 8, 2048 + d * 128, 128)),
                                 ((lambda v: v[:, :, 128:256]), wsrc(W2, 0, 8, 2560 + d * 128, 128))], False)
                  for d in range(4)]
        for c0, wname in ((4096, "w_na_out_2_0"), (5120, "w_hg_out_2_0")):
            for g in range(2):
                specs += [tm_piece("y", wname, 0, g * 512, raw=True), fm_piece("gate", W2, c0 + g * 512),
                          fm_piece("gate", W2, c0 + g * 512 + 256)]
        specs += out_pieces("w_o_2_0") + mlp_pieces("w_up_2_0", "w_down_2_0")
        weights = Stream(specs)

        allb = Banks(list(range(8)))

        b = allb.get()
        s = PE(lambda e, b=b: e.transpose(b.ap[:, 0:NROWS], rows[:, :], ident[0:NROWS, 0:NROWS]), rows_d, ident_d)
        cols_r = DVE(lambda e, b=b: e.tensor_copy(cols[:, 0:NROWS], b.ap[:, 0:NROWS]), s)
        b.done(cols_r)

        def col(name, k):
            return cols[:, ROW_AT[name] + k:ROW_AT[name] + k + 1]

        def rstd_of(ss, n, scale, part=128):
            v = small.get()
            s1 = DVE(lambda e: e.tensor_scalar(v.ap[0:part, 0:n], ss.ap[0:part, 0:n], scale, EPS, ALU.mult, ALU.add),
                     ss.ready, v.free)
            ss.done(s1)
            r = small.get()
            r.ready = POOL(lambda e: e.tensor_tensor(r.ap[0:part, 0:n], v.ap[0:part, 0:n], half[0:part, 0:n], ALU.pow),
                           s1, half_m, r.free)
            v.done(r.ready)
            return r

        def sum_squares(src, ready, part=128):
            junk = tmp4.get()
            ss = small.get()
            ss.ready = ACTL(lambda e: e.activation(junk.ap[0:part, :], src, ACT.Square,
                                                   accum_out=ss.ap[0:part, 0:1]), ready, junk.free, ss.free)
            junk.done(ss.ready)
            return ss

        def evac(n, outp, inp, scale, *after):
            if n % 2:
                return ACTL(lambda e: e.activation(outp, inp, ACT.Copy, scale=scale), *after)
            return DVE(lambda e: e.tensor_scalar(outp, inp, scale, None, ALU.mult), *after)

        def parts_of(hi, lo, src, scale, *after):
            a = ACTL(lambda e: e.activation(hi, src, ACT.Copy, scale=scale), *after)
            d = DVE(lambda e: e.scalar_tensor_tensor(out=lo, in0=src, scalar=scale, in1=hi.bitcast(F32), op0=ALU.mult,
                                                     op1=ALU.subtract), a)
            return [a, d]

        def norm_T(h_ready, gname, g0, uT_free, meta=None):
            scaled = []
            ready = [None] * NT
            xs = [big[:, ARENA - (i + 1) * D:ARENA - i * D] for i in range(NT)]
            for i in range(NT):
                r = rstd_of(sum_squares(h[:, i, :], h_ready[i]), 1, 1.0 / D)
                ready[i] = DVE(lambda e, i=i, r=r: e.tensor_scalar(xs[i], h[:, i, :], r.ap[:, 0:1], None, ALU.mult),
                               r.ready, h_ready[i], uT_free)
                r.done(ready[i])
            out_steps = []
            mready = []
            if meta is not None:
                mx = tmp4.get()
                hm_d = POOL.dma(mx.ap[0:META, :], ins["meta_tokens_2"], tmp_sem[mx.i], mx.free)
                r = rstd_of(sum_squares(mx.ap[0:META, :], hm_d, META), 1, 1.0 / D, META)
                ms = DVE(lambda e: e.tensor_scalar(mx.ap[0:META, :], mx.ap[0:META, :], r.ap[0:META, 0:1], None, ALU.mult),
                         r.ready)
                r.done(ms)
                mb = allb.get()
                for k in range(KT):
                    t = PE(lambda e, k=k: e.transpose(mb.ap[:, k * META:(k + 1) * META],
                                                      mx.ap[0:META, k * 128:(k + 1) * 128], ident[0:META, 0:META]),
                           ms, mb.free)
                mx.done(t)
                y = w2k.get()
                yv = y.ap[:, 0:KT * META].rearrange("p (k n) -> p k n", n=META)
                gc = cols[:, ROW_AT[gname] + g0:ROW_AT[gname] + g0 + KT].unsqueeze(2).to_broadcast([128, KT, META])
                ym = DVE(lambda e: e.tensor_tensor(yv, mb.ap[:, 0:KT * META].rearrange("p (k n) -> p k n", n=META), gc,
                                                   ALU.mult), t, cols_r, y.free)
                mready = parts_of(uTh[:, :, T:T + META], uTl[:, :, T:T + META], yv, 1.0, ym, uT_free)
                y.done(mready)
                mready.append(ym)
                mb.done(mready)
            for k in range(KT):
                b = allb.get()
                for i in range(NT):
                    t = PE(lambda e, i=i, k=k, b=b: e.transpose(b.ap[:, i * 128:(i + 1) * 128],
                                                                xs[i][:, k * 128:(k + 1) * 128], ident), ready[i], b.free, ident_d)
                s = parts_of(uTh[:, k, 0:T], uTl[:, k, 0:T], b.ap, col(gname, g0 + k), t, cols_r, uT_free)
                b.done(s)
                out_steps += s
            return out_steps + mready

        def products(outp, pairs, start, stop, *after):
            n = len(pairs)
            for k, (lh, ll, rh, rl) in enumerate(pairs):
                for m, (x, y) in enumerate(((lh, rh), (lh, rl), (ll, rh))):
                    t = PE(lambda e, x=x, y=y, k=k, m=m: e.matmul(outp, x, y, start=(start and k == 0 and m == 0),
                                                                  stop=(stop and k == n - 1 and m == 2)), *after)
            return t

        def fm(bk, w, c0, ready, n0=0, n=T):
            return products(bk.ap[:, 0:n], [(w.h[:, k, c0:c0 + 128], w.l[:, k, c0:c0 + 128],
                                             uTh[:, k, n0:n0 + n], uTl[:, k, n0:n0 + n]) for k in range(KT)],
                            True, True, w.ready, ready, bk.free)

        def tm(outp, w, t0, part, c0, ncols, k0, start, stop, *after):
            return products(outp, [(uTh[:, k0 + k, t0:t0 + part], uTl[:, k0 + k, t0:t0 + part],
                                    w.h[:, k, c0:c0 + ncols], w.l[:, k, c0:c0 + ncols]) for k in range(w.kts)],
                            start, stop, w.ready, *after)

        def run_pipe(units, lags):
            for n in range(len(units) + lags[-1]):
                for d in range(len(lags) - 1, -1, -1):
                    if 0 <= n - lags[d] < len(units):
                        units[n - lags[d]][d]()

        def rope_unit(bk, key, half, dest, scale, ready, dfree):
            st = {}

            def s0():
                st["b"] = bk.get()
                if half == 0:
                    taken[0] = weights.take(key)
                st["t"] = fm(st["b"], taken[0], half * 128, ready)
                if half == 1:
                    taken[0].done(st["t"])

            def s1():
                x = st["x"] = w2k.get()
                b = st["b"]
                st["c"] = ACTL(lambda e: e.activation(x.ap[:, 0:T], b.ap, ACT.Copy, scale=scale), st["t"], x.free)
                b.done(st["c"])

            def s2():
                x, y, t1 = st["x"], bk.get(), w2t.get()
                a = PE(lambda e: e.matmul(y.ap, rotm, x.ap[:, 0:T], start=True, stop=True), st["c"], y.free, rot_d)
                p = POOL(lambda e: e.tensor_tensor(t1.ap[:, 0:T], x.ap[:, 0:T], cosT, ALU.mult), st["c"], t1.free, cos_d)
                x.done(a, p)
                t2 = w2t.get()
                q = DVE(lambda e: e.tensor_tensor(t2.ap[:, 0:T], y.ap, sinT, ALU.mult), a, t2.free, sin_d)
                y.done(q)
                r = DVE(lambda e: e.tensor_tensor(dest, t1.ap[:, 0:T], t2.ap[:, 0:T], ALU.add), p, q, dfree)
                t1.done(r)
                t2.done(r)
                st["r"] = r
            return [s0, s1, s2], st

        def add_products(lhs, nk, lready, key="out"):
            new = [None] * NT
            for c in range(2):
                bks = [allb.get() for _ in range(NT)]
                for g in range(nk // 4):
                    w = weights.take(key)
                    for i in range(NT):
                        t = products(bks[i].ap, [(*lhs(g * 4 + k, i), w.h[:, k, :], w.l[:, k, :]) for k in range(4)],
                                     g == 0, g == nk // 4 - 1, w.ready, bks[i].free,
                                     [lready(g * 4 + k) for k in range(4)])
                        if g == nk // 4 - 1:
                            new[i] = DVE(lambda e, i=i, c=c, bks=bks: e.tensor_tensor(
                                h[:, i, c * 512:(c + 1) * 512], h[:, i, c * 512:(c + 1) * 512], bks[i].ap, ALU.add), t,
                                h_last[i])
                            h_last[i] = new[i]
                            bks[i].done(new[i])
                    w.done(t)
            return list(new), t

        h_last = [None] * NT
        taken = [None]

        def from_uT(k, i):
            return uTh[:, k, i * 128:(i + 1) * 128], uTl[:, k, i * 128:(i + 1) * 128]

        def mlp(uready, big_free):
            hT = [[hTr[:, (q * 2 + x) * 4096:(q * 2 + x + 1) * 4096].rearrange("p (k n) -> p k n", n=T)
                   for x in range(2)] for q in range(2)]
            free = [big_free, big_free]

            def up_quarter(q):
                hready = []
                for g in range(4):
                    w = weights.take("up")
                    for f in range(2):
                        b = allb.get()
                        t = fm(b, w, f * 128, uready)
                        r = w2k.get()
                        a = ACTL(lambda e, b=b, r=r: e.activation(r.ap[:, 0:T], b.ap, ACT.Relu), t, r.free)
                        b.done(a)
                        p = POOL(lambda e, r=r: e.tensor_tensor(r.ap[:, 0:T], r.ap[:, 0:T], r.ap[:, 0:T], ALU.mult), a)
                        hi, lo = (hT[q % 2][x][:, g * 2 + f, :] for x in range(2))
                        a = ACTL(lambda e, r=r, hi=hi: e.activation(hi, r.ap[:, 0:T], ACT.Copy), p, free[q % 2])
                        d = DVE(lambda e, r=r, hi=hi, lo=lo: e.tensor_tensor(lo, r.ap[:, 0:T], hi.bitcast(F32),
                                                                             ALU.subtract), a)
                        r.done(d)
                        hready.append([a, d])
                    w.done(t)
                return hready, t

            def down_quarter(q, hready):
                new, t = add_products(lambda k, i: tuple(hT[q % 2][x][:, k, i * 128:(i + 1) * 128] for x in range(2)),
                                      8, lambda k: hready[k], "down")
                free[q % 2] = t
                return new, t
            hready, _ = up_quarter(0)
            for q in range(4):
                after, uread = up_quarter(q + 1) if q < 3 else (None, uread)
                new, last = down_quarter(q, hready)
                hready = after
            return new, last, uread

        A = {}
        at = [0]

        def region(name, shape, base=None):
            n = int(np.prod(shape[1:]))
            o = at[0]
            at[0] += n
            assert at[0] <= ARENA, (name, at[0])
            v = big[0:shape[0], o:o + n]
            if len(shape) == 3:
                v = v.rearrange("p (a b) -> p a b", b=shape[2])
            A[name] = v
            return v

        at_X = 10624
        lev_f = POOL.dma(big[:, at_X:at_X + 1792], ins["c_lev"], dsem())
        c1 = POOL.dma(big[:, at_X + 1792:at_X + 1920], ins["c_causal"], dsem())
        c2 = POOL.dma(big[:, at_X + 1920:at_X + 2048], ins["c_cmp"], dsem())
        u0 = norm_T(h_ready, "mix_norm_g", 0, [])
        causal_d = POOL(lambda e: e.tensor_copy(causal, big[:, at_X + 1792:at_X + 1920]), c1)
        cmpm_d = POOL(lambda e: e.tensor_copy(cmpm, big[:, at_X + 1920:at_X + 2048]), c2)
        identb_d = POOL(lambda e: e.tensor_copy(identb, ident), ident_d)
        lev_d = POOL(lambda e: e.tensor_copy(lev, big[:, at_X:at_X + 1792]), lev_f)
        EV = "even_w_in"
        qaT = region("qaT", [128, 4, T])
        kaT = region("kaT", [128, T])
        va = region("va", [128, 4, 64])
        qiT = region("qiT", [128, 2, T])
        kiT = region("kiT", [128, T])
        qbT = region("qbT", [128, 4, T])
        kcT = region("kcT", [128, T])
        ksT = region("ksT", [128, T])
        vsb = region("vsb", [128, 4, 128])
        kwT = region("kwT", [128, T])
        vcT = region("vcT", [128, T])
        vw = region("vw", [128, 4, 128])
        wi = sb("wi", [128, 16])
        gate = sb("gate", [128, 4, 24])
        pk = Banks([0, 1, 2, 3, 4, 5])
        pv2 = Banks([6, 7])
        xs_read = u0

        units, sts = [], {}

        def add(name, key, half, dest, scale=1.0, dfree=()):
            u, st = rope_unit(pk, key, half, dest, scale, u0, list(dfree))
            units.append(u)
            sts[name] = st

        add("ki", "P1", 0, kiT)
        add("qi0", "P1", 1, qiT[:, 0, :])
        add("qi1", "P2", 0, qiT[:, 1, :])
        add("ka", "P2", 1, kaT)
        run_pipe(units, ROPE_LAGS)
        w = weights.take("P3")
        b = pk.get()
        for i in range(NT):
            t = tm(b.ap[:, i * 128:i * 128 + 68], w, i * 128, 128, 0, 68, 0, True, True, u0, b.free)
        w.done(t)
        wi_r = DVE(lambda e, b=b: e.tensor_copy(wi.rearrange("p (a b) -> p a b", b=4),
                                                b.ap.rearrange("p (a b) -> p a b", b=128)[:, :, 64:68]), t)
        va_r = DVE(lambda e, b=b: e.tensor_copy(va, b.ap.rearrange("p (a b) -> p a b", b=128)[:, :, 0:64]), t, u0)
        b.done(wi_r, va_r)

        sc = {i: region(f"sc{i}", [128, (i + 1) * 128]) for i in (1, 2, 3)}
        sel = sb("sel", [128, 3, T], BF16)
        sc_r = {}
        for i in (1, 2, 3):
            n = (i + 1) * 128
            for hh in range(4):
                b = pk.get()
                p0 = (hh % 2) * 64
                t = PE(lambda e, b=b, i=i, hh=hh, p0=p0, n=n: e.matmul(
                    b.ap[:, 0:n], qiT[p0:p0 + 64, hh // 2, i * 128:(i + 1) * 128], kiT[p0:p0 + 64, 0:n],
                    start=True, stop=True), sts[f"qi{hh // 2}"]["r"], sts["ki"]["r"], b.free)
                r = w2k.get()
                a = ACTL(lambda e, b=b, r=r, n=n: e.activation(r.ap[:, 0:n], b.ap[:, 0:n], ACT.Relu), t, r.free)
                b.done(a)
                wc = wi[:, i * 4 + hh:i * 4 + hh + 1]
                if hh == 0:
                    s = DVE(lambda e, r=r, i=i, n=n, wc=wc: e.tensor_scalar(sc[i][:, 0:n], r.ap[:, 0:n], wc, None, ALU.mult),
                            a, wi_r)
                else:
                    s = DVE(lambda e, r=r, i=i, n=n, wc=wc: e.scalar_tensor_tensor(
                        out=sc[i][:, 0:n], in0=r.ap[:, 0:n], scalar=wc, in1=sc[i][:, 0:n], op0=ALU.mult, op1=ALU.add),
                        a, wi_r, sc_r[i])
                r.done(s)
                sc_r[i] = s
            sc_r[i] = DVE(lambda e, i=i: e.tensor_tensor(sc[i][:, i * 128:(i + 1) * 128], sc[i][:, i * 128:(i + 1) * 128],
                                                         causal, ALU.add), sc_r[i], causal_d)

        m8 = sb("m8", [128, 3, 8])

        def topk():
            for _ in range(TAKE // 8):
                for i in (1, 2, 3):
                    n = (i + 1) * 128
                    s = DVE(lambda e, i=i, n=n: e.max(m8[:, i - 1, :], sc[i][:, 0:n]), sc_r[i])
                    sc_r[i] = DVE(lambda e, i=i, n=n: e.match_replace(sc[i][:, 0:n], m8[:, i - 1, :], sc[i][:, 0:n], TAKEN), s)
                    yield
            for i in (1, 2, 3):
                n = (i + 1) * 128
                sc_r[i] = DVE(lambda e, i=i, n=n: e.tensor_scalar(sel[:, i - 1, 0:n], sc[i][:, 0:n], -2e38, NEG,
                                                                  ALU.is_gt, ALU.mult), sc_r[i])

        taking = topk()

        def advance(g, n):
            for _ in range(n):
                if next(g, "end") == "end":
                    break

        units = []
        for j in range(4):
            add(f"qa{j}", "qa", j % 2, qaT[:, j, :], 0.125)
        add("kc", "kvc", 0, kcT)
        run_pipe(units, ROPE_LAGS)
        b = pk.get()
        t = fm(b, taken[0], 128, u0)
        taken[0].done(t)
        vc_r = ACTL(lambda e, b=b: e.activation(vcT, b.ap, ACT.Copy), t)
        b.done(vc_r)
        assert at[0] == at_X
        X = [region(f"X{c}", [128, 2, T]) for c in range(2)]
        X_r = []
        for c, (src, r) in enumerate(((kcT, sts["kc"]["r"]), (vcT, vc_r))):
            xs = dsem()
            X_m = DVE(lambda e, c=c: e.memset(X[c][64:128, :, T - 1:T], 0.0), u0, lev_d)
            for g in range(2):
                d1 = POOL.dma(X[c][0:64, g, :], src[g * 64:(g + 1) * 64, :], xs, r)
                d2 = POOL.dma(X[c][64:128, g, 0:T - 1], src[g * 64:(g + 1) * 64, 1:T], xs, r)
            X_r.append([d2, X_m])
        units = []
        add("ks", "ksw", 0, ksT)
        add("kw", "ksw", 1, kwT)
        run_pipe(units, ROPE_LAGS)
        w = weights.take("vs")
        vs_r, gb_r = [], []
        for i in range(NT):
            b = pk.get()
            t = tm(b.ap[:, 0:152], w, i * 128, 128, 0, 152, 0, True, True, u0, b.free)
            vs_r.append(DVE(lambda e, b=b, i=i: e.tensor_copy(vsb[:, i, :], b.ap[:, 0:128]), t))
            gb_r.append(ACTL(lambda e, b=b, i=i: e.activation(gate[:, i, :], b.ap[:, 128:152], ACT.Exp, scale=-1.0), vs_r[-1]))
            b.done(vs_r[-1], gb_r[-1])
        w.done(t)
        w = weights.take("vw")
        b = pk.get()
        for i in range(NT):
            t = tm(b.ap[:, i * 128:(i + 1) * 128], w, i * 128, 128, 0, 128, 0, True, True, u0, b.free)
        vw_r = DVE(lambda e, b=b: e.tensor_copy(vw, b.ap.rearrange("p (a b) -> p a b", b=128)), t)
        b.done(vw_r)
        w.done(t)
        units = []
        for j in range(4):
            add(f"qb{j}", "qb", j % 2, qbT[:, j, :], 0.125)
        run_pipe(units, ROPE_LAGS)
        g2 = DVE(lambda e: e.tensor_scalar(gate, gate, 1.0, None, ALU.add), gb_r)
        gate_r = DVE(lambda e: e.reciprocal(gate, gate), g2)
        advance(taking, 10)

        cH = region("cH", [128, 4, 62])
        cG = region("cG", [128, 4, 62])
        cb = sb("cb", [128, 4])
        w2s = region("w2s", [128, 4, 64])
        w2_d = POOL.dma(w2s, ins["even_cmp_w2"].rearrange("o c (f p) d -> p (o c f) d", p=128), dsem(), u0)
        kcc = region("kcc", [128, 32])
        vcc = region("vcc", [128, 8, 64])
        vcc_m = POOL(lambda e: e.memset(vcc, 0.0), u0)
        hs = []
        for c in range(2):
            bks = [pk.get() for _ in range(4)]
            for hf in range(2):
                w = weights.take("w1")
                for f in range(2):
                    for lq in range(8):
                        lp = hf * 8 + lq
                        a0, b0 = (2 * lp) // 16, (2 * lp) % 16
                        rhs = X[c].rearrange("p g (n s) -> p g n s", s=16)[:, :, a0:a0 + 31, b0]
                        wv = w.raw[:, lq, f * 128:(f + 1) * 128]
                        PE(lambda e, b=bks[f], wv=wv, lp=lp, rhs=rhs: e.matmul(
                            b.ap[:, 0:62], wv, rhs, start=(lp == 0), stop=(lp == 15)), w.ready, X_r[c], bks[f].free)
                        t = PE(lambda e, b=bks[2 + f], wv=wv, lp=lp, c=c: e.matmul(
                            b.ap[:, 0:1], wv, col("even_cmp_pe", c * 16 + lp), start=(lp == 0), stop=(lp == 15)),
                            cols_r, bks[2 + f].free)
                w.done(t)
            for f in range(2):
                s1 = ACTL(lambda e, b=bks[2 + f], n=c * 2 + f: e.activation(cb[:, n:n + 1], b.ap[:, 0:1], ACT.Copy), t)
                s2 = ACTL(lambda e, b=bks[f], n=c * 2 + f: e.activation(cH[:, n, :], b.ap[:, 0:62], ACT.Identity,
                                                                        bias=cb[:, n:n + 1]), s1)
                bks[f].done(s2)
                bks[2 + f].done(s1)
                hs.append(s2)
        s = POOL(lambda e: e.tensor_tensor(cG, cH, cH, ALU.mult), hs)
        s = POOL(lambda e: e.tensor_tensor(cG, cG, cH, ALU.mult), s)
        s = DVE(lambda e: e.scalar_tensor_tensor(out=cG, in0=cG, scalar=0.044715, in1=cH, op0=ALU.mult, op1=ALU.add), s)
        s = ACTL(lambda e: e.activation(cG, cG, ACT.Tanh, scale=math.sqrt(2.0 / math.pi)), s)
        s = DVE(lambda e: e.tensor_scalar(cG, cG, 0.5, 0.5, ALU.mult, ALU.add), s)
        cg_r = DVE(lambda e: e.tensor_tensor(cG, cG, cH, ALU.mult), s)
        b = pk.get()
        for g in range(2):
            for f in range(2):
                t = PE(lambda e, b=b, g=g, f=f: e.matmul(b.ap[g * 64:(g + 1) * 64, 0:31], w2s[:, f, :],
                                                         cG[:, f, g * 31:(g + 1) * 31], start=(f == 0), stop=(f == 1)),
                       cg_r, w2_d, b.free)
        kcc_r = DVE(lambda e, b=b: e.tensor_copy(kcc[:, 0:31], b.ap[:, 0:31]), t)
        b.done(kcc_r)
        b = pk.get()
        for i in range(NT):
            for g in range(2):
                for f in range(2):
                    t = PE(lambda e, b=b, g=g, f=f, i=i: e.matmul(
                        b.ap[i * 32:i * 32 + 31, g * 64:(g + 1) * 64], cG[:, 2 + f, g * 31:(g + 1) * 31],
                        w2s[:, 2 + f, :], start=(f == 0), stop=(f == 1), tile_position=(0, i * 32)),
                        cg_r, w2_d, b.free)
        vcc_r = [DVE(lambda e, b=b, i=i: e.tensor_copy(
            vcc[i * 32:i * 32 + 31, i * 2:i * 2 + 2, :],
            b.ap[i * 32:i * 32 + 31, 0:128].rearrange("p (a b) -> p a b", b=64)), t, vcc_m) for i in range(NT)]
        b.done(vcc_r)

        w2k.more([big[:, o:o + 528] for o in (at_X, at_X + 528)], cg_r)
        w2t.more([big[:, at_X + 1056:at_X + 1584]], cg_r)
        sb_s = Banks([0, 1, 2])
        sb_p = Banks([3, 4, 5])
        sb_o = Banks([6, 7])

        def softmax_unit(qv, kv, n, masks, qready, vs, gatev, obk, oreg, first, last, vready):
            st = {}
            nb = (n + 127) // 128

            def s0():
                b = st["b"] = sb_s.get()
                t = PE(lambda e: e.matmul(b.ap[:, 0:n], qv, kv, start=True, stop=not masks), qready, b.free)
                for m, (c0, c1, mv, mr) in enumerate(masks):
                    t = PE(lambda e, c0=c0, c1=c1, mv=mv, m=m: e.matmul(
                        b.ap[:, c0:c1], identb, mv, start=False, stop=(m == len(masks) - 1)), mr, identb_d)
                st["t"] = t

            def s1():
                b = st["b"]
                m = st["m"] = small.get()
                s = DVE(lambda e: e.tensor_reduce(m.ap[:, 0:1], b.ap[:, 0:n], AX.X, ALU.max, negate=True), st["t"], m.free)
                p = st["p"] = w2k.get()
                st["e"] = ACTL(lambda e: e.activation(p.ap[:, 0:n], b.ap[:, 0:n], ACT.Exp, bias=m.ap[:, 0:1],
                                                      accum_out=m.ap[:, 1:2]), s, p.free)
                b.done(st["e"])

            def s2():
                m, p = st["m"], st["p"]
                s = st["e"]
                s = DVE(lambda e: e.reciprocal(m.ap[:, 2:3], m.ap[:, 1:2]), s)
                if gatev is None:
                    s = DVE(lambda e: e.tensor_scalar(p.ap[:, 0:n], p.ap[:, 0:n], m.ap[:, 2:3], None, ALU.mult), s)
                else:
                    s = DVE(lambda e: e.tensor_scalar(p.ap[:, 0:n], p.ap[:, 0:n], m.ap[:, 2:3], gatev, ALU.mult,
                                                      ALU.mult), s, gate_r)
                m.done(s)
                st["n"] = s

            def s3():
                p = st["p"]
                b = st["b2"] = sb_p.get()
                for k in range(nb):
                    w = min(128, n - k * 128)
                    t = PE(lambda e, k=k, w=w: e.transpose(b.ap[0:w, k * 128:(k + 1) * 128], p.ap[:, k * 128:k * 128 + w],
                                                           ident), st["n"], b.free)
                p.done(t)
                x = st["x"] = w2t.get()
                w = min(n, 128)
                s = ACTL(lambda e: e.activation(x.ap[0:w, 0:nb * 128], b.ap[0:w, 0:nb * 128], ACT.Copy), t, x.free)
                b.done(s)
                st["v"] = s

            def s4():
                x = st["x"]
                o = obk()
                for k in range(nb):
                    w = min(128, n - k * 128)
                    t = PE(lambda e, k=k, w=w: e.matmul(oreg(o), vs(k), x.ap[0:w, k * 128:(k + 1) * 128],
                                                        start=(first and k == 0), stop=(last and k == nb - 1)),
                           st["v"], vready, o.free)
                x.done(t)
                o.last = t
            return [s0, s1, s2, s3, s4]

        cx = Ring([kcT[:, 0:256], kcT[:, 256:512]])

        def compressed_unit(j, obk):
            st = {}

            def s0():
                st["b"] = [sb_s.get(), sb_s.get()]
                st["t"] = []
                for g, b in enumerate(st["b"]):
                    PE(lambda e, b=b: e.matmul(b.ap[:, 0:128], identb, cmpm, start=True, stop=False),
                       cmpm_d, identb_d, b.free)
                    for i in range(NT):
                        t = PE(lambda e, g=g, i=i, b=b: e.matmul(
                            b.ap[:, i * 32:i * 32 + 31], qbT[g * 64:(g + 1) * 64, j, i * 128:(i + 1) * 128],
                            kcc[g * 64:(g + 1) * 64, 0:31], start=False, stop=(i == 3)), sts[f"qb{j}"]["r"], kcc_r)
                    st["t"].append(t)

            def s1():
                m = st["m"] = small.get()
                p = st["p"] = w2k.get()
                for g, b in enumerate(st["b"]):
                    v = b.ap[:, 0:128].rearrange("p (a n) -> p a n", n=32)
                    mg = m.ap[:, g * 4:g * 4 + 4]
                    pv = p.ap[:, g * 128:(g + 1) * 128].rearrange("p (a n) -> p a n", n=32)
                    s = DVE(lambda e, v=v, mg=mg: e.tensor_reduce(mg, v, AX.X, ALU.max), st["t"][g], m.free)
                    s = DVE(lambda e, mg=mg: e.tensor_scalar(mg, mg, -1e28, None, ALU.max), s)
                    s = DVE(lambda e, v=v, mg=mg, pv=pv: e.tensor_tensor(
                        pv, v, mg.unsqueeze(2).to_broadcast([128, 4, 32]), ALU.subtract), s, p.free)
                    b.done(s)
                st["e"] = ACTL(lambda e: e.activation(p.ap[:, 0:256], p.ap[:, 0:256], ACT.Exp), s)

            def s2():
                m, p = st["m"], st["p"]
                pv = p.ap[:, 0:256].rearrange("p (a n) -> p a n", n=32)
                gv = gate.rearrange("p i (g j x) -> p g j x i", g=2, j=4)[:, :, j, 0, :]
                s = DVE(lambda e: e.tensor_reduce(m.ap[:, 8:16], pv, AX.X, ALU.add), st["e"])
                s = DVE(lambda e: e.tensor_scalar(m.ap[:, 8:16], m.ap[:, 8:16], 1e-30, None, ALU.max), s)
                s = DVE(lambda e: e.reciprocal(m.ap[:, 8:16], m.ap[:, 8:16]), s)
                s = DVE(lambda e: e.tensor_tensor(m.ap[:, 8:16].rearrange("p (g i) -> p g i", g=2),
                                                  m.ap[:, 8:16].rearrange("p (g i) -> p g i", g=2), gv, ALU.mult),
                        s, gate_r)
                s = DVE(lambda e: e.tensor_tensor(pv, pv, m.ap[:, 8:16].unsqueeze(2).to_broadcast([128, 8, 32]),
                                                  ALU.mult), s)
                m.done(s)
                st["n"] = s

            def s3():
                p = st["p"]
                b = st["b2"] = sb_p.get()
                for g in range(2):
                    t = PE(lambda e, g=g: e.transpose(b.ap[:, g * 128:(g + 1) * 128], p.ap[:, g * 128:(g + 1) * 128],
                                                      ident), st["n"], b.free)
                p.done(t)
                x = st["x"] = cx.get()
                st["v"] = ACTL(lambda e: e.activation(x.ap, b.ap[:, 0:256], ACT.Copy), t, x.free, X_r)
                b.done(st["v"])

            def product(g, i):
                x = st["x"]
                o = obk()
                t = PE(lambda e: e.matmul(o.ap[g * 64:(g + 1) * 64, i * 128:(i + 1) * 128], vcc[:, i * 2 + g, :],
                                          x.ap[:, g * 128:(g + 1) * 128], start=True, stop=False),
                       st["v"], vcc_r, o.free)
                if g == 1 and i == NT - 1:
                    x.done(t)
            return [s0, s1, s2, s3, lambda: None], product

        def pair_bank(flush):
            st = {}

            def get():
                if "b" not in st:
                    st["b"] = sb_o.get()
                return st["b"]
            return get, st

        units = []
        flushes = {}
        oT_r = [None] * 8
        for j in range(4):
            get, st = pair_bank(None)
            unit, product = compressed_unit(j, get)
            units.append(unit)
            for i in range(NT):
                n = (i + 1) * 128
                for g in range(2):
                    p = slice(g * 64, g * 64 + 64)
                    qv = qbT[p, j, i * 128:(i + 1) * 128]
                    reg = lambda o, p=p, i=i: o.ap[p, i * 128:(i + 1) * 128]
                    gc = lambda x, i=i, g=g, j=j: gate[:, i, (g * 4 + j) * 3 + x:(g * 4 + j) * 3 + x + 1]
                    qr = sts[f"qb{j}"]["r"]
                    cm = [(i * 128, n, causal, causal_d)]
                    units.append(softmax_unit(qv, ksT[p, 0:n], n, cm, [qr, sts["ks"]["r"]],
                                              lambda k, g=g: vsb[:, k, g * 64:g * 64 + 64], gc(1), get, reg,
                                              False, False, vs_r))
                    old = units[-1][4]
                    units[-1][4] = lambda old=old, g=g, i=i, product=product: (product(g, i), old())
                    units.append(softmax_unit(qv, kwT[p, 0:n], n, cm, [qr, sts["kw"]["r"]],
                                              lambda k, g=g: vw[:, k, g * 64:g * 64 + 64], gc(2), get, reg,
                                              False, True, vw_r))

            def flush(st=st, j=j):
                b = st["b"]
                oT_r[4 + j] = parts_of(uTh[:, 4 + j, 0:T], uTl[:, 4 + j, 0:T], b.ap, 1.0, b.last)
                b.done(oT_r[4 + j])
            old = units[-1][4]
            units[-1][4] = lambda old=old, flush=flush: (old(), flush())
        for n, u in enumerate(units):
            if n % 2 == 0:
                old = u[2]
                u[2] = lambda old=old: (old(), advance(taking, 2))
        run_pipe(units, ATT_LAGS)
        advance(taking, 1000)
        nsa_done = oT_r[7]

        units = []
        for j in range(4):
            get, st = pair_bank(None)
            for i in range(NT):
                n = (i + 1) * 128
                for c in range(2):
                    p = slice(c * 64, c * 64 + 64)
                    if i < 1:
                        masks = [(i * 128, n, causal, causal_d)]
                    else:
                        masks = [(0, n, sel[:, i - 1, 0:n], sc_r[i])]
                    units.append(softmax_unit(qaT[p, j, i * 128:(i + 1) * 128], kaT[p, 0:n], n, masks,
                                              [sts[f"qa{j}"]["r"], sts["ka"]["r"]], lambda k: va[:, k, :], None,
                                              get, lambda o, p=p, i=i: o.ap[p, i * 128:(i + 1) * 128], True, True, va_r))

            def flush(st=st, j=j):
                b = st["b"]
                oT_r[j] = parts_of(uTh[:, j, 0:T], uTl[:, j, 0:T], b.ap, 1.0, b.last)
                b.done(oT_r[j])
            old = units[-1][4]
            units[-1][4] = lambda old=old, flush=flush: (old(), flush())
        run_pipe(units, ATT_LAGS)

        w2k.less(2)
        w2t.less(1)
        hr, last = add_products(from_uT, 8, lambda k: oT_r[k])
        u = norm_T(hr, "mlp_norm_g", 0, [last])
        hr, last, _ = mlp(u, u)

        u0 = u = norm_T(hr, "mix_norm_g", 8, [last])
        at[0] = 0
        QT = region("QT", [128, 8, T])
        KTt = region("KTt", [128, 8, T])
        V = region("V", [128, 4, D])
        OQ = region("OQ", [128, 2, D])
        O = {}
        units = []
        sts = {}
        V_r = []
        for g in range(8):
            add(f"k{g}", "k", g % 2, KTt[:, g, :], dfree=u)
        run_pipe(units, ROPE_LAGS)
        for c in range(2):
            bks = [pk.get() for _ in range(NT)]
            for k0 in (0, 4):
                w = weights.take("v")
                for i in range(NT):
                    t = tm(bks[i].ap, w, i * 128, 128, 0, 512, k0, k0 == 0, k0 == 4, u, bks[i].free)
                    if k0 == 4:
                        s = evac(i, V[:, i, c * 512:(c + 1) * 512], bks[i].ap, 1.0, t, u)
                        bks[i].done(s)
                        V_r.append(s)
                w.done(t)
        units = []
        for g in range(8):
            add(f"q{g}", "q", g % 2, QT[:, g, :], 0.125, dfree=u)
        run_pipe(units, ROPE_LAGS)
        uT_read = sts["q7"]["t"]

        lm = region("lm", [128, 128])
        lamb = region("lamb", [128, 256])
        lamb_d = POOL.dma(lamb, bass.AP(ins["odd_lambda"].tensor, 0, [[0, 128], [1, 256]]), dsem(), u)
        lv = region("lv", [128, 4])
        lvv = lamb.rearrange("p (a b d) -> p a b d", a=2, b=2)
        s = DVE(lambda e: e.tensor_tensor(lm.rearrange("p (a d) -> p a d", d=64), lvv[:, :, 0, :], lvv[:, :, 1, :], ALU.mult), lamb_d)
        s = DVE(lambda e: e.tensor_reduce(lv[:, 0:2], lm.rearrange("p (a d) -> p a d", d=64), AX.X, ALU.add), s)
        s = ACTL(lambda e: e.activation(lv[:, 0:2], lv[:, 0:2], ACT.Exp), s)
        s = DVE(lambda e: e.tensor_scalar(lv[:, 2:3], lv[:, 1:2], LAMBDA_INIT, None, ALU.subtract), s)
        lam_r = DVE(lambda e: e.tensor_tensor(lv[:, 2:3], lv[:, 2:3], lv[:, 0:1], ALU.subtract), s)
        subg = region("subg", [128, 1])
        subg_r = DVE(lambda e: e.tensor_scalar(subg, col("odd_subln_g", 0), 1.0 - LAMBDA_INIT, None, ALU.mult), cols_r, u)

        w2k.more([region(f"pd{i}", [128, 528]) for i in range(3)], u)
        w2t.more([region("td", [128, 528])], u)
        dS = Banks([0, 1, 2, 3])
        dP = Banks([4, 5])
        dO = Banks([6, 7])
        Oq = Ring([OQ[:, i, :] for i in range(2)])
        oT_s = []
        first_q = {"r": [last]}

        def diff_unit(hh, i, oq, ost):
            st = {}
            n = (i + 1) * 128
            Q = QT[:, hh, :]

            def s0():
                st["b"] = []
                for c in range(2):
                    b = dS.get()
                    p = slice(c * 64, c * 64 + 64)
                    PE(lambda e, b=b, p=p: e.matmul(b.ap[:, 0:n], Q[p, i * 128:(i + 1) * 128], KTt[p, hh, 0:n],
                                                    start=True, stop=False), sts[f"q{hh}"]["r"], sts[f"k{hh}"]["r"], b.free)
                    b.t = PE(lambda e, b=b: e.matmul(b.ap[:, i * 128:n], identb, causal, start=False, stop=True))
                    st["b"].append(b)

            def s1():
                m = st["m"] = small.get()
                st["p"], st["e"] = [], []
                for c in range(2):
                    b = st["b"][c]
                    s = DVE(lambda e, b=b, c=c: e.tensor_reduce(m.ap[:, c:c + 1], b.ap[:, 0:n], AX.X, ALU.max, negate=True),
                            b.t, m.free)
                    p = w2k.get()
                    x = ACTL(lambda e, b=b, c=c, p=p: e.activation(p.ap[:, 0:n], b.ap[:, 0:n], ACT.Exp, bias=m.ap[:, c:c + 1],
                                                                   accum_out=m.ap[:, 2 + c:3 + c]), s, p.free)
                    b.done(x)
                    st["p"].append(p)
                    st["e"].append(x)

            def s2():
                m = st["m"]
                p0, p1 = st["p"]
                s = DVE(lambda e: e.reciprocal(m.ap[:, 4:6], m.ap[:, 2:4]), st["e"])
                s = DVE(lambda e: e.tensor_scalar(p1.ap[:, 0:n], p1.ap[:, 0:n], m.ap[:, 5:6], lv[:, 2:3], ALU.mult, ALU.mult),
                        s, lam_r)
                s = DVE(lambda e: e.scalar_tensor_tensor(out=p0.ap[:, 0:n], in0=p0.ap[:, 0:n], scalar=m.ap[:, 4:5],
                                                         in1=p1.ap[:, 0:n], op0=ALU.mult, op1=ALU.add), s)
                m.done(s)
                p1.done(s)
                st["n"] = s

            def s3():
                p0 = st["p"][0]
                b = dP.get()
                for k in range(i + 1):
                    t = PE(lambda e, k=k: e.transpose(b.ap[:, k * 128:(k + 1) * 128], p0.ap[:, k * 128:(k + 1) * 128], ident),
                           st["n"], b.free)
                p0.done(t)
                x = st["x"] = w2t.get()
                s = ACTL(lambda e: e.activation(x.ap[:, 0:n], b.ap[:, 0:n], ACT.Copy), t, x.free)
                b.done(s)
                st["v"] = s

            def s4():
                x = st["x"]
                if hh % 4 == 0:
                    ost["b"] = dO.get()
                o = ost["b"]
                for k in range(i + 1):
                    t = PE(lambda e, k=k: e.matmul(o.ap[:, (hh % 4) * 128:(hh % 4 + 1) * 128], x.ap[:, k * 128:(k + 1) * 128],
                                                   V[:, k, hh * 128:(hh + 1) * 128], start=(k == 0), stop=(k == i)),
                           st["v"], V_r, o.free)
                x.done(t)
                if hh == 0:
                    ost["q"] = Oq.get()
                if hh % 4 == 3:
                    q = ost["q"]
                    hf = hh // 4
                    s = DVE(lambda e: e.tensor_copy(q.ap[:, hf * 512:(hf + 1) * 512], o.ap), t, q.free)
                    o.done(s)
                    ost[hf] = s
                if hh == 7:
                    q = ost["q"]
                    qv = q.ap.rearrange("p (a b) -> p a b", b=128)
                    sq = tmp4.get()
                    s = POOL(lambda e: e.tensor_tensor(sq.ap, q.ap, q.ap, ALU.mult), ost[0], ost[1], sq.free)
                    ss = small.get()
                    ss.ready = DVE(lambda e: e.tensor_reduce(ss.ap[:, 0:8], sq.ap.rearrange("p (a b) -> p a b", b=128), AX.X,
                                                             ALU.add), s, ss.free)
                    sq.done(ss.ready)
                    r = rstd_of(ss, 8, 1.0 / 128)
                    s = DVE(lambda e: e.tensor_tensor(qv, qv, r.ap[:, 0:8].unsqueeze(2).to_broadcast([128, 8, 128]), ALU.mult),
                            r.ready)
                    r.done(s)
                    ost["n"] = s
            return [s0, s1, s2, s3, s4]

        def turn_back(i, ost):
            q = ost["q"]
            for hf in range(2):
                b = dP.get()
                for k in range(4):
                    t = PE(lambda e, k=k, b=b, hf=hf: e.transpose(b.ap[:, k * 128:(k + 1) * 128],
                                                                  q.ap[:, (hf * 4 + k) * 128:(hf * 4 + k + 1) * 128], ident),
                           ost["n"], b.free)
                v = (slice(None), slice(hf * 4, hf * 4 + 4), slice(i * 128, (i + 1) * 128))
                s = parts_of(uTh[v], uTl[v], b.ap.rearrange("p (a b) -> p a b", b=128), subg, t, uT_read, subg_r)
                b.done(s)
                oT_s.append(s)
            q.done(t)

        units = []
        for i in range(NT):
            ost = {}
            for hh in range(8):
                u_ = diff_unit(hh, i, None, ost)
                units.append(u_)
            if i:
                old = units[-3][0]
                units[-3][0] = lambda old=old, i=i, prev=prev: (old(), turn_back(i - 1, prev))
            prev = ost
        run_pipe(units, ATT_LAGS)
        turn_back(3, prev)
        w2k.less(3)
        w2t.less(1)
        hr, last = add_products(from_uT, 8, lambda k: oT_s)
        u = norm_T(hr, "mlp_norm_g", 8, [last])
        hr, last, _ = mlp(u, u)
        def final_norm(name, after):
            g = big[:, ARENA - D:ARENA]
            gd = POOL.dma(g, bass.AP(ins[name].tensor, 0, [[0, 128], [1, D]]), dsem(), after)
            res = []
            for i in range(NT):
                r = rstd_of(sum_squares(h[:, i, :], hr[i]), 1, 1.0 / D)
                res.append(DVE(lambda e, i=i, r=r: e.scalar_tensor_tensor(
                    out=h[:, i, :], in0=h[:, i, :], scalar=r.ap[:, 0:1], in1=g, op0=ALU.mult, op1=ALU.mult), r.ready, gd))
                r.done(res[-1])
            return res

        hr = final_norm("final_norm_g", u)

        u = norm_T(hr, "norm_mix_2", 0, [last], meta=True)
        u0 = u
        at[0] = 0
        nq = region("nq", [128, 4, T])
        onT = nq
        at_hg = at[0]
        nk = region("nk", [128, 4, T + META])
        nv = region("nv", [128, 4, T])
        nbr = region("nbr", [128, 2, 896])
        at[0] = max(at[0], at_hg + 7040)
        end_hg = at[0]
        hv = region("hv", [128, 4, T])
        hsg = region("hsg", [128, 4, T])
        hq = region("hq", [128, 4, T])
        ohT = hq
        nvm = region("nvm", [META, T])
        hvm = region("hvm", [META, T])
        ST = region("ST", [128, 8, 128])
        oh = region("oh", [128, 4, 128])

        fb = Banks([0, 1, 2, 3])
        nq_r, nk_r, nv_r = [], [], []
        for f in range(4):
            if f % 2 == 0:
                w = weights.take("nq")
            b = fb.get()
            t = fm(b, w, f % 2 * 128, u)
            s = evac(f, nq[:, f, :], b.ap[:, ::-1], 0.125, t, u)
            b.done(s)
            nq_r.append(s)
            if f % 2:
                w.done(t)
        for f in range(4):
            if f % 2 == 0:
                w = weights.take("nk")
            b = fb.get()
            t = fm(b, w, f % 2 * 128, u)
            s = evac(f, nk[:, f, 0:T], b.ap, 1.0, t, u)
            b.done(s)
            b = fb.get()
            t = fm(b, w, f % 2 * 128, u, T, META)
            s2 = evac(f, nk[:, f, T:T + META], b.ap[:, 0:META], 1.0, t, u)
            b.done(s2)
            nk_r.append([s, s2])
            if f % 2:
                w.done(t)

        def token_major(fin, finm):
            bks = [allb.get() for _ in range(NT + (finm is not None))]
            for k0 in (0, 4):
                w = weights.take("tok")
                for i, b in enumerate(bks):
                    part = 128 if i < NT else META
                    t = tm(b.ap[0:part, :], w, i * 128, part, 0, 512, k0, k0 == 0, k0 == 4, u, b.free)
                    if k0 == 4:
                        (fin if i < NT else finm)(i, b, t)
                w.done(t)

        def keep(dest, rr):
            def fin(i, b, t):
                d = dest[:, i, :] if i < NT else dest
                s = evac(i, d, b.ap[0:128 if i < NT else META, :], 1.0, t, u)
                b.done(s)
                rr.append(s)
            return fin

        token_major(keep(nv, nv_r), keep(nvm, nv_r))

        pad = nc.dram_tensor("pad", (8, 15, 128), F32, kind="Internal").ap()
        pz = dsem()
        s = POOL.dma(pad.rearrange("h a b -> (h a) b"), ins["c_zero"], pz)
        s = POOL.dma(pad[:, :, 48:79], ins["na_rpb_2"].rearrange("o h a b -> (o h) a b"), pz, s)
        nb_ring = Ring([nbr[:, i, :] for i in range(2)])
        nb_sem = [dsem(), dsem()]

        def bias(hh):
            b = nb_ring.get()
            for e2 in range(2):
                src = bass.AP(pad.tensor, hh * 15 * 128 + e2 * 128, [[1, 64], [128, 14], [1, 64]])
                d = POOL.dma(b.ap[e2 * 64:(e2 + 1) * 64, :].rearrange("p (a b) -> p a b", b=64), src, nb_sem[b.i], b.free, s, u)
            b.ready = POOL(lambda e: e.tensor_tensor(b.ap.rearrange("p (a b) -> p a b", b=64),
                                                     b.ap.rearrange("p (a b) -> p a b", b=64),
                                                     winm.unsqueeze(1).to_broadcast([128, 14, 64]), ALU.add), d, win_d)
            return b

        nS = [(0, 1), (2, 3)]
        nSat = [0]
        nP = Banks([4, 5])
        nO = Banks([6, 7])
        on_r = [None] * 4
        bias_of = {}

        def na_unit(hh, i, get, last):
            st = {}
            p = slice((hh % 2) * 64, (hh % 2) * 64 + 64)

            def s0():
                if i == 0:
                    bias_of[hh] = bias(hh)
                b0, b1 = fb.get(), fb.get()
                t0 = PE(lambda e: e.matmul(b0.ap, nq[p, hh // 2, T - (i + 1) * 128:T - i * 128], nk[p, hh // 2, 0:T],
                                           start=True, stop=True), nq_r[hh // 2], nk_r[hh // 2], b0.free)
                t1 = PE(lambda e: e.matmul(b1.ap[:, 0:META], nq[p, hh // 2, T - (i + 1) * 128:T - i * 128],
                                           nk[p, hh // 2, T:T + META], start=True, stop=True), b1.free)
                st["b"], st["t"] = (b0, b1), (t0, t1)

            def s1():
                b0, b1 = st["b"]
                q = st["q"] = w2k.get()
                bb = bias_of[hh]
                o = (6 - 2 * i) * 64
                x0 = DVE(lambda e: e.tensor_tensor(q.ap[:, 0:T], b0.ap, bb.ap[:, o:o + T], ALU.add), st["t"][0],
                         bb.ready, q.free)
                x1 = DVE(lambda e: e.tensor_copy(q.ap[:, T:T + META], b1.ap[:, 0:META]), st["t"][1])
                b0.done(x0)
                b1.done(x1)
                bb.done(x0)
                m = st["m"] = small.get()
                x = DVE(lambda e: e.tensor_reduce(m.ap[:, 0:1], q.ap, AX.X, ALU.max, negate=True), x0, x1, m.free)
                st["e"] = ACTL(lambda e: e.activation(q.ap, q.ap, ACT.Exp, bias=m.ap[:, 0:1], accum_out=m.ap[:, 1:2]), x)

            def s2():
                m, q = st["m"], st["q"]
                x = DVE(lambda e: e.reciprocal(m.ap[:, 2:3], m.ap[:, 1:2]), st["e"])
                st["n"] = DVE(lambda e: e.tensor_scalar(q.ap, q.ap, m.ap[:, 2:3], None, ALU.mult), x)
                m.done(st["n"])

            def s3():
                q = st["q"]
                b, b2 = nP.get(), nP.get()
                for k in range(4):
                    t = PE(lambda e, k=k: e.transpose(b.ap[:, k * 128:(k + 1) * 128], q.ap[:, k * 128:(k + 1) * 128], ident),
                           st["n"], b.free)
                t2 = PE(lambda e: e.transpose(b2.ap[0:META, 0:128], q.ap[:, T:T + META], ident), b2.free)
                q.done(t2)
                x, y = st["x"], st["y"] = w2t.get(), w2t.get()
                s = ACTL(lambda e: e.activation(x.ap[:, 0:T], b.ap, ACT.Copy), t, x.free)
                s2_ = DVE(lambda e: e.tensor_copy(y.ap[0:META, 0:128], b2.ap[0:META, 0:128]), t2, y.free)
                b.done(s)
                b2.done(s2_)
                st["v"] = (s, s2_)

            def s4():
                x, y = st["x"], st["y"]
                o = get()
                for k in range(4):
                    PE(lambda e, k=k: e.matmul(o.ap[p, T - (i + 1) * 128:T - i * 128], nv[:, k, hh * 64:hh * 64 + 64],
                                               x.ap[:, k * 128:(k + 1) * 128], start=(k == 0), stop=False),
                       st["v"], nv_r, o.free)
                t = PE(lambda e: e.matmul(o.ap[p, T - (i + 1) * 128:T - i * 128], nvm[:, hh * 64:hh * 64 + 64],
                                          y.ap[0:META, 0:128], start=False, stop=True))
                x.done(t)
                y.done(t)
                if last:
                    on_r[hh // 2] = ACTL(lambda e: e.activation(onT[:, hh // 2, :], o.ap[:, ::-1], ACT.Copy), t, u)
                    o.done(on_r[hh // 2])
            return [s0, s1, s2, s3, s4]

        na_units = []
        for j in range(4):
            st_ = {}

            def get(st_=st_):
                if "b" not in st_:
                    st_["b"] = nO.get()
                return st_["b"]
            for c in range(2):
                for i in range(NT):
                    na_units.append(na_unit(2 * j + c, i, get, c == 1 and i == 3))
        run_pipe(na_units, NA_LAGS)

        lb = sb("lb", [128, 2, 2, 4])
        lg = cols[:, ROW_AT["hg_lb_logits_2"]:ROW_AT["hg_lb_logits_2"] + 16].rearrange("p (a l k) -> p a l k", a=2, l=2)
        s1 = DVE(lambda e: e.tensor_tensor(lb[:, :, 0, :], lg[:, :, 1, :], lg[:, :, 0, :], ALU.subtract), cols_r)
        s2 = DVE(lambda e: e.tensor_tensor(lb[:, :, 1, :], lg[:, :, 0, :], lg[:, :, 1, :], ALU.subtract), cols_r)
        s3 = ACTL(lambda e: e.activation(lb, lb, ACT.Exp), s1, s2)
        s4 = DVE(lambda e: e.tensor_scalar(lb, lb, 1.0, None, ALU.add), s3)
        lb_r = DVE(lambda e: e.reciprocal(lb, lb), s4)

        hv_r = []
        token_major(keep(hv, hv_r), keep(hvm, hv_r))
        hg_r = []
        hgain = tmp4.get()
        hgain_d = POOL.dma(hgain.ap[:, 0:T], bass.AP(ins["hg_norm_2"].tensor, 0, [[0, 128], [1, T]]), tmp_sem[hgain.i],
                           hgain.free)

        def silu_gain(i, b, t):
            x = w2k.get()
            a = ACTL(lambda e: e.activation(x.ap[:, 0:T], b.ap, ACT.Sigmoid), t, x.free)
            a = DVE(lambda e: e.tensor_tensor(x.ap[:, 0:T], x.ap[:, 0:T], b.ap, ALU.mult), a)
            b.done(a)
            a = POOL(lambda e: e.tensor_tensor(hsg[:, i, :], x.ap[:, 0:T], hgain.ap[:, 0:T], ALU.mult), a, hgain_d, u)
            x.done(a)
            hg_r.append(a)

        token_major(silu_gain, None)
        hgain.done(hg_r)
        hq_r = []
        for f in range(4):
            if f % 2 == 0:
                w = weights.take("hq")
            b = fb.get()
            t = fm(b, w, f % 2 * 128, u)
            x = w2k.get()
            a = ACTL(lambda e, b=b, x=x: e.activation(x.ap[:, 0:T], b.ap, ACT.Sigmoid), t, x.free)
            a = DVE(lambda e, b=b, x=x, f=f: e.tensor_tensor(hq[:, f, :], x.ap[:, 0:T], b.ap, ALU.mult), a, u)
            b.done(a)
            x.done(a)
            hq_r.append(a)
            if f % 2:
                w.done(t)

        at[0] = at_hg
        FQK = [[[region(f"fqk{s_}{d}{c}", [128, T if c == 1 or (c == 0 and d) else T + META]) for c in range(3)]
                for d in range(2)] for s_ in range(2)]
        assert at[0] <= end_hg
        set_free = [[on_r, on_r], [on_r, on_r]]
        free = {"ST": u, "oh": None}
        pz_b = Banks([0, 1])
        pA = Banks([2, 3])
        pT = Banks([4, 5, 6])
        pOo = Banks([7])
        oh_r = [None] * 4
        LEV = (1, 2, 4, 8, 16, 32, 64)

        def chunks(x):
            return x.rearrange("p (c t) -> p c t", t=128)

        class Head:
            pass

        def gates_of(hd):
            H = Head()
            H.f, H.q, H.k = [None, None], [None, None], [None, None]
            S = FQK[hd % 2]
            w = weights.take("z")
            for d in range(2):
                F_, Q_, K_ = S[d]
                for c0, n in [(0, T)] + ([(T, META)] if d == 0 else []):
                    b = pz_b.get()
                    for k in range(KT):
                        t = products(b.ap[:, 0:n], [(w.h[:, k, d * 128:(d + 1) * 128], w.l[:, k, d * 128:(d + 1) * 128],
                                                     uTh[:, k, c0:c0 + n], uTl[:, k, c0:c0 + n])],
                                     k == 0, k == KT - 1, w.ready, u, b.free)
                        if n == T and k % 2:
                            yield
                    a = ACTL(lambda e, b=b, n=n, c0=c0, F_=F_: e.activation(F_[:, c0:c0 + n], b.ap[:, 0:n], ACT.Sigmoid),
                             t, set_free[hd % 2][d])
                    a2 = ACTL(lambda e, b=b, n=n, c0=c0, K_=K_: e.activation(K_[:, c0:c0 + n], b.ap[:, 0:n], ACT.Sigmoid,
                                                                             scale=-1.0), t, set_free[hd % 2][d])
                    b.done(a2)
                    f = DVE(lambda e, n=n, c0=c0, F_=F_, d=d: e.tensor_scalar(
                        F_[:, c0:c0 + n], F_[:, c0:c0 + n], lb[:, d, 1, hd:hd + 1], lb[:, d, 0, hd:hd + 1], ALU.mult,
                        ALU.add), a, lb_r)
                    kk = DVE(lambda e, n=n, c0=c0, K_=K_, d=d: e.tensor_scalar(
                        K_[:, c0:c0 + n], K_[:, c0:c0 + n], lb[:, d, 1, hd:hd + 1], None, ALU.mult), a2, lb_r)
                    H.f[d] = [H.f[d], f]
                    H.k[d] = [H.k[d], kk]
                    yield
                w.done(t)
                H.q[d] = POOL(lambda e, F_=F_, Q_=Q_: e.tensor_tensor(Q_, hq[:, hd, :], F_[:, 0:T], ALU.mult),
                              H.f[d], hq_r[hd], set_free[hd % 2][d])
            x = w2k.get()
            s = POOL(lambda e: e.tensor_tensor(x.ap[:, 0:T], S[0][2][:, 0:T], S[1][2][:, 0:T], ALU.add), H.k, x.free)
            H.k = [[H.k[0], s], [H.k[1], s]]
            yield
            b = pz_b.get()
            for c in range(4):
                t = PE(lambda e, c=c, b=b: e.matmul(b.ap[:, c * 128:(c + 1) * 128], x.ap[:, c * 128:(c + 1) * 128],
                                                    hq[:, hd, c * 128:(c + 1) * 128], start=True, stop=True),
                       s, hq_r[hd], b.free)
            x.done(t)
            H.AT = tmp4.get()
            H.at = DVE(lambda e: e.tensor_tensor(chunks(H.AT.ap[:, 0:T]), chunks(b.ap),
                                                 ident.unsqueeze(1).to_broadcast([128, 4, 128]), ALU.mult), t, H.AT.free)
            b.done(H.at)
            heads[hd] = H

        def levels_of(hd):
            H = heads[hd]
            A_ = H.AT.ap
            for li, m in enumerate(LEV):
                for d in range(2):
                    F_, Q_, K_ = FQK[hd % 2][d]
                    L = T + META if (d == 0 and m <= 8) else T

                    def pairs(x, L, m=m):
                        return x[:, 0:L].rearrange("p (n two m) -> p n two m", two=2, m=m)
                    qs, ks = (1, 0) if d == 0 else (0, 1)
                    b = pA.get()
                    for c in range(4):
                        t = PE(lambda e, c=c, b=b, K_=K_, Q_=Q_: e.matmul(
                            b.ap[:, c * 128:(c + 1) * 128], K_[:, c * 128:(c + 1) * 128], Q_[:, c * 128:(c + 1) * 128],
                            start=True, stop=True), H.q[d], H.k[d], b.free)
                    nb = L // (2 * m)
                    kq = DVE(lambda e, K_=K_, F_=F_, L=L, pairs=pairs, nb=nb, m=m, ks=ks, qs=qs: e.tensor_tensor(
                        pairs(K_, L)[:, :, ks, :], pairs(K_, L)[:, :, ks, :],
                        pairs(F_, L)[:, :, qs, 0:1].to_broadcast([128, nb, m]), ALU.mult), t, H.f[d])
                    nq_ = T // (2 * m)
                    qq = POOL(lambda e, Q_=Q_, F_=F_, pairs=pairs, nq_=nq_, m=m, ks=ks, qs=qs: e.tensor_tensor(
                        pairs(Q_, T)[:, :, qs, :], pairs(Q_, T)[:, :, qs, :],
                        pairs(F_, T)[:, :, ks, 0:1].to_broadcast([128, nq_, m]), ALU.mult), t, H.f[d])
                    mk = lev[:, (d * 7 + li) * 128:(d * 7 + li + 1) * 128].unsqueeze(1).to_broadcast([128, 4, 128])
                    H.at = DVE(lambda e, b=b, mk=mk: e.copy_predicated(chunks(A_[:, 0:T]), mk, chunks(b.ap)),
                               t, H.at, lev_d)
                    b.done(H.at)
                    H.q[d], H.k[d] = qq, kq
                    H.f[d] = POOL(lambda e, F_=F_, L=L, pairs=pairs: e.tensor_tensor(
                        pairs(F_, L)[:, :, 0, 0:1], pairs(F_, L)[:, :, 0, 0:1], pairs(F_, L)[:, :, 1, 0:1], ALU.mult),
                        kq, qq)
                    yield

        def rest_of(hd):
            H = heads[hd]
            S = FQK[hd % 2]
            kh = [w2t.get(), w2t.get()]
            km = w2t.get()
            kh_r = [None, None]
            for d in range(2):
                K_ = S[d][2]
                b = pT.get()
                for c in range(4):
                    t = PE(lambda e, c=c, b=b, K_=K_: e.transpose(b.ap[:, c * 128:(c + 1) * 128],
                                                                  K_[:, c * 128:(c + 1) * 128], ident), H.k[d], b.free)
                kh_r[d] = ACTL(lambda e, b=b, d=d: e.activation(kh[d].ap[:, 0:T], b.ap, ACT.Copy), t, kh[d].free)
                b.done(kh_r[d])
                yield
            b = pT.get()
            km_t = PE(lambda e, b=b: e.transpose(b.ap[0:META, 0:128], S[0][2][:, T:T + META], ident), b.free)
            km_r = ACTL(lambda e, b=b: e.activation(km.ap[0:META, 0:128], b.ap[0:META, 0:128], ACT.Copy), km_t, km.free)
            b.done(km_r)
            yield
            st_r = [None] * 8
            hs_ = slice(hd * 128, (hd + 1) * 128)
            bf = pT.get()
            t = PE(lambda e: e.matmul(bf.ap[:, 384:512], km.ap[0:META, 0:128], hvm[:, hs_], start=True, stop=True),
                   km_r, hv_r, bf.free)
            km.done(t)
            for c in range(3):
                t = PE(lambda e, c=c: e.matmul(bf.ap[:, c * 128:(c + 1) * 128], kh[0].ap[:, c * 128:(c + 1) * 128],
                                               hv[:, c, hs_], start=True, stop=True), kh_r[0], hv_r)
            kh[0].done(t)
            bb = pT.get()
            for c in (3, 2, 1):
                tb = PE(lambda e, c=c: e.matmul(bb.ap[:, c * 128:(c + 1) * 128], kh[1].ap[:, c * 128:(c + 1) * 128],
                                                hv[:, c, hs_], start=True, stop=True), kh_r[1], bb.free)
            kh[1].done(tb)
            st_r[0] = ACTL(lambda e: e.activation(ST[:, 0, :], bf.ap[:, 384:512], ACT.Copy), t, free["ST"])
            st_r[6] = ACTL(lambda e: e.activation(ST[:, 6, :], bb.ap[:, 384:512], ACT.Copy), tb, free["ST"])
            yield
            for c in range(3):
                st_r[c + 1] = DVE(lambda e, c=c: e.scalar_tensor_tensor(
                    out=ST[:, c + 1, :], in0=ST[:, c, :], scalar=S[0][0][:, c * 128:c * 128 + 1],
                    in1=bf.ap[:, c * 128:(c + 1) * 128], op0=ALU.mult, op1=ALU.add), t, st_r[c], H.f[0], free["ST"])
                if c < 2:
                    g = 2 - c
                    st_r[g + 3] = DVE(lambda e, g=g: e.scalar_tensor_tensor(
                        out=ST[:, g + 3, :], in0=ST[:, g + 4, :], scalar=S[1][0][:, g * 128:g * 128 + 1],
                        in1=bb.ap[:, g * 128:(g + 1) * 128], op0=ALU.mult, op1=ALU.add), tb, st_r[g + 4], H.f[1],
                        free["ST"])
                yield
            bf.done(st_r[0:4])
            bb.done(st_r[4:7])
            b = pOo.get()
            for c in range(4):
                o = b.ap[:, c * 128:(c + 1) * 128]
                cs = slice(c * 128, (c + 1) * 128)
                PE(lambda e, o=o, cs=cs, c=c: e.matmul(o, H.AT.ap[:, cs], hv[:, c, hs_], start=True, stop=False),
                   H.at, b.free)
                t = PE(lambda e, o=o, cs=cs, c=c: e.matmul(o, S[0][1][:, cs], ST[:, c, :], start=False, stop=(c == 3)),
                       H.q[0], st_r[c])
                if c < 3:
                    t = PE(lambda e, o=o, cs=cs, c=c: e.matmul(o, S[1][1][:, cs], ST[:, 4 + c, :], start=False,
                                                               stop=True), H.q[1], st_r[4 + c])
                if c % 2:
                    yield
            H.AT.done(t)
            free["ST"] = t
            set_free[hd % 2] = [[st_r[1:4], st_r[4:6], t, H.k, H.f, km_t]] * 2
            x = ACTL(lambda e, b=b: e.activation(oh, chunks(b.ap), ACT.Copy), t, free["oh"])
            b.done(x)
            sq = w2k.get()
            s = POOL(lambda e: e.tensor_tensor(chunks(sq.ap[:, 0:T]), oh, oh, ALU.mult), x, sq.free)
            ss = small.get()
            ss.ready = DVE(lambda e: e.tensor_reduce(ss.ap[:, 0:4], chunks(sq.ap[:, 0:T]), AX.X, ALU.add), s, ss.free)
            sq.done(ss.ready)
            r = rstd_of(ss, 4, 1.0 / 128)
            yield
            s = DVE(lambda e: e.tensor_tensor(oh, oh, r.ap[:, 0:4].unsqueeze(2).to_broadcast([128, 4, 128]), ALU.mult),
                    r.ready)
            r.done(s)
            s = DVE(lambda e: e.tensor_tensor(oh, oh, hsg[:, :, hs_], ALU.mult), s, hg_r)
            yield
            b = pT.get()
            for c in range(4):
                t = PE(lambda e, c=c: e.transpose(b.ap[:, c * 128:(c + 1) * 128], oh[:, c, :], ident), s, b.free)
            free["oh"] = t
            oh_r[hd] = ACTL(lambda e: e.activation(ohT[:, hd, :], b.ap, ACT.Copy), t)
            b.done(oh_r[hd])

        heads = {}
        advance(gates_of(0), 1000)
        for hd in range(4):
            beside = []
            if hd:
                beside.append(rest_of(hd - 1))
            if hd < 3:
                beside.append(gates_of(hd + 1))
            for n, _ in enumerate(levels_of(hd)):
                if hd:
                    advance(beside[0], 2)
                if hd < 3 and n >= 2:
                    advance(beside[-1], 1)
            for g in beside:
                advance(g, 1000)
        advance(rest_of(3), 1000)

        mixT = big[:, 2048:6144].rearrange("p (k n) -> p k n", n=T)
        mix_free = [on_r, oh_r, nk_r]
        parts = {}
        mix_r = []
        for br, (oT_, orr) in enumerate(((onT, on_r), (ohT, oh_r))):
            for g in range(2):
                w = weights.take("y")
                bys = []
                for f in range(4):
                    by = allb.get()
                    for k in range(4):
                        ty = PE(lambda e, k=k, by=by, w=w, f=f, oT_=oT_: e.matmul(
                            by.ap, w.raw[:, k, f * 128:(f + 1) * 128], oT_[:, k, :], start=(k == 0), stop=(k == 3)),
                            w.ready, orr, by.free)
                    bys.append((by, ty))
                w.done(ty)
                for f in range(4):
                    ft = g * 4 + f
                    if f % 2 == 0:
                        w = weights.take("gate")
                    bg = allb.get()
                    t = fm(bg, w, f % 2 * 128, u)
                    if f % 2:
                        w.done(t)
                    by, ty = bys[f]
                    x = w2k.get()
                    a = ACTL(lambda e, bg=bg, x=x: e.activation(x.ap[:, 0:T], bg.ap, ACT.Sigmoid), t, x.free)
                    bg.done(a)
                    if br == 0:
                        a = DVE(lambda e, x=x, by=by, ft=ft: e.tensor_tensor(mixT[:, ft, :], x.ap[:, 0:T], by.ap, ALU.mult),
                                a, ty, mix_free)
                        by.done(a)
                        x.done(a)
                        parts[ft] = a
                    else:
                        a = DVE(lambda e, x=x, by=by: e.tensor_tensor(x.ap[:, 0:T], x.ap[:, 0:T], by.ap, ALU.mult), a, ty)
                        by.done(a)
                        a = POOL(lambda e, x=x, ft=ft: e.tensor_tensor(mixT[:, ft, :], mixT[:, ft, :], x.ap[:, 0:T], ALU.add),
                                 a, parts[ft])
                        x.done(a)
                        parts[ft] = a
        for k in range(KT):
            mix_r.append(parts_of(uTh[:, k, 0:T], uTl[:, k, 0:T], mixT[:, k, :], 1.0, parts[k], t))
        hr, last = add_products(from_uT, 8, lambda k: mix_r[k])
        u = norm_T(hr, "norm_mlp_2", 0, [last])
        hr, last, _ = mlp(u, u)
        out_v = out.rearrange("a (i p) d -> (a p) i d", p=128)
        hr = final_norm("norm_final_2", u)
        stores = [SP.dma(out_v[:, i, :], h[:, i, :], dsem(), hr[i]) for i in range(NT)]
        number(lanes)

        block = ctx.enter_context(nc.Block())

        @block.sync
        def _(e):
            play(SP, e)
            for s in stores:
                e.wait_ge(s.sem.sem, s.count)

        @block.gpsimd
        def _(e):
            play(POOL, e)

        @block.scalar
        def _(e):
            play(ACTL, e)

        @block.tensor
        def _(e):
            play(PE, e)

        @block.vector
        def _(e):
            play(DVE, e)


_INS = ["x", "mix_norm_g", "mlp_norm_g", "even_w_in", "even_cmp_pe", "even_cmp_w1", "even_cmp_w2", "even_w_out",
        "odd_w_in", "odd_lambda", "odd_subln_g", "odd_w_out", "mlp_w_up", "mlp_w_down", "final_norm_g",
        "meta_tokens_2", "w_in_2", "w_na_out_2", "w_hg_out_2", "w_o_2", "w_up_2", "w_down_2", "norm_mix_2",
        "norm_mlp_2", "norm_final_2", "hg_norm_2", "na_rpb_2", "hg_lb_logits_2"]


def kernel(**inputs):
    import concourse.bacc as bacc
    from concourse.bass_utils import run_bass_kernel_spmd

    nc = bacc.Bacc("TRN2", target_bir_lowering=False, num_devices=1)
    arrays = {n: np.ascontiguousarray(inputs[n]) for n in _INS}
    arrays.update(shape_constants())
    ins = {}
    for n, a in arrays.items():
        ins[n] = nc.dram_tensor(n, a.shape, mybir.dt.from_np(a.dtype), kind="ExternalInput").ap()
    for n in ("even_w_in", "even_w_out"):
        ins[n] = ins[n][0]
    for n in ("odd_w_in", "odd_w_out", "w_in_2", "w_na_out_2", "w_hg_out_2", "w_o_2", "w_up_2", "w_down_2"):
        ins[n + "_0"] = ins[n][0]
    for k in range(2):
        ins[f"mlp_up_{k}"] = ins["mlp_w_up"][k]
        ins[f"mlp_down_{k}"] = ins["mlp_w_down"][k]
    out = nc.dram_tensor("out", (1, T, D), F32, kind="ExternalOutput").ap()
    build(nc, ins, out)
    r = run_bass_kernel_spmd(nc, [arrays], core_ids=[0])
    return r.results[0]["out"]
```
